# Optimizing a Trainium2 kernel written in Bass

```python
import jax, jax.numpy as jnp
from jax import lax
import numpy as np
import math

D_MODEL = 1024
BATCH = 1
SEQ = 512
DEPTH = 2

GRID_W = 64
CTX_LEN = 256
CONV_W = 512
CONV_K = 31
CONV_GROUPS = 8
RWKV_W = D_MODEL - CONV_W
HEAD = 64
N_HEADS = RWKV_W // HEAD
DECAY_RANK = 64
ICLR_RANK = 64
GATE_RANK = 160
SHIFT_K = 3
CONV_IN = 2 * CONV_W
RWKV_IN = 3 * RWKV_W + DECAY_RANK + ICLR_RANK + GATE_RANK
IN_COLS = CONV_IN + RWKV_IN
D_FF = -(-8 * D_MODEL // (3 * 256)) * 256
RMS_EPS = 1e-6
LN_EPS = 1e-5
GN_EPS = 64e-5
DECAY_SCALE = 0.606531


def rmsnorm(x, g):
    xf = x.astype(jnp.float32)
    y = xf * lax.rsqrt(jnp.mean(xf * xf, axis=-1, keepdims=True) + RMS_EPS)
    return (y * g).astype(x.dtype)

def modulate(h, shift, scale):
    return h * (1.0 + scale) + shift

def group_norm(x, n_groups, g, b, eps):
    shp = x.shape
    xg = x.astype(jnp.float32).reshape(shp[:-1] + (n_groups, shp[-1] // n_groups))
    mu = jnp.mean(xg, axis=-1, keepdims=True)
    var = jnp.mean(jnp.square(xg - mu), axis=-1, keepdims=True)
    xg = (xg - mu) * lax.rsqrt(var + eps)
    return xg.reshape(shp) * g + b

def dwconv(x, w):
    ch = x.shape[-1]
    return lax.conv_general_dilated(
        x, w[:, None, :].astype(x.dtype), window_strides=(1,), padding="SAME",
        dimension_numbers=("NWC", "WIO", "NWC"), feature_group_count=ch)

def grid_transpose(t, rows, cols):
    b, _, ch = t.shape
    return t.reshape(b, rows, cols, ch).transpose(0, 2, 1, 3).reshape(b, rows * cols, ch)

def to_heads(t):
    return t.reshape(t.shape[:-1] + (N_HEADS, HEAD))

def conformer_conv(u, conv_w, conv_b, cnorm_g, cnorm_b):
    val, gate = jnp.split(u, 2, axis=-1)
    z = val * jax.nn.sigmoid(gate)
    z = dwconv(z, conv_w) + conv_b
    z = group_norm(z, CONV_GROUPS, cnorm_g, cnorm_b, LN_EPS)
    return jax.nn.silu(z)

def rwkv_prep(u, shift_w, decay_b0, decay_up, iclr_b0, iclr_up, k_k, k_a, g_up):
    u = dwconv(u, shift_w).astype(jnp.float32)
    o1 = 3 * RWKV_W
    o2 = o1 + DECAY_RANK
    o3 = o2 + ICLR_RANK
    r, k, v, w_lo, a_lo, g_lo = jnp.split(u, [RWKV_W, 2 * RWKV_W, o1, o2, o3], axis=-1)
    kk = to_heads(k * k_k)
    kk = kk / jnp.maximum(jnp.sqrt(jnp.sum(kk * kk, axis=-1, keepdims=True)), 1e-12)
    dirs = []
    for d in range(2):
        decay = jnp.exp(-DECAY_SCALE * jax.nn.sigmoid(decay_b0[d] + jnp.tanh(w_lo) @ decay_up[d]))
        a = jax.nn.sigmoid(iclr_b0[d] + a_lo @ iclr_up[d])
        k_d = k * (1.0 + (a - 1.0) * k_a)
        dirs.append((to_heads(k_d), to_heads(decay), to_heads(a)))
    g = jax.nn.sigmoid(g_lo) @ g_up
    return to_heads(r), to_heads(k), to_heads(v), kk, dirs, g

def wkv_scan(r, k, v, decay, kk, a, s0, reverse, emit):
    xs = tuple(jnp.swapaxes(t, 0, 1) for t in (r, k, v, decay, kk, kk * a))

    def step(s, inp):
        r_t, k_t, v_t, w_t, kk_t, b_t = inp
        sa = -jnp.einsum("bhvk,bhk->bhv", s, kk_t)
        s = (s * w_t[:, :, None, :] + sa[..., None] * b_t[:, :, None, :]
             + v_t[..., None] * k_t[:, :, None, :])
        y = jnp.einsum("bhvk,bhk->bhv", s, r_t) if emit else None
        return s, y

    s_fin, ys = lax.scan(step, s0, xs, reverse=reverse)
    return (jnp.swapaxes(ys, 0, 1) if emit else None), s_fin

def rwkv_scans(prep, s0_f, s0_b, emit):
    r, k, v, kk, dirs, g = prep
    (k_f, w_f, a_f), (k_b, w_b, a_b) = dirs
    y_f, s_f = wkv_scan(r, k_f, v, w_f, kk, a_f, s0_f, False, emit)
    y_b, s_b = wkv_scan(r, k_b, v, w_b, kk, a_b, s0_b, True, emit)
    y = (y_f + y_b) if emit else None
    return y, s_f, s_b

def rwkv_out(y, prep, r_k, gn_g, gn_b):
    r, k, v, kk, dirs, g = prep
    b, t = y.shape[:2]
    y = group_norm(y.reshape(b, t, RWKV_W), N_HEADS, gn_g, gn_b, GN_EPS)
    bonus = jnp.sum(r * k * to_heads(r_k), axis=-1, keepdims=True) * v
    return (y + bonus.reshape(b, t, RWKV_W)) * g

def swiglu(h, wg, wu, wd):
    return (jax.nn.silu(h @ wg) * (h @ wu)) @ wd

def first_inputs(seed: int = 0) -> dict:
    key = jax.random.key(seed)
    ks = iter(jax.random.split(key, 40))

    def nrm(shape, scale):
        return jax.random.normal(next(ks), shape, jnp.float32) * scale

    L = DEPTH
    shift_base = jnp.array([0.25, 1.0, 0.25], jnp.float32)[None, :, None]
    return {
        "x": nrm((BATCH, SEQ, D_MODEL), 1.0),
        "c": nrm((BATCH, D_MODEL), 1.0),
        "ctx": nrm((BATCH, CTX_LEN, D_MODEL), 1.0),
        "c_ctx": nrm((D_MODEL,), 1.0),
        "ada_w": nrm((L, D_MODEL, 6 * D_MODEL), 0.5 * D_MODEL ** -0.5),
        "ada_b": nrm((L, 6 * D_MODEL), 0.02),
        "norm1_g": 1.0 + nrm((L, D_MODEL), 0.02),
        "norm2_g": 1.0 + nrm((L, D_MODEL), 0.02),
        "w_in": nrm((L, D_MODEL, IN_COLS), D_MODEL ** -0.5),
        "conv_w": nrm((L, CONV_K, CONV_W), CONV_K ** -0.5),
        "conv_b": nrm((L, CONV_W), 0.02),
        "cnorm_g": 1.0 + nrm((L, CONV_W), 0.02),
        "cnorm_b": nrm((L, CONV_W), 0.02),
        "shift_w": shift_base + nrm((L, SHIFT_K, RWKV_IN), 0.1),
        "decay_b0": jax.random.uniform(next(ks), (L, 2, RWKV_W), jnp.float32, -6.0, 0.0),
        "decay_up": nrm((L, 2, DECAY_RANK, RWKV_W), 0.5 * DECAY_RANK ** -0.5),
        "iclr_b0": nrm((L, 2, RWKV_W), 0.5),
        "iclr_up": nrm((L, 2, ICLR_RANK, RWKV_W), 0.5 * ICLR_RANK ** -0.5),
        "k_k": 0.85 + nrm((L, RWKV_W), 0.05),
        "k_a": 1.0 + nrm((L, RWKV_W), 0.05),
        "g_up": nrm((L, GATE_RANK, RWKV_W), GATE_RANK ** -0.5),
        "r_k": nrm((L, RWKV_W), 0.1),
        "gn_g": 1.0 + nrm((L, RWKV_W), 0.02),
        "gn_b": nrm((L, RWKV_W), 0.02),
        "w_out": nrm((L, D_MODEL, D_MODEL), D_MODEL ** -0.5),
        "ffn_wg": nrm((L, D_MODEL, D_FF), D_MODEL ** -0.5),
        "ffn_wu": nrm((L, D_MODEL, D_FF), D_MODEL ** -0.5),
        "ffn_wd": nrm((L, D_FF, D_MODEL), D_FF ** -0.5),
        "final_g": 1.0 + nrm((D_MODEL,), 0.02),
    }

def first_block(x, c, ctx, c_ctx, ada_w, ada_b, norm1_g, norm2_g, w_in, conv_w, conv_b,
              cnorm_g, cnorm_b, shift_w, decay_b0, decay_up, iclr_b0, iclr_up, k_k, k_a,
              g_up, r_k, gn_g, gn_b, w_out, ffn_wg, ffn_wu, ffn_wd, final_g):
    rows = x.shape[1] // GRID_W
    batch = x.shape[0]
    s_zero = jnp.zeros((batch, N_HEADS, HEAD, HEAD), jnp.float32)
    silu_c = jax.nn.silu(c)
    silu_cc = jax.nn.silu(c_ctx)
    for l in range(DEPTH):
        last = l == DEPTH - 1
        col_major = l % 2 == 1
        mod_x = (silu_c @ ada_w[l] + ada_b[l])[:, None, :]
        sh1, sc1, gt1, sh2, sc2, gt2 = jnp.split(mod_x, 6, axis=-1)
        mod_c = silu_cc @ ada_w[l] + ada_b[l]
        csh1, csc1, cgt1, csh2, csc2, cgt2 = jnp.split(mod_c, 6, axis=-1)
        rw = (shift_w[l], decay_b0[l], decay_up[l], iclr_b0[l], iclr_up[l], k_k[l], k_a[l], g_up[l])
        cv = (conv_w[l], conv_b[l], cnorm_g[l], cnorm_b[l])
        post = (r_k[l], gn_g[l], gn_b[l])

        ux = modulate(rmsnorm(x, norm1_g[l]), sh1, sc1) @ w_in[l]
        uc = modulate(rmsnorm(ctx, norm1_g[l]), csh1, csc1) @ w_in[l]
        if col_major:
            ux = grid_transpose(ux, rows, GRID_W)

        prep_c = rwkv_prep(uc[..., CONV_IN:], *rw)
        yc, s_f, s_b = rwkv_scans(prep_c, s_zero, s_zero, emit=not last)
        prep_x = rwkv_prep(ux[..., CONV_IN:], *rw)
        yx, _, _ = rwkv_scans(prep_x, s_f, s_b, emit=True)

        mix_x = jnp.concatenate(
            [conformer_conv(ux[..., :CONV_IN], *cv), rwkv_out(yx, prep_x, *post)],
            axis=-1).astype(x.dtype)
        if col_major:
            mix_x = grid_transpose(mix_x, GRID_W, rows)
        x = x + gt1 * (mix_x @ w_out[l])

        x = x + gt2 * swiglu(modulate(rmsnorm(x, norm2_g[l]), sh2, sc2),
                             ffn_wg[l], ffn_wu[l], ffn_wd[l])

        if not last:
            mix_c = jnp.concatenate(
                [conformer_conv(uc[..., :CONV_IN], *cv), rwkv_out(yc, prep_c, *post)],
                axis=-1).astype(ctx.dtype)
            ctx = ctx + cgt1 * (mix_c @ w_out[l])
            ctx = ctx + cgt2 * swiglu(modulate(rmsnorm(ctx, norm2_g[l]), csh2, csc2),
                                      ffn_wg[l], ffn_wu[l], ffn_wd[l])
    return rmsnorm(x, final_g)


DEPTH_2 = 1

HEAD_DIM = 64
GQA_HEADS = 8
GQA_KV_HEADS = 2
GQA_GROUP = GQA_HEADS // GQA_KV_HEADS
DIFF_HEADS = 4
DIFF_V_DIM = 2 * HEAD_DIM
MIX_WIDTH = GQA_HEADS * HEAD_DIM + DIFF_HEADS * DIFF_V_DIM
A_Q_COLS = GQA_HEADS * HEAD_DIM
A_KV_COLS = GQA_KV_HEADS * HEAD_DIM
B_QK_COLS = DIFF_HEADS * 2 * HEAD_DIM
B_V_COLS = DIFF_HEADS * DIFF_V_DIM
QKV_COLS = A_Q_COLS + 2 * A_KV_COLS + 2 * B_QK_COLS + B_V_COLS
Q_BLOCK = 128
ROPE_THETA = 10000.0
N_EXPERTS = 32
TOP_K = 4
D_FF_2 = D_MODEL
SWIGLU_ALPHA = 1.702
SWIGLU_LIMIT = 7.0
EXPERT_BLOCK = 128
N_MOD = 6
EPS = 1e-6


def rms_norm(x, g):
    xf = x.astype(jnp.float32)
    y = xf * lax.rsqrt(jnp.mean(xf * xf, axis=-1, keepdims=True) + EPS)
    return (y * g.astype(jnp.float32)).astype(x.dtype)

def modulate_2(h, shift, scale):
    return h * (1 + scale) + shift

def axial_rope_tables(n_tokens):
    rows = n_tokens // GRID_W
    row = jnp.broadcast_to(jnp.arange(rows, dtype=jnp.float32)[:, None], (rows, GRID_W)).reshape(-1)
    col = jnp.broadcast_to(jnp.arange(GRID_W, dtype=jnp.float32)[None, :], (rows, GRID_W)).reshape(-1)
    n_freq = HEAD_DIM // 4
    inv_freq = ROPE_THETA ** (-jnp.arange(n_freq, dtype=jnp.float32) / n_freq)
    ang = jnp.stack([row[:, None] * inv_freq, col[:, None] * inv_freq], axis=1)
    return jnp.cos(ang), jnp.sin(ang)

def apply_axial_rope(x, cos, sin):
    b, t, h, _ = x.shape
    xr = x.reshape(b, t, h, 2, 2, HEAD_DIM // 4)
    x1, x2 = xr[..., 0, :], xr[..., 1, :]
    cs = cos[None, :, None]
    sn = sin[None, :, None]
    out = jnp.stack([x1 * cs - x2 * sn, x2 * cs + x1 * sn], axis=-2)
    return out.reshape(x.shape).astype(x.dtype)

def split_projection(p):
    b, t, _ = p.shape
    offs = [A_Q_COLS, A_Q_COLS + A_KV_COLS, A_Q_COLS + 2 * A_KV_COLS,
            A_Q_COLS + 2 * A_KV_COLS + B_QK_COLS, A_Q_COLS + 2 * A_KV_COLS + 2 * B_QK_COLS]
    qa, ka, va, qb, kb, vb = jnp.split(p, offs, axis=-1)
    qa = qa.reshape(b, t, GQA_HEADS, HEAD_DIM)
    ka = ka.reshape(b, t, GQA_KV_HEADS, HEAD_DIM)
    va = va.reshape(b, t, GQA_KV_HEADS, HEAD_DIM)
    qb = qb.reshape(b, t, DIFF_HEADS, 2, HEAD_DIM)
    kb = kb.reshape(b, t, DIFF_HEADS, 2, HEAD_DIM)
    vb = vb.reshape(b, t, DIFF_HEADS, DIFF_V_DIM)
    return qa, ka, va, qb, kb, vb

def rope_diff(x, cos, sin):
    b, t, h, two, d = x.shape
    return apply_axial_rope(x.reshape(b, t, h * two, d), cos, sin).reshape(x.shape)

def gqa_attention(q, k, v, q_block):
    b, t, _, d = q.shape
    nb = t // q_block
    qb = q.reshape(b, nb, q_block, GQA_KV_HEADS, GQA_GROUP, d).transpose(1, 0, 3, 4, 2, 5)
    scale = d ** -0.5

    def block(qi):
        s = jnp.einsum('bhgqd,bkhd->bhgqk', qi, k, preferred_element_type=jnp.float32) * scale
        p = jax.nn.softmax(s, axis=-1)
        return jnp.einsum('bhgqk,bkhd->bqhgd', p.astype(v.dtype), v)

    o = lax.map(block, qb)
    return o.transpose(1, 0, 2, 3, 4, 5).reshape(b, t, GQA_HEADS * d)

def diff_attention(q, k, v, lam, sub_g, lambda_init, q_block):
    b, t, h, _, d = q.shape
    nb = t // q_block
    qb = q.reshape(b, nb, q_block, h, 2, d).transpose(1, 0, 3, 4, 2, 5)
    scale = d ** -0.5

    def block(qi):
        s = jnp.einsum('bhcqd,bkhcd->bhcqk', qi, k, preferred_element_type=jnp.float32) * scale
        p = jax.nn.softmax(s, axis=-1)
        a = p[:, :, 0] - lam * p[:, :, 1]
        return jnp.einsum('bhqk,bkhe->bqhe', a.astype(v.dtype), v)

    o = lax.map(block, qb).transpose(1, 0, 2, 3, 4).reshape(b, t, h, DIFF_V_DIM)
    o = rms_norm(o, sub_g) * (1.0 - lambda_init)
    return o.reshape(b, t, h * DIFF_V_DIM)

def moe_ffn(h, w_router, b_router, w_in, b_in, w_out, b_out):
    b, t, dm = h.shape
    n = b * t
    xt = h.reshape(n, dm)
    logits = (xt @ w_router + b_router).astype(jnp.float32)
    top_val, top_idx = lax.top_k(logits, TOP_K)
    gates = jax.nn.softmax(top_val, axis=-1)
    n_assign = n * TOP_K
    exp_flat = top_idx.reshape(-1).astype(jnp.int32)
    tok_flat = jnp.repeat(jnp.arange(n, dtype=jnp.int32), TOP_K)
    gate_flat = gates.reshape(-1)
    order = jnp.argsort(exp_flat)
    exp_sorted = exp_flat[order]
    counts = jax.ops.segment_sum(jnp.ones_like(exp_flat), exp_flat, num_segments=N_EXPERTS)
    starts = jnp.cumsum(counts) - counts
    padded = (counts + EXPERT_BLOCK - 1) // EXPERT_BLOCK * EXPERT_BLOCK
    pad_ends = jnp.cumsum(padded)
    pad_starts = pad_ends - padded
    dest = pad_starts[exp_sorted] + (jnp.arange(n_assign, dtype=jnp.int32) - starts[exp_sorted])
    n_blocks = -(-n_assign // EXPERT_BLOCK) + N_EXPERTS
    n_rows = n_blocks * EXPERT_BLOCK
    row_tok = jnp.full((n_rows,), n, jnp.int32).at[dest].set(tok_flat[order])
    row_gate = jnp.zeros((n_rows,), jnp.float32).at[dest].set(gate_flat[order])
    block_start = jnp.arange(n_blocks, dtype=jnp.int32) * EXPERT_BLOCK
    block_exp = jnp.minimum(jnp.searchsorted(pad_ends, block_start, side='right'), N_EXPERTS - 1)
    x_pad = jnp.concatenate([xt, jnp.zeros((1, dm), xt.dtype)], axis=0)
    xs = x_pad[row_tok].reshape(n_blocks, EXPERT_BLOCK, dm)

    def expert_block(args):
        xb, e = args
        hcat = xb @ w_in[e] + b_in[e]
        x_glu = jnp.minimum(hcat[:, :D_FF_2], SWIGLU_LIMIT)
        x_lin = jnp.clip(hcat[:, D_FF_2:], -SWIGLU_LIMIT, SWIGLU_LIMIT)
        act = x_glu * jax.nn.sigmoid(SWIGLU_ALPHA * x_glu) * (x_lin + 1)
        return act @ w_out[e] + b_out[e]

    ys = lax.map(expert_block, (xs, block_exp)).reshape(n_rows, dm)
    y = jax.ops.segment_sum(ys * row_gate[:, None].astype(ys.dtype), row_tok, num_segments=n + 1)[:n]
    return y.reshape(b, t, dm)

def second_inputs(seed: int = 0) -> dict:
    key = jax.random.key(seed)
    ks = jax.random.split(key, 21)
    f32 = jnp.float32
    nrm = lambda k, shape, s: jax.random.normal(k, shape, f32) * s
    return {
        'x': nrm(ks[0], (BATCH, SEQ, D_MODEL), 1.0),
        'c': nrm(ks[1], (BATCH, D_MODEL), 1.0),
        'ctx': nrm(ks[2], (BATCH, CTX_LEN, D_MODEL), 1.0),
        'c_ctx': nrm(ks[3], (D_MODEL,), 1.0),
        'w_ada': nrm(ks[4], (DEPTH_2, D_MODEL, N_MOD * D_MODEL), 0.5 * D_MODEL ** -0.5),
        'b_ada': nrm(ks[5], (DEPTH_2, N_MOD * D_MODEL), 0.02),
        'g_attn': 1.0 + nrm(ks[6], (DEPTH_2, D_MODEL), 0.05),
        'w_qkv': nrm(ks[7], (DEPTH_2, D_MODEL, QKV_COLS), D_MODEL ** -0.5),
        'gqa_q_norm': 1.0 + nrm(ks[8], (DEPTH_2, HEAD_DIM), 0.05),
        'gqa_k_norm': 1.0 + nrm(ks[9], (DEPTH_2, HEAD_DIM), 0.05),
        'diff_lambda': nrm(ks[10], (DEPTH_2, 4, HEAD_DIM), 0.1),
        'diff_subln': 1.0 + nrm(ks[11], (DEPTH_2, DIFF_V_DIM), 0.05),
        'w_o': nrm(ks[12], (DEPTH_2, MIX_WIDTH, D_MODEL), MIX_WIDTH ** -0.5),
        'g_ffn': 1.0 + nrm(ks[13], (DEPTH_2, D_MODEL), 0.05),
        'w_router': nrm(ks[14], (DEPTH_2, D_MODEL, N_EXPERTS), D_MODEL ** -0.5),
        'b_router': nrm(ks[15], (DEPTH_2, N_EXPERTS), 0.01),
        'w_in': nrm(ks[16], (DEPTH_2, N_EXPERTS, D_MODEL, 2 * D_FF_2), D_MODEL ** -0.5),
        'b_in': nrm(ks[17], (DEPTH_2, N_EXPERTS, 2 * D_FF_2), 0.02),
        'w_out': nrm(ks[18], (DEPTH_2, N_EXPERTS, D_FF_2, D_MODEL), D_FF_2 ** -0.5),
        'b_out': nrm(ks[19], (DEPTH_2, N_EXPERTS, D_MODEL), 0.02),
        'g_final': 1.0 + nrm(ks[20], (D_MODEL,), 0.05),
    }

def second_block(x, c, ctx, c_ctx, w_ada, b_ada, g_attn, w_qkv, gqa_q_norm, gqa_k_norm, diff_lambda,
              diff_subln, w_o, g_ffn, w_router, b_router, w_in, b_in, w_out, b_out, g_final):
    n_tok = x.shape[1]
    cos, sin = axial_rope_tables(n_tok)
    for l in range(DEPTH_2):
        lambda_init = 0.8 - 0.6 * math.exp(-0.3 * l)
        mod_x = (jax.nn.silu(c) @ w_ada[l] + b_ada[l])[:, None, :]
        mod_c = (jax.nn.silu(c_ctx) @ w_ada[l] + b_ada[l])[None, None, :]
        sh1, sc1, gt1, sh2, sc2, gt2 = jnp.split(mod_x, N_MOD, axis=-1)
        csh1, csc1, cgt1, csh2, csc2, cgt2 = jnp.split(mod_c, N_MOD, axis=-1)

        h = modulate_2(rms_norm(x, g_attn[l]), sh1, sc1)
        hc = modulate_2(rms_norm(ctx, g_attn[l]), csh1, csc1)
        qa, ka, va, qb, kb, vb = split_projection(h @ w_qkv[l])
        qa_c, ka_c, va_c, qb_c, kb_c, vb_c = split_projection(hc @ w_qkv[l])
        qa = apply_axial_rope(rms_norm(qa, gqa_q_norm[l]), cos, sin)
        ka = apply_axial_rope(rms_norm(ka, gqa_k_norm[l]), cos, sin)
        ka_c = rms_norm(ka_c, gqa_k_norm[l])
        qb = rope_diff(qb, cos, sin)
        kb = rope_diff(kb, cos, sin)
        lamf = diff_lambda[l].astype(jnp.float32)
        lam = jnp.exp(jnp.sum(lamf[0] * lamf[1])) - jnp.exp(jnp.sum(lamf[2] * lamf[3])) + lambda_init
        ka_all = jnp.concatenate([ka_c, ka], axis=1)
        va_all = jnp.concatenate([va_c, va], axis=1)
        kb_all = jnp.concatenate([kb_c, kb], axis=1)
        vb_all = jnp.concatenate([vb_c, vb], axis=1)
        lat_mix = jnp.concatenate([
            gqa_attention(qa, ka_all, va_all, Q_BLOCK),
            diff_attention(qb, kb_all, vb_all, lam, diff_subln[l], lambda_init, Q_BLOCK),
        ], axis=-1)
        x = x + gt1 * (lat_mix @ w_o[l])
        x = x + gt2 * moe_ffn(modulate_2(rms_norm(x, g_ffn[l]), sh2, sc2),
                              w_router[l], b_router[l], w_in[l], b_in[l], w_out[l], b_out[l])

        if l < DEPTH_2 - 1:
            qa_c = rms_norm(qa_c, gqa_q_norm[l])
            ctx_len = ctx.shape[1]
            ctx_mix = jnp.concatenate([
                gqa_attention(qa_c, ka_c, va_c, ctx_len),
                diff_attention(qb_c, kb_c, vb_c, lam, diff_subln[l], lambda_init, ctx_len),
            ], axis=-1)
            ctx = ctx + cgt1 * (ctx_mix @ w_o[l])
            ctx = ctx + cgt2 * moe_ffn(modulate_2(rms_norm(ctx, g_ffn[l]), csh2, csc2),
                                       w_router[l], b_router[l], w_in[l], b_in[l], w_out[l], b_out[l])
    return rms_norm(x, g_final)


def setup_inputs(seed=0):
    out = dict(first_inputs(seed))
    for name, value in second_inputs(seed + 1).items():
        if name != "x":
            out[name + "_2"] = value
    return out


def reference(
    x, c, ctx, c_ctx, ada_w, ada_b, norm1_g, norm2_g, w_in, conv_w, conv_b, cnorm_g, cnorm_b,
    shift_w, decay_b0, decay_up, iclr_b0, iclr_up, k_k, k_a, g_up, r_k, gn_g, gn_b, w_out,
    ffn_wg, ffn_wu, ffn_wd, final_g, c_2, ctx_2, c_ctx_2, w_ada_2, b_ada_2, g_attn_2, w_qkv_2,
    gqa_q_norm_2, gqa_k_norm_2, diff_lambda_2, diff_subln_2, w_o_2, g_ffn_2, w_router_2,
    b_router_2, w_in_2, b_in_2, w_out_2, b_out_2, g_final_2,
):
    x = first_block(
        x, c, ctx, c_ctx, ada_w, ada_b, norm1_g, norm2_g, w_in, conv_w, conv_b, cnorm_g,
        cnorm_b, shift_w, decay_b0, decay_up, iclr_b0, iclr_up, k_k, k_a, g_up, r_k, gn_g, gn_b,
        w_out, ffn_wg, ffn_wu, ffn_wd, final_g,
    )
    return second_block(
        x, c_2, ctx_2, c_ctx_2, w_ada_2, b_ada_2, g_attn_2, w_qkv_2, gqa_q_norm_2, gqa_k_norm_2,
        diff_lambda_2, diff_subln_2, w_o_2, g_ffn_2, w_router_2, b_router_2, w_in_2, b_in_2,
        w_out_2, b_out_2, g_final_2,
    )


_drawn_inputs = setup_inputs


def setup_inputs(seed=0):
    import zlib

    import numpy as np

    out = dict(_drawn_inputs(seed))
    spreads = {}
    factors = {'norm1_g': 3.325,
     'norm2_g': 4.054,
     'conv_b': 4.714,
     'cnorm_g': 6.199,
     'cnorm_b': 6.209,
     'decay_up': 3.767,
     'gn_g': 7.01,
     'gn_b': 6.611,
     'g_attn_2': 4.298,
     'gqa_q_norm_2': 8.0,
     'gqa_k_norm_2': 8.0,
     'diff_lambda_2': 2.799,
     'diff_subln_2': 3.944,
     'b_router_2': 17.981,
     'b_in_2': 8.0,
     'b_out_2': 25.687,
     'g_ffn_2': 2.785}
    for name, (base, spread) in spreads.items():
        noise = np.random.default_rng([zlib.crc32(name.encode()), seed]).standard_normal(out[name].shape)
        drawn = base * np.exp(spread * noise) if base else spread * noise
        out[name] = __import__('jax').numpy.asarray(drawn.astype(out[name].dtype))
    for name, factor in factors.items():
        out[name] = (out[name] * factor).astype(out[name].dtype)
    return out
```

```python
import numpy as np
from contextlib import ExitStack, contextmanager

import concourse.bass as bass
from concourse import mybir

F32 = mybir.dt.float32
U32 = mybir.dt.uint32
ALU = mybir.AluOpType
ACT = mybir.ActivationFunctionType
AX_X = mybir.AxisListType.X

P = 128
DM = 1024
KT = DM // P
SEQ, CTX = 512, 256
GRID_W, GRID_R = 64, 8
GAP = 15
XO = CTX + GAP
W = XO + SEQ
TAPS = 31
PADW = GAP + W + GAP
FT = 22
RING = 4
SLOT = 2048
C = 64
CS, XS = CTX // C, SEQ // C
DECAY = 0.606531
LEVELS = (2, 4, 8, 16, 32)
KEYS = CTX + SEQ
TK, TQ = KEYS // P, SEQ // P
NE, TOPK, CAP = 32, 4, P
ROUNDS = SEQ // CAP
EXPERT_SLOTS = 12
MIX_SLOTS = 192
ALPHA, LIMIT = 1.702, 7.0
LAMBDA_INIT = 0.8 - 0.6 * float(np.exp(0.0))

LAYER_VECS = [("ada_b", 48), ("norm1", 8), ("norm2", 8), ("k_k", 4), ("k_a", 4), ("r_k", 4), ("gn_g", 4),
              ("gn_b", 4), ("conv_b", 4), ("cn_g", 4), ("cn_b", 4), ("conv_w", 4 * TAPS), ("shift_w", 48)]
VECS = [(f"{n}{l}", c) for l in range(2) for n, c in LAYER_VECS] + [
    ("final1", 8), ("ada_b2", 48), ("norm12", 8), ("norm22", 8), ("q_norm", 1), ("k_norm", 1), ("subln", 1),
    ("final2", 8), ("cond0", 16), ("cond1", 16)]
VOFF = {}
for _n, _c in VECS:
    VOFF[_n] = (sum(c for _, c in VOFF.values()), _c)
CON2 = [("lam", 256), ("b_router", 32), ("b_in", 512), ("rot", 128), ("cos", 512), ("sin", 512), ("before", 128),
        ("ones", 128), ("iota", 128)]
C2OFF = {}
for _n, _c in CON2:
    C2OFF[_n] = (sum(c for _, c in C2OFF.values()), _c)
NC2 = sum(c for _, c in CON2)
NV = sum(c for _, c in VECS)
CONSTS = [("ident", 128), ("mean_dm", 128), ("head_mean", 128), ("head_sum", 128), ("scan", 512),
          ("tri", 4 * C), ("level", 2 * len(LEVELS) * C), ("level1", 2 * C), ("id64", C)]
COFF = {}
for _n, _c in CONSTS:
    COFF[_n] = (sum(c for _, c in COFF.values()), _c)
NC = sum(c for _, c in CONSTS)


class Counts:

    def __init__(self):
        self.seen, self.turn, self.per = {}, None, {}

    def value(self, sem, n):
        return n if self.turn is None else self.turn * self.per[sem] + n

    def next(self, sem, more=1):
        self.seen[sem] = self.seen.get(sem, 0) + more
        return self.value(sem, self.seen[sem])

    def skip(self, sem, more=1):
        self.seen[sem] = self.seen.get(sem, 0) + more

    @contextmanager
    def loop(self, eng, loops, per):
        start = dict(self.seen)
        self.per = per
        if len(loops) == 1:
            with eng.Fori(0, loops[0]) as e:
                self.turn = e
                yield e, e
                self.turn = None
        else:
            with eng.Fori(0, loops[0]) as r:
                with eng.Fori(0, loops[1]) as e:
                    self.turn = r * loops[1] + e
                    yield self.turn, e
                    self.turn = None
        turns = int(np.prod(loops))
        for sem in set(self.seen) | set(per):
            n = self.seen.get(sem, 0) - start.get(sem, 0)
            assert n == per.get(sem, 0), (sem, n, per.get(sem, 0))
            self.seen[sem] = start.get(sem, 0) + n * turns


class Results:

    def __init__(self):
        self.n = {"dve": 0, "act": 0}
        self.tile, self.last = 0, {}

    def pair(self, owner):
        self.n[owner] += 1
        self.tile += 1
        return (self.tile - 1) % 4

    def place(self, owner):
        j = self.pair(owner)
        stands = self.last.get(j, (None, 0))
        self.last[j] = (owner, self.n[owner])
        return (j,) + stands


def recurrence_plan():
    names = [("decay", "act"), ("rate", "act"), ("q1", "dve"), ("q2", "dve"), ("q3", "dve"), ("vb", "act"), ("kt", "act")]
    for m in LEVELS:
        names.append((f"w{m}", "act"))
        if m != LEVELS[-1]:
            names.append((f"x{m}", "dve"))
        names.append((f"z{m}", "dve"))
    names += [("rhs", "act"), ("u", "act"), ("y", "dve"), ("s", "dve")]
    plan, n = {}, {"dve": 0, "act": 0}
    order = []
    for i, (name, owner) in enumerate(names):
        for g in range(2):
            n[owner] += 1
            plan[name, g] = (4 * g + i % 4, owner, n[owner])
            order.append((name, g))
    return plan, n, order


PLAN, PLAN_N, PLAN_ORDER = recurrence_plan()


def expert_plan():
    names = [("hidden", (0, 1, 2, 3), "dve")] + [(f"add{k}", (4 + k % 4,), "dve") for k in range(KT)] + [
        ("gather", (4, 5), "act"), ("spread", (0,), "dve"), ("expert_out", (6, 7), "act")]
    plan, n = {}, {"dve": 0, "act": 0}
    for name, b, owner in names:
        n[owner] += 1
        plan[name] = (b, owner, n[owner])
    return plan, n


EPLAN, EPLAN_N = expert_plan()


class Turn:

    def __init__(self, base, i):
        self.base, self.i = base, i
        self.users = {b: (name, True) for name, (banks, _, _) in EPLAN.items() for b in banks}

    def count(self, name, before=False):
        _, o, n = EPLAN[name]
        return self.i * EPLAN_N[o] + (self.base[o] + n - (EPLAN_N[o] if before else 0))

    def stands(self, name):
        need = {}
        for b in EPLAN[name][0]:
            user, before = self.users[b]
            o, n = EPLAN[user][1:]
            need[o] = max(need.get(o, (-99,)), (n - EPLAN_N[o] * before, user, before))
            self.users[b] = (name, False)
        return [(o, self.count(user, before)) for o, (_, user, before) in need.items()]


def build(nc, ins, out):
    ctx = ExitStack()
    with ctx:
        def sb(name, cols, parts=P):
            return ctx.enter_context(nc.sbuf_tensor(name, [parts, cols], F32))[:, :]

        def sem(name):
            return ctx.enter_context(nc.semaphore(name))

        xt = sb("xt", KT * W).rearrange("p (k w) -> p k w", k=KT)
        ht = sb("ht", KT * W).rearrange("p (k w) -> p k w", k=KT)
        ring = sb("ring", RING * SLOT).rearrange("p (s c) -> p s c", s=RING)
        vec = sb("vec", NV)
        con = sb("con", NC)
        mod = sb("mod", 96).rearrange("p (q k c) -> p q k c", q=6, k=KT)
        gain = sb("gain", 32).rearrange("p (h k c) -> p h k c", h=2, k=KT)
        rs = sb("rs", W)
        mark, junk = sb("mark", 1), sb("junk", 1)
        work = sb("work", 12 * W + 4 * W + 4 * W + 4 * PADW + 4 * W + 4700)
        rkv = work[:, 0:12 * W].rearrange("p (k w) -> p k w", k=12)
        lo = work[:, 12 * W:16 * W].rearrange("p (k w) -> p k w", k=4)
        kk = work[:, 16 * W:20 * W].rearrange("p (k w) -> p k w", k=4)
        zoff = 20 * W
        zp = work[:, zoff:zoff + 4 * PADW].rearrange("p (k w) -> p k w", k=4)
        scr = work[:, zoff + 4 * PADW:zoff + 4 * PADW + 4 * W].rearrange("p (k w) -> p k w", k=4)
        toff = zoff + 4 * PADW + 4 * W
        tmp = work[:, toff:toff + 2 * (W + 2)].rearrange("p (k w) -> p k w", k=2)
        row = work[0:2, toff + 1600:toff + 1600 + 2048].rearrange("p (b c) -> p b c", b=2)
        act_ff = work[:, 0:FT * (SEQ + CTX)].rearrange("p (k w) -> p k w", k=FT)
        silu_ff = work[:, FT * 768:FT * 768 + 4 * 768].rearrange("p (k w) -> p k w", k=4)
        rec = work[:, zoff:zoff + 21 * 512 + 64]

        def wide(i, n=1):
            return rec[:, 512 * i:512 * (i + n)]

        at = [0]

        def carve(n):
            at[0] += n
            assert at[0] <= work.shape[1], at[0]
            return work[:, at[0] - n:at[0]]

        con2 = carve(NC2)
        q_buf = carve(8 * SEQ).rearrange("p (k c) -> p k c", k=8)
        k_buf = carve(6 * KEYS).rearrange("p (k c) -> p k c", k=6)
        v_buf = carve(TK * 640).rearrange("p (t c) -> p t c", t=TK)
        pt_buf = carve(2 * TK * SEQ).rearrange("p (b t q) -> p b t q", b=2, t=TK)
        sq_buf = work[:, at[0] - 2 * TK * SEQ:at[0] - 2 * TK * SEQ + 6 * KEYS].rearrange("p (k c) -> p k c", k=6)
        prob = carve(4 * KEYS).rearrange("p (b c) -> p b c", b=4)
        neg_max, row_sum, row_inv = carve(64), carve(64), carve(64)
        lam = sb("lam", 8)
        rope_tmp = carve(SEQ)
        at[0] = NC2
        htok = carve(TQ * DM).rearrange("p (t c) -> p t c", t=TQ)
        y_acc = carve(KT * SEQ).rearrange("p (k c) -> p k c", k=KT)
        x_sel = carve(DM).rearrange("p (k c) -> p k c", k=KT)
        glu, lin, sig = carve(DM), carve(DM), carve(DM)
        y_sel = carve(DM)
        sel = carve(SEQ).rearrange("p (t c) -> p t c", t=TQ)
        sel_gate = carve(SEQ).rearrange("p (t c) -> p t c", t=TQ)
        spread = carve(SEQ)
        gate_t = carve(SEQ)
        EC = ROUNDS * NE + 1
        rank = carve(TQ * EC).rearrange("p (t c) -> p t c", t=TQ)
        gates = carve(TQ * EC).rearrange("p (t c) -> p t c", t=TQ)
        picked = carve(TQ * NE).rearrange("p (t c) -> p t c", t=TQ)
        logit = carve(TQ * NE).rearrange("p (t c) -> p t c", t=TQ)
        top8 = carve(TQ * 8).rearrange("p (t c) -> p t c", t=TQ)
        idx8 = carve(TQ * 8).rearrange("p (t c) -> p t c", t=TQ)
        idxf = carve(TQ * 8).rearrange("p (t c) -> p t c", t=TQ)
        expv = carve(TQ * 4).rearrange("p (t c) -> p t c", t=TQ)
        esum, einv, hot = carve(TQ), carve(TQ), carve(NE)
        flag = carve(4)
        out_buf = htok

        psum = ctx.enter_context(nc.psum_tensor("psum", [P, 8 * 512], F32))[:, :].rearrange("p (b c) -> p b c", b=8)

        def V(name, i=0, n=None):
            o, c = VOFF[name]
            return vec[:, o + i:o + i + (n or 1)]

        def Cn(name, rows=P):
            o, c = COFF[name]
            return con[0:rows, o:o + c]

        def C2(name):
            o, c = C2OFF[name]
            return con2[:, o:o + c]

        ident = Cn("ident")
        id64 = Cn("id64")

        consts_in = sem("consts_in")
        x_in = sem("x_in")
        zeroed = sem("zeroed")
        slot_loaded = [sem(f"slot_loaded{i}") for i in range(RING)]
        slot_used = sem("slot_used")
        ready = {o: sem(f"product_ready_{o}") for o in ("dve", "act")}
        freed = {o: sem(f"product_read_{o}") for o in ("dve", "act")}
        dve_chain = sem("dve_chain")
        act_chain = sem("act_chain")
        cond_ready = sem("cond_ready")
        x_updated = sem("x_updated")
        sq_act = sem("squares_act")
        sq_dve = sem("squares_dve")
        std_ready = sem("std_ready")
        normed = sem("normed")
        h_ready = sem("h_ready")
        raw_used = sem("raw_used")
        shifted = sem("shifted")
        conv_out = sem("conv_out")
        sq_grp = sem("sq_grp")
        gstd = sem("gstd")
        grp_normed = sem("grp_normed")
        conv_done = sem("conv_done")
        kk_raw = sem("kk_raw")
        kk_sq = sem("kk_sq")
        lo_tanh = sem("lo_tanh")
        r_cum = sem("r_cum")
        r_pow = sem("r_pow")
        r_fac = sem("r_fac")
        r_vcopy = sem("r_vcopy")
        r_inv = sem("r_inv")
        state = sem("state")
        y_scaled = sem("y_scaled")
        bonus_in = sem("bonus_in")
        stored = sem("stored")
        con2_in = sem("con2_in")
        ctx2_in = sem("ctx2_in")
        lam_exp = sem("lam_exp")
        lam_ready = sem("lam_ready")
        attention_free = sem("attention_free")
        qk_normed = sem("qk_normed")
        roped = sem("roped")
        maxed = sem("maxed")
        prob_ready = sem("prob_ready")
        head_sq = sem("head_sq")
        attended = sem("attended")
        top_ready = sem("top_ready")
        top_exp = sem("top_exp")
        gates_ready = sem("gates_ready")
        rank_ready = sem("rank_ready")
        sel_ready = sem("sel_ready")
        gate_ready = sem("gate_ready")
        glu_ready = sem("glu_ready")
        sig_ready = sem("sig_ready")
        act_ready = sem("act_ready")
        cleared = sem("cleared")
        fin_chain = sem("fin_chain")
        fin_sq = sem("fin_sq")
        fin_ms = sem("fin_ms")
        fin_eps = sem("fin_eps")
        fin_std = sem("fin_std")
        fin_x = sem("fin_x")
        fin_tok = sem("fin_tok")
        fin_row = sem("fin_row")
        passed_pe = sem("passed_pe")
        passed_dve = sem("passed_dve")

        def xs(t):
            return t[..., XO:XO + SEQ]

        def cs(t):
            return t[..., 0:CTX]

        def grid(t, layer):
            return t.rearrange("p (c r) -> p r c", r=GRID_R) if layer == 1 else t.rearrange("p (r c) -> p r c", c=GRID_W)

        def natural(t):
            return t.rearrange("p (r c) -> p r c", c=GRID_W)

        def halves(j):
            return psum[:, 2 * j, :], psum[:, 2 * j + 1, 0:CTX]

        def pairs4(t):
            return t.rearrange("p (k c) -> p k c", k=4)

        GROUPS, GROUP_PROB, n_map = [], [], 0
        for head in range(12):
            for qt in range(TQ):
                if head < 8:
                    r = slice(64 * (head % 2), 64 * (head % 2) + 64)
                    maps = [("shared", head // 2, head // 4, r)]
                else:
                    maps = [("paired", 4 + head - 8, 2 + head - 8, slice(64 * c, 64 * c + 64)) for c in range(2)]
                GROUPS.append((head, qt, maps))
                GROUP_PROB.append(n_map % 4)
                n_map += len(maps)

        f0 = {CS: 0, XS: XO}
        b0 = {CS: CTX - C, XS: XO + SEQ - C}

        def heads(t):
            return t.rearrange("p (g k c) -> p g k c", g=2, k=4)

        condv = [sb(f"cond_silu{b}", 16).rearrange("p (k c) -> p k c", k=KT) for b in range(2)]
        R_sgaa = wide(0, 2)
        R_sg, R_aa = heads(wide(0)), heads(wide(1))
        R_li, R_lx = heads(wide(2)), heads(wide(3))
        R_kr = wide(4, 2).rearrange("p (g k c) -> p g k c", g=2, k=4)
        R_pi, R_bh, R_kh = wide(6), heads(wide(7)), heads(wide(1))
        R_bb, R_kb, R_vc = heads(wide(8)), heads(wide(9)), heads(wide(10))
        R_m1 = wide(11, 2).rearrange("p (g k h c) -> p g k h c", g=2, k=4, h=2)
        R_m2 = wide(13, 2).rearrange("p (g k h c) -> p g k h c", g=2, k=4, h=2)
        R_x, R_z, R_w, R_w1, R_u = heads(wide(15)), heads(wide(16)), heads(wide(0)), heads(wide(2)), heads(wide(3))
        R_vt, R_bt, R_ktk, R_s = heads(wide(17)), heads(wide(18)), heads(wide(19)), heads(wide(20))
        R_vb = wide(17, 2).rearrange("p (h g k) -> p h g k", h=2, g=2)
        R_tot, R_pc = rec[:, 21 * 512:21 * 512 + 8], rec[:, 21 * 512 + 8:21 * 512 + 16]

        def chunk(t, col):
            return t[:, :, bass.ds(col, C)]
        block = ctx.enter_context(nc.Block())

        @block.sync
        def _(sp):
            sp.dma_start(vec, ins["vecs"]).then_inc(consts_in, 16)
            sp.dma_start(con, ins["consts"]).then_inc(consts_in, 16)
            stream = ins["stream"]
            n_slots = stream.shape[0]
            for s in range(RING):
                sp.dma_start(ring[:, s, :], stream[s]).then_inc(slot_loaded[s], 16)
                if s == 0:
                    for k in range(KT):
                        sp.dma_start(xs(xt[:, k, :]), ins["x_cm"][:, k, :]).then_inc(x_in, 16)
                        sp.dma_start(cs(xt[:, k, :]), ins["ctx_cm"][:, k, :]).then_inc(x_in, 16)
            with sp.Fori(1, n_slots // RING) as turn:
                for s in range(RING):
                    sp.wait_ge(slot_used, turn * RING + (s + 1 - RING))
                    sp.dma_start(ring[:, s, :], stream[bass.ds(turn * RING + s, 1)].rearrange("o p c -> (o p) c")
                                 ).then_inc(slot_loaded[s], 16)

            def expert_weights(e, turn, late):
                for j in range(EXPERT_SLOTS):
                    sp.wait_ge(slot_used, turn * EXPERT_SLOTS + (MIX_SLOTS + j + 1 - RING + late))
                    if j < KT:
                        src = ins["w_in"][bass.ds(e, 1), P * j:P * j + P, :].rearrange("o p c -> (o p) c")
                        dst = ring[:, j % RING, :]
                    else:
                        f = 2 * P * (j - KT)
                        src = ins["w_out"][bass.ds(e, 1), f:f + 2 * P, :].rearrange("o (f p) c -> (o p) f c", p=P)
                        dst = ring[:, j % RING, :].rearrange("p (f c) -> p f c", f=2)
                    sp.dma_start(dst, src).then_inc(slot_loaded[j % RING], 16)

            with sp.Fori(0, NE) as e:
                expert_weights(e, e, 0)
            sp.wait_ge(rank_ready, 1)
            over = sp.alloc_register("over_sp")
            sp.reg_load(over, flag[0:1, 0:1].bitcast(mybir.dt.int32))
            with sp.If_eq(over, 1):
                with sp.Fori(1, ROUNDS) as r:
                    with sp.Fori(0, NE) as e:
                        expert_weights(e, r * NE + e, 1)
            for t in range(TQ):
                sp.wait_ge(fin_row, t + 1)
                sp.dma_start(out[0, P * t:P * t + P, :], out_buf[:, t, :]).then_inc(stored, 16)
            sp.wait_ge(stored, 16 * TQ)

        @block.gpsimd
        def _(pool):
            pool.wait_ge(attention_free, 1)
            pool.dma_start(con2, ins["con2"]).then_inc(con2_in, 16)
            pool.dma_start(cs(xt), ins["ctx2_cm"]).then_inc(ctx2_in, 16)

        @block.tensor
        def _(pe):
            w = Counts()
            banks = Results()
            slot = [0]
            used_up = [0]

            def matmul(*args, **kwargs):
                mm = pe.matmul(*args, **kwargs)
                if used_up[0]:
                    mm.then_inc(slot_used, used_up[0])
                    used_up[0] = 0
                return mm

            def take_slot():
                n = slot[0]
                slot[0] += 1
                pe.wait_ge(slot_loaded[n % RING], 16 * (n // RING + 1))
                return ring[:, n % RING, :]

            def product(owner, terms, with_ctx=True, rows=P, used=0, with_x=True):
                j, stands, n_stands = banks.place(owner)
                if stands:
                    pe.wait_ge(freed[stands], n_stands)
                px, pc = halves(j)
                n = len(terms)
                for i, (lhs, rhs) in enumerate(terms):
                    if with_x:
                        mm = matmul(px[0:rows], lhs, xs(rhs), start=(i == 0), stop=(i == n - 1))
                if with_ctx:
                    for i, (lhs, rhs) in enumerate(terms):
                        mm = matmul(pc[0:rows], lhs, cs(rhs), start=(i == 0), stop=(i == n - 1))
                mm.then_inc(ready[owner], 1)
                used_up[0] += used

            def modulation(block_n):
                for q in range(6):
                    j, stands, n_stands = banks.place("act")
                    if stands:
                        pe.wait_ge(freed[stands], n_stands)
                    for s in range(4):
                        wt = take_slot().rearrange("p (k c) -> p k c", k=KT)
                        for k in range(KT):
                            mm = matmul(psum[0:2, 2 * j + s // 2, 256 * (s % 2):256 * (s % 2) + 256],
                                           condv[block_n][:, k, :], wt[:, k, :], start=(k == 0), stop=(k == KT - 1))
                        used_up[0] += 1
                    mm.then_inc(ready["act"], 1)
                    pe.wait_ge(freed["act"], banks.n["act"])
                    j, stands, n_stands = banks.place("dve")
                    if stands:
                        pe.wait_ge(freed[stands], n_stands)
                    for k in range(KT):
                        mm = pe.transpose(psum[:, 2 * j, 2 * k:2 * k + 2], row[:, q % 2, 128 * k:128 * k + 128], ident[0:2, 0:2])
                    mm.then_inc(ready["dve"], 1)

            def mean_square():
                pe.wait_ge(sq_act, w.next(sq_act))
                pe.wait_ge(sq_dve, w.next(sq_dve))
                product("dve", [(Cn("mean_dm"), ht[:, k, :]) for k in range(KT)])

            def input_projection():
                pe.wait_ge(h_ready, w.next(h_ready, KT))
                for t in range(4):
                    wt = take_slot().rearrange("p (k c) -> p k c", k=KT)
                    for h in range(2):
                        product("act" if t % 2 == 0 else "dve",
                                [(wt[:, k, 128 * h:128 * h + 128], ht[:, k, :]) for k in range(KT)], used=h)
                for t in range(6):
                    wt = take_slot().rearrange("p (k c) -> p k c", k=KT)
                    for h in range(2):
                        product("act", [(wt[:, k, 128 * h:128 * h + 128], ht[:, k, :]) for k in range(KT)], used=h)
                wt = take_slot().rearrange("p (k c) -> p k c", k=KT)
                product("act", [(wt[:, k, 0:64], ht[:, k, :]) for k in range(KT)], rows=64)
                product("act", [(wt[:, k, 64:128], ht[:, k, :]) for k in range(KT)], rows=64)
                product("act", [(wt[:, k, 128:256], ht[:, k, :]) for k in range(KT)], used=1)
                wt = take_slot().rearrange("p (k c) -> p k c", k=KT)
                product("act", [(wt[:, k, 0:32], ht[:, k, :]) for k in range(KT)], rows=32, used=1)

            def group_norm(base):
                for t in range(4):
                    if base == 0:
                        if t == 0:
                            pe.wait_ge(conv_out, w.next(conv_out))
                    product("dve", [(Cn("head_mean"), ht[:, base + t, :])])
                for t in range(4):
                    pe.wait_ge(sq_grp, w.next(sq_grp))
                    product("dve", [(Cn("head_mean"), scr[:, t, :])])

            def key_norm():
                pe.wait_ge(kk_sq, w.next(kk_sq))
                for t in range(4):
                    product("dve", [(Cn("head_sum"), scr[:, t, :])])

            def recurrence(lora, turns):
                up_d = lora[0:65, 0:1024].rearrange("p (g c) -> p g c", g=2)
                up_a = lora[0:65, 1024:2048].rearrange("p (g c) -> p g c", g=2)
                for o in ("dve", "act"):
                    pe.wait_ge(freed[o], banks.n[o])
                banks.last = {}
                base = dict(banks.n)
                per = {r_fac: 2, r_vcopy: 2, r_inv: 2}
                hs = ((0, slice(0, 64)), (1, slice(64, 128)))

                with w.loop(pe, [turns], per) as (i, _):
                    waited, need, users = {}, {"dve": 0, "act": 0}, {}

                    def done(name, g):
                        _, o, n = PLAN[name, g]
                        need[o] = max(need.get(o, 0), n)

                    def out_of(name, g):
                        bank, owner, n = PLAN[name, g]
                        if bank in users:
                            done(*users[bank])
                        users[bank] = (name, g)
                        for o, m in need.items():
                            if m > waited.get(o, -1):
                                pe.wait_ge(freed[o], i * PLAN_N[o] + (base[o] + m))
                                pe.sem_inc(passed_pe, 1)
                                waited[o] = m
                        need.clear()
                        return psum[:, bank, :], owner

                    col = {0: i * C + f0[turns], 1: i * (-C) + b0[turns]}
                    for name, up, src in (("decay", up_d, lo[0:65, 0, :]), ("rate", up_a, lo[0:65, 1, :])):
                        for g in range(2):
                            ps, o = out_of(name, g)
                            for p in range(4):
                                mm = matmul(ps[:, 64 * p:64 * p + 64], up[:, g, 128 * p:128 * p + 128],
                                               src[:, bass.ds(col[g], C)], start=True, stop=True)
                            mm.then_inc(ready[o], 1)

                    def each(name, g, terms, cols=64):
                        ps, o = out_of(name, g)
                        for p in range(4):
                            for hh, r in hs:
                                n = len(terms)
                                for t, (lhs, rhs) in enumerate(terms):
                                    mm = matmul(ps[r, cols * p:cols * p + cols], lhs(g, p, r), rhs(g, p, r),
                                                   start=(t == 0), stop=(t == n - 1))
                        mm.then_inc(ready[o], 1)

                    def op(t):
                        return lambda g, p, r: t[r, g, p, :]

                    pe.wait_ge(r_fac, w.next(r_fac, 2))
                    pe.sem_inc(passed_pe, 1)
                    for g in range(2):
                        each("q1", g, [(op(R_bh), lambda g, p, r: R_kr[r, g, p, :])], cols=128)
                    for g in range(2):
                        each("q2", g, [(op(R_kh), lambda g, p, r: R_kr[r, g, p, :])], cols=128)
                    for g in range(2):
                        each("q3", g, [(lambda g, p, r: R_kr[r, g, p, 0:64], op(R_bh))])
                    pe.wait_ge(r_vcopy, w.next(r_vcopy, 2))
                    pe.sem_inc(passed_pe, 1)
                    for g in range(2):
                        ps, o = out_of("vb", g)
                        for h, src in ((0, R_vc), (1, R_bb)):
                            for p in range(4):
                                for hh, r in hs:
                                    mm = matmul(ps[r, 256 * h + 64 * p:256 * h + 64 * p + 64], src[r, g, p, :], id64[r, :],
                                                   start=True, stop=True)
                        mm.then_inc(ready[o], 1)
                    for g in range(2):
                        each("kt", g, [(op(R_kb), lambda g, p, r: id64[r, :])])
                    pe.wait_ge(r_inv, w.next(r_inv, 2))
                    pe.sem_inc(passed_pe, 1)
                    done("q3", 1)
                    for n, m in enumerate(LEVELS):
                        for g in range(2):
                            if n:
                                done(f"x{LEVELS[n - 1]}", g)
                            each(f"w{m}", g, [(lambda g, p, r: R_m1[r, g, p, 0, :], op(R_x))])
                        for g in range(2):
                            done(f"w{m}", g)
                            if n:
                                done(f"z{LEVELS[n - 1]}", g)
                            if m != LEVELS[-1]:
                                each(f"x{m}", g, [(op(R_z), op(R_w))])
                        for g in range(2):
                            each(f"z{m}", g, [(op(R_w), op(R_z))])
                    done("kt", 1)
                    for g in range(2):
                        each("rhs", g, [(lambda g, p, r: R_kr[r, g, p, 0:64], op(R_s)),
                                        (lambda g, p, r: R_m2[r, g, p, 0, :], op(R_vt))])
                    for g in range(2):
                        done(f"z{LEVELS[-1]}", g)
                        done("rhs", g)
                        each("u", g, [(op(R_z), op(R_w1))])
                    for g in range(2):
                        done("u", g)
                        each("y", g, [(op(R_s), lambda g, p, r: R_kr[r, g, p, 64:128]),
                                      (op(R_u), lambda g, p, r: R_m1[r, g, p, 1, :]),
                                      (op(R_vt), lambda g, p, r: R_m2[r, g, p, 1, :])])
                    for g in range(2):
                        each("s", g, [(op(R_bt), op(R_u)), (op(R_ktk), op(R_vt))])
                for o in ("dve", "act"):
                    banks.n[o] += turns * PLAN_N[o]
                banks.last = {}
                for o in ("dve", "act"):
                    pe.wait_ge(freed[o], banks.n[o])
                banks.last = {}

            def mix_out(gup):
                g_hi, g_lo = gup[:, 0:512], gup[0:32, 512:1024]
                pe.wait_ge(bonus_in, w.next(bonus_in))
                for t in range(4):
                    product("dve", [(Cn("head_sum"), scr[:, t, :])])
                for t in range(4):
                    j, stands, n_stands = banks.place("dve")
                    if stands:
                        pe.wait_ge(freed[stands], n_stands)
                    px, pc = halves(j)
                    for dst, f in ((px, xs), (pc, cs)):
                        matmul(dst, g_hi[:, 128 * t:128 * t + 128], f(lo[:, 2, :]), start=True, stop=False)
                        mm = matmul(dst, g_lo[:, 128 * t:128 * t + 128], f(lo[0:32, 3, :]), start=False, stop=True)
                    mm.then_inc(ready["dve"], 1)
                used_up[0] += 2

            def output_projection(with_ctx):
                pe.wait_ge(freed["dve"], banks.n["dve"])
                pe.wait_ge(conv_done, w.next(conv_done, 4))
                for t in range(4):
                    wt = take_slot().rearrange("p (k c) -> p k c", k=KT)
                    for h in range(2):
                        product("dve", [(wt[:, k, 128 * h:128 * h + 128], ht[:, k, :]) for k in range(KT)], with_ctx, used=h)

            def output_projection_2():
                pe.wait_ge(attended, w.next(attended))
                pe.wait_ge(freed["act"], banks.n["act"])
                for t in range(4):
                    wt = take_slot().rearrange("p (k c) -> p k c", k=KT)
                    for h in range(2):
                        product("dve", [(wt[:, k, 128 * h:128 * h + 128], ht[:, k, :]) for k in range(KT)], False, used=h)

            def feed_forward(with_ctx):
                pe.wait_ge(h_ready, w.next(h_ready, KT))
                for t in range(FT // 2):
                    for owner in ("act", "dve"):
                        wt = take_slot().rearrange("p (k c) -> p k c", k=KT)
                        for h in range(2):
                            product(owner, [(wt[:, k, 128 * h:128 * h + 128], ht[:, k, :]) for k in range(KT)], with_ctx, used=h)
                pe.wait_ge(freed["dve"], banks.n["dve"])
                for t in range(4):
                    parts = [take_slot().rearrange("p (k c) -> p k c", k=KT) for _ in range(3)]
                    for h in range(2):
                        j, stands, n_stands = banks.place("dve")
                        if stands:
                            pe.wait_ge(freed[stands], n_stands)
                        px, pc = halves(j)
                        dsts = ((px, CTX, 768), (pc, 0, CTX))[:2 if with_ctx else 1]
                        for dst, a, b in dsts:
                            for k in range(FT):
                                mm = matmul(dst, parts[k // 8][:, k % 8, 128 * h:128 * h + 128], act_ff[:, k, a:b],
                                               start=(k == 0), stop=(k == FT - 1))
                                if h and dst is dsts[-1][0] and k in (7, 15):
                                    mm.then_inc(slot_used, 1)
                        mm.then_inc(ready["dve"], 1)
                        used_up[0] += h

            pe.wait_ge(consts_in, 32)
            pe.wait_ge(cond_ready, w.next(cond_ready, 2))
            for layer in range(2):
                modulation(0)
                mean_square()
                input_projection()
                group_norm(0)
                key_norm()
                lora, gup = take_slot(), take_slot()
                pe.wait_ge(lo_tanh, w.next(lo_tanh))
                pe.wait_ge(state, w.next(state))
                for turns in (CS, XS):
                    recurrence(lora, turns)
                group_norm(4)
                mix_out(gup)
                output_projection(layer == 0)
                mean_square()
                feed_forward(layer == 0)
            mean_square()

            def qkv():
                pe.wait_ge(h_ready, w.next(h_ready, KT))
                for cols, used in ((256, 1), (256, 1), (128, 1)):
                    wt = take_slot().rearrange("p (k c) -> p k c", k=KT)
                    for t in range(TK):
                        j, stands, n_stands = banks.place("act")
                        if stands:
                            pe.wait_ge(freed[stands], n_stands)
                        c = P * t if t < 2 else XO + P * (t - 2)
                        for k in range(KT):
                            mm = matmul(psum[:, 2 * j, 0:cols], ht[:, k, c:c + P], wt[:, k, 0:cols], start=(k == 0), stop=(k == KT - 1))
                        mm.then_inc(ready["act"], 1)
                    used_up[0] += used
                for t in range(7):
                    wt = take_slot().rearrange("p (k c) -> p k c", k=KT)
                    for h in range(2):
                        product("act", [(wt[:, k, 128 * h:128 * h + 128], ht[:, k, :]) for k in range(KT)],
                                with_ctx=t in (0, 5, 6), used=h)
                for t in range(6):
                    pe.wait_ge(head_sq, w.next(head_sq))
                    j, stands, n_stands = banks.place("dve")
                    if stands:
                        pe.wait_ge(freed[stands], n_stands)
                    mm = matmul(psum[:, 2 * j, :], Cn("head_mean"), sq_buf[:, t, CTX:KEYS], start=True, stop=True)
                    if t < 2:
                        mm = matmul(psum[:, 2 * j + 1, 0:CTX], Cn("head_mean"), sq_buf[:, t, 0:CTX], start=True, stop=True)
                    mm.then_inc(ready["dve"], 1)
                for t in range(14):
                    if t < 6:
                        pe.wait_ge(qk_normed, w.next(qk_normed))
                    j, stands, n_stands = banks.place("dve")
                    if stands:
                        pe.wait_ge(freed[stands], n_stands)
                    src = k_buf[:, t, CTX:KEYS] if t < 2 else q_buf[:, t - 2, :] if t < 10 else k_buf[:, t - 8, CTX:KEYS]
                    matmul(psum[:, 2 * j, :], C2("rot"), src, start=True, stop=True).then_inc(ready["dve"], 1)

            def attention():
                pe.wait_ge(roped, w.next(roped, 14))
                pending = []

                def turn_over(n):
                    pe.wait_ge(prob_ready, w.next(prob_ready))
                    j, stands, n_stands = banks.place("act")
                    if stands:
                        pe.wait_ge(freed[stands], n_stands)
                    for t in range(TK):
                        b, c = divmod(P * t, 512)
                        mm = pe.transpose(psum[:, 2 * j + b, c:c + P], prob[:, GROUP_PROB[n], P * t:P * t + P], ident)
                    mm.then_inc(ready["act"], 1)

                def weigh(head):
                    pe.wait_ge(freed["act"], banks.n["act"])
                    j, stands, n_stands = banks.place("act")
                    if stands:
                        pe.wait_ge(freed[stands], n_stands)
                    rows = slice(0, P) if head >= 8 else slice(64 * (head % 2), 64 * (head % 2) + 64)
                    c = 64 * (head // 4) if head < 8 else 128 + 128 * (head - 8)
                    for t in range(TK):
                        mm = matmul(psum[rows, 2 * j, :], v_buf[:, t, c:c + (128 if head >= 8 else 64)], pt_buf[:, head % 2, t, :],
                                    start=(t == 0), stop=(t == TK - 1))
                    mm.then_inc(ready["act"], 1)

                for n, (head, qt, maps) in enumerate(GROUPS):
                    for kind, tile, key, r in maps:
                        j, stands, n_stands = banks.place("act")
                        if stands:
                            pe.wait_ge(freed[stands], n_stands)
                        q = q_buf[r, tile, P * qt:P * qt + P]
                        matmul(psum[:, 2 * j, :], q, k_buf[r, key, 0:512], start=True, stop=True)
                        matmul(psum[:, 2 * j + 1, 0:KEYS - 512], q, k_buf[r, key, 512:KEYS], start=True, stop=True
                               ).then_inc(ready["act"], 1)
                    if n >= 1:
                        turn_over(n - 1)
                        if n >= 1 and GROUPS[n - 1][1] == TQ - 1:
                            weigh(GROUPS[n - 1][0])
                turn_over(len(GROUPS) - 1)
                weigh(GROUPS[-1][0])
                for t in range(4):
                    pe.wait_ge(head_sq, w.next(head_sq))
                    j, stands, n_stands = banks.place("dve")
                    if stands:
                        pe.wait_ge(freed[stands], n_stands)
                    matmul(psum[:, 2 * j, :], Cn("mean_dm"), q_buf[:, t, :], start=True, stop=True).then_inc(ready["dve"], 1)

            def routing():
                pe.wait_ge(h_ready, w.next(h_ready, KT))
                misc = take_slot()
                for t in range(TQ):
                    j, stands, n_stands = banks.place("dve")
                    if stands:
                        pe.wait_ge(freed[stands], n_stands)
                    for k in range(KT):
                        mm = matmul(psum[:, 2 * j, 0:NE], ht[:, k, XO + P * t:XO + P * t + P], misc[:, NE * k:NE * k + NE],
                                    start=(k == 0), stop=(k == KT - 1))
                    mm.then_inc(ready["dve"], 1)
                for t in range(TQ):
                    j, stands, n_stands = banks.place("act")
                    if stands:
                        pe.wait_ge(freed[stands], n_stands)
                    for k in range(KT):
                        mm = pe.transpose(psum[:, 2 * j + k // 4, P * (k % 4):P * (k % 4) + P], ht[:, k, XO + P * t:XO + P * t + P], ident)
                    mm.then_inc(ready["act"], 1)
                pe.wait_ge(gates_ready, w.next(gates_ready))
                for t in range(TQ + 1):
                    j, stands, n_stands = banks.place("dve")
                    if stands:
                        pe.wait_ge(freed[stands], n_stands)
                    terms = [(C2("ones"), picked[:, u, :]) for u in range(min(t, TQ))] + ([(C2("before"), picked[:, t, :])] if t < TQ else [])
                    for n, (lhs, rhs) in enumerate(terms):
                        mm = matmul(psum[:, 2 * j, 0:NE], lhs, rhs, start=(n == 0), stop=(n == len(terms) - 1))
                    mm.then_inc(ready["dve"], 1)
                j, stands, n_stands = banks.place("dve")
                if stands:
                    pe.wait_ge(freed[stands], n_stands)
                for t in range(TQ):
                    mm = pe.transpose(psum[0:NE, 2 * j, P * t:P * t + P], gates[:, t, 0:NE], ident)
                mm.then_inc(ready["dve"], 1)
                pe.wait_ge(freed["dve"], banks.n["dve"])
                for k in range(KT):
                    j, stands, n_stands = banks.place("dve")
                    if stands:
                        pe.wait_ge(freed[stands], n_stands)
                    mm = matmul(psum[:, 2 * j, :], misc[0:NE, 256 + P * k:256 + P * k + P], gate_t[0:NE, :], start=True, stop=True)
                    mm.then_inc(ready["dve"], 1)
                used_up[0] += 1
                for o in ("dve", "act"):
                    pe.wait_ge(freed[o], banks.n[o])
                banks.last = {}

            def gather():
                for k in range(KT):
                    for t in range(TQ):
                        mm = matmul(psum[:, 4 + k // 4, P * (k % 4):P * (k % 4) + P], htok[:, t, P * k:P * k + P], sel[:, t, :],
                                    start=(t == 0), stop=(t == TQ - 1))
                mm.then_inc(ready["act"], 1)

            def add_back(turn, k):
                pe.matmul(psum[:, 4 + k % 4, :], y_sel[:, P * k:P * k + P], spread, start=True, stop=True).then_inc(ready["dve"], 1)

            def experts(loops, slots_before):
                base = dict(banks.n)
                loads = [16 * ((slots_before + s) // RING) for s in range(RING)]
                with w.loop(pe, loops, {sel_ready: 1, gate_ready: 1, act_ready: 1}) as (i, _):
                    turn = Turn(base, i)
                    used_up[0] = 1
                    n_slot = [0]

                    def slot_of_turn():
                        n = n_slot[0]
                        n_slot[0] += 1
                        pe.wait_ge(slot_loaded[n % RING], i * (16 * EXPERT_SLOTS // RING) + (loads[n % RING] + 16 * (n // RING + 1)))
                        return ring[:, n % RING, :]

                    pe.wait_ge(freed["act"], turn.count("gather", True))
                    for o, n in turn.stands("hidden"):
                        pe.wait_ge(freed[o], n)
                    for k in range(KT):
                        wt = slot_of_turn()
                        for f in range(16):
                            mm = matmul(psum[:, f // 4, P * (f % 4):P * (f % 4) + P], wt[:, P * f:P * f + P], x_sel[:, k, :],
                                        start=(k == 0 and f % 4 == 0), stop=(k == KT - 1), skip_group_check=True)
                        if k < KT - 1:
                            used_up[0] += 1
                    mm.then_inc(ready["dve"], 1)
                    used_up[0] += 1
                    pe.wait_ge(freed["dve"], turn.count("spread", True))
                    pe.wait_ge(freed["act"], turn.count("expert_out", True))
                    for k in range(KT):
                        for o, n in turn.stands(f"add{k}"):
                            pe.wait_ge(freed[o], n)
                        add_back(turn, k)
                    pe.wait_ge(sel_ready, w.next(sel_ready))
                    for o, n in turn.stands("gather"):
                        pe.wait_ge(freed[o], n)
                    gather()
                    pe.wait_ge(gate_ready, w.next(gate_ready))
                    for o, n in turn.stands("spread"):
                        pe.wait_ge(freed[o], n)
                    for t in range(TQ):
                        mm = pe.transpose(psum[:, 0, P * t:P * t + P], sel_gate[:, t, :], ident)
                    mm.then_inc(ready["dve"], 1)
                    pe.wait_ge(act_ready, w.next(act_ready))
                    for o, n in turn.stands("expert_out"):
                        pe.wait_ge(freed[o], n)
                    for h in range(4):
                        wt = slot_of_turn().rearrange("p (f c) -> p f c", f=2)
                        for f in range(2):
                            for c in range(2):
                                mm = matmul(psum[:, 6 + c, :], sig[:, P * (2 * h + f):P * (2 * h + f) + P], wt[:, f, 512 * c:512 * c + 512],
                                            start=(h == 0 and f == 0), stop=(h == 3 and f == 1))
                        used_up[0] += 1
                    mm.then_inc(ready["act"], 1)
                    assert used_up[0] == 1
                for o in ("dve", "act"):
                    banks.n[o] += int(np.prod(loops)) * EPLAN_N[o]

            def first_gather():
                pe.wait_ge(sel_ready, w.next(sel_ready))
                gather()
                banks.n["act"] += 1
                pe.wait_ge(freed["act"], banks.n["act"])

            def last_add():
                pe.wait_ge(freed["dve"], banks.n["dve"])
                pe.wait_ge(freed["act"], banks.n["act"])
                for k in range(KT):
                    if k >= 4:
                        pe.wait_ge(freed["dve"], banks.n["dve"] - 3)
                    add_back(None, k)
                    banks.n["dve"] += 1
                for o in ("dve", "act"):
                    pe.wait_ge(freed[o], banks.n[o])
                banks.last = {}

            modulation(1)
            mean_square()
            qkv()
            attention()
            output_projection_2()
            mean_square()
            routing()
            first_gather()
            take_slot()
            used_up[0] += 1
            experts([NE], MIX_SLOTS)
            last_add()
            pe.wait_ge(rank_ready, 1)
            over = pe.alloc_register("over_pe")
            pe.reg_load(over, flag[0:1, 0:1].bitcast(mybir.dt.int32))
            with pe.If_eq(over, 1):
                pe.wait_ge(cleared, w.next(cleared))
                experts([ROUNDS - 1, NE], MIX_SLOTS + NE * EXPERT_SLOTS)
                last_add()
            pe.wait_ge(fin_sq, 1)
            for k in range(KT):
                mm = pe.matmul(psum[:, 0, :], Cn("mean_dm"), xs(ht[:, k, :]), start=(k == 0), stop=(k == KT - 1))
            mm.then_inc(fin_ms, 1)
            pe.wait_ge(fin_x, KT)
            for t in range(TQ):
                for k in range(KT):
                    mm = pe.transpose(psum[:, 2 * t + k // 4, P * (k % 4):P * (k % 4) + P], xt[:, k, XO + P * t:XO + P * t + P], ident)
                mm.then_inc(fin_tok, 1)

        @block.vector
        def _(dve):
            w = Counts()
            banks = Results()
            tt, ts, stt = dve.tensor_tensor, dve.tensor_scalar, dve.scalar_tensor_tensor


            def modulation(layer):
                for q in range(6):
                    banks.pair("act")
                    j = banks.pair("dve")
                    dve.wait_ge(ready["dve"], banks.n["dve"])
                    tt(mod[:, q], psum[:, 2 * j, 0:16].rearrange("p (k c) -> p k c", k=KT), V(f"ada_b{layer}", 8 * q, 8).rearrange("p (k c) -> p k c", c=1).to_broadcast([P, KT, 2]), ALU.add).then_inc(freed["dve"], 1)
                    dve.wait_ge(freed["dve"], banks.n["dve"])
                    if q in (1, 4):
                        g = V(f"norm{1 + q // 4}{layer}", 0, 8).rearrange("p (k c) -> p k c", c=1).to_broadcast([P, KT, 2])
                        stt(gain[:, q // 4], mod[:, q], 1.0, g, ALU.add, ALU.mult).then_inc(dve_chain, 1)
                        dve.wait_ge(dve_chain, w.next(dve_chain))

            def norm(which, final=None):
                tt(ht[:, 4:8, :], xt[:, 4:8, :], xt[:, 4:8, :], ALU.mult).then_inc(sq_dve, 1)
                j = banks.pair("dve")
                dve.wait_ge(ready["dve"], banks.n["dve"])
                px, pc = halves(j)
                ts(xs(rs), px, 1e-6, None, ALU.add)
                ts(cs(rs), pc, 1e-6, None, ALU.add).then_inc(freed["dve"], 1)
                dve.wait_ge(std_ready, w.next(std_ready))
                dve.reciprocal(rs, rs).then_inc(dve_chain, 1)
                dve.wait_ge(dve_chain, w.next(dve_chain))
                for k in range(KT):
                    if final:
                        stt(xs(xt[:, k, :]), xs(xt[:, k, :]), V(final, k), xs(rs), ALU.mult, ALU.mult).then_inc(dve_chain, 1)
                        dve.wait_ge(dve_chain, w.next(dve_chain))
                        continue
                    stt(xs(ht[:, k, :]), xs(xt[:, k, :]), gain[:, which, k, 0:1], xs(rs), ALU.mult, ALU.mult)
                    stt(cs(ht[:, k, :]), cs(xt[:, k, :]), gain[:, which, k, 1:2], cs(rs), ALU.mult, ALU.mult).then_inc(normed, 1)

            def clear_pads():
                dve.memset(zp, 0.0)
                dve.memset(tmp, 0.0).then_inc(zeroed, 1)
                dve.wait_ge(zeroed, w.next(zeroed))

            def gated_values(layer):
                for t in range(2):
                    for _ in range(2):
                        banks.pair("act")
                    for h in range(2):
                        c = 2 * t + h
                        j = banks.pair("dve")
                        dve.wait_ge(ready["dve"], banks.n["dve"])
                        px, pc = halves(j)
                        dve.wait_ge(freed["act"], banks.n["act"] - 1 + h)
                        z = zp[:, c, GAP:GAP + W]
                        tt(grid(xs(z), layer), natural(px), grid(xs(kk[:, c, :]), layer), ALU.mult)
                        tt(cs(z), pc, cs(kk[:, c, :]), ALU.mult).then_inc(freed["dve"], 1)

            def token_shift(layer):
                for n in range(16):
                    banks.pair("act")
                    dve.wait_ge(freed["act"], banks.n["act"])
                    rows = 64 if n in (12, 13) else 32 if n == 15 else P
                    dst = (rkv[:, n, :] if n < 12 else lo[:, n - 12, :])[0:rows]
                    src = tmp[0:rows, n % 2, :]
                    tap = lambda k: V(f"shift_w{layer}", 3 * n + k)[0:rows]
                    ts(dst, src[:, 1:1 + W], tap(1), None, ALU.mult).then_inc(dve_chain, 1)
                    dve.wait_ge(dve_chain, w.next(dve_chain))
                    stt(dst, src[:, 0:W], tap(0), dst, ALU.mult, ALU.add).then_inc(dve_chain, 1)
                    dve.wait_ge(dve_chain, w.next(dve_chain))
                    stt(dst, src[:, 2:2 + W], tap(2), dst, ALU.mult, ALU.add).then_inc(raw_used, 1)
                    dve.wait_ge(raw_used, w.next(raw_used))
                dve.memset(lo[64:65, 0:2, :], 1.0).then_inc(shifted, 1)

            def long_convolution(layer):
                for k in range(TAPS):
                    for c in range(4):
                        src, wt = zp[:, c, k:k + W], V(f"conv_w{layer}", c * TAPS + k)
                        if k:
                            dve.wait_ge(dve_chain, w.seen[dve_chain] - 3)
                            ins = stt(ht[:, c, :], src, wt, ht[:, c, :], ALU.mult, ALU.add)
                        else:
                            ins = ts(ht[:, c, :], src, wt, V(f"conv_b{layer}", c), ALU.mult, ALU.add)
                        ins.then_inc(dve_chain, 1)
                        w.skip(dve_chain)
                dve.memset(ht[:, 4:8, :], 0.0).then_inc(conv_out, 1)
                dve.wait_ge(conv_out, w.next(conv_out))

            def root_scale(target, eps, floor=None):
                for t in range(4):
                    j = banks.pair("dve")
                    dve.wait_ge(ready["dve"], banks.n["dve"])
                    px, pc = halves(j)
                    ts(xs(scr[:, t, :]), px, eps, None, ALU.add)
                    ts(cs(scr[:, t, :]), pc, eps, None, ALU.add).then_inc(freed["dve"], 1)
                for t in range(4):
                    dve.wait_ge(gstd, w.next(gstd))
                    for f in (xs, cs):
                        s = f(scr[:, t, :])
                        if floor:
                            ts(s, s, floor, None, ALU.max).then_inc(dve_chain, 1)
                            dve.wait_ge(dve_chain, w.next(dve_chain))
                        dve.reciprocal(s, s).then_inc(dve_chain, 1)
                        dve.wait_ge(dve_chain, w.next(dve_chain))
                        ins = tt(f(target[:, t, :]), f(target[:, t, :]), s, ALU.mult)
                    ins.then_inc(grp_normed, 1)
                    dve.wait_ge(grp_normed, w.next(grp_normed))

            def group_norm(base, eps):
                for t in range(4):
                    j = banks.pair("dve")
                    dve.wait_ge(ready["dve"], banks.n["dve"])
                    px, pc = halves(j)
                    b = ht[:, base + t, :]
                    tt(xs(b), xs(b), px, ALU.subtract)
                    tt(cs(b), cs(b), pc, ALU.subtract).then_inc(freed["dve"], 1)
                    dve.wait_ge(freed["dve"], banks.n["dve"])
                root_scale(ht[:, base:base + 4, :], eps)

            def key_norm(layer):
                for t in range(4):
                    ins = ts(kk[:, t, :], rkv[:, 4 + t, :], V(f"k_k{layer}", t), None, ALU.mult)
                ins.then_inc(kk_raw, 1)
                root_scale(kk, 0.0, 1e-12)

            def recurrence(layer, turns):
                base = dict(banks.n)
                own_n = 14
                per = {dve_chain: own_n, r_cum: 1, r_pow: 4, r_fac: 2, r_inv: 2}
                with w.loop(dve, [turns], per) as (i, _):
                    col = {0: i * C + f0[turns], 1: i * (-C) + b0[turns]}

                    def panel(name, g):
                        bank, o, n = PLAN[name, g]
                        dve.wait_ge(ready[o], i * PLAN_N[o] + (base[o] + n))
                        if name[0] in "xz":
                            dve.sem_inc(passed_dve, 1)
                        return psum[:, bank, :]

                    def read(name, g, ins, own=True):
                        _, o, n = PLAN[name, g]
                        ins.then_inc(freed[o], 1)
                        if own:
                            dve.wait_ge(freed[o], i * PLAN_N[o] + (base[o] + n))

                    dve.wait_ge(freed["act"], i * PLAN_N["act"] + (base["act"] + PLAN["rate", 1][2]))
                    ts(R_sgaa, R_sgaa, 1.0, None, ALU.add).then_inc(dve_chain, 1)
                    dve.wait_ge(dve_chain, w.next(dve_chain))
                    dve.reciprocal(R_sgaa, R_sgaa).then_inc(dve_chain, 1)
                    dve.wait_ge(dve_chain, w.next(dve_chain))
                    dve.tensor_tensor_scan(wide(2), Cn("scan"), wide(0), 0.0, ALU.mult, ALU.add).then_inc(dve_chain, 1)
                    dve.wait_ge(dve_chain, w.next(dve_chain))
                    dve.tensor_copy(R_tot.rearrange("p (g k) -> p g k", g=2), R_li[:, :, :, C - 1]).then_inc(dve_chain, 1)
                    dve.wait_ge(dve_chain, w.next(dve_chain))
                    tot1 = R_tot[:, 4:8].rearrange("p (k c) -> p k c", c=1).to_broadcast([P, 4, C])
                    tt(R_lx[:, 1], tot1, R_li[:, 1], ALU.subtract).then_inc(dve_chain, 1)
                    dve.wait_ge(dve_chain, w.next(dve_chain))
                    tt(R_lx[:, 0], R_li[:, 0], R_sg[:, 0], ALU.subtract)
                    tt(R_li[:, 1], R_lx[:, 1], R_sg[:, 1], ALU.add).then_inc(r_cum, 1)
                    dve.wait_ge(r_cum, w.next(r_cum))
                    k_a = V(f"k_a{layer}", 0, 4).rearrange("p (k c) -> p k c", c=1).to_broadcast([P, 4, C])
                    for g in range(2):
                        tt(R_bh[:, g], chunk(kk, col[g]), R_aa[:, g], ALU.mult).then_inc(dve_chain, 1)
                        dve.wait_ge(dve_chain, w.next(dve_chain))
                        stt(R_aa[:, g], R_aa[:, g], -1.0, k_a, ALU.add, ALU.mult).then_inc(dve_chain, 1)
                        dve.wait_ge(dve_chain, w.next(dve_chain))
                        stt(R_aa[:, g], R_aa[:, g], 1.0, chunk(rkv[:, 4:8, :], col[g]), ALU.add, ALU.mult).then_inc(dve_chain, 1)
                        dve.wait_ge(dve_chain, w.next(dve_chain))
                    dve.wait_ge(r_pow, w.next(r_pow, 4))
                    for g in range(2):
                        stt(R_kr[:, g, :, 0:C], chunk(kk, col[g]), -1.0, R_kr[:, g, :, 0:C], ALU.mult, ALU.mult)
                        tt(R_kr[:, g, :, C:], R_kr[:, g, :, C:], chunk(rkv[:, 0:4, :], col[g]), ALU.mult)
                    tt(wide(7), wide(7), R_pi, ALU.mult)
                    tt(wide(1), wide(1), R_pi, ALU.mult).then_inc(r_fac, 1)
                    dve.wait_ge(r_fac, w.next(r_fac))
                    pc = R_pc.rearrange("p (k c) -> p k c", c=1)
                    pc512 = pc.to_broadcast([P, 8, C])
                    flat8 = lambda t: t.rearrange("p (k c) -> p k c", k=8)
                    tt(flat8(wide(8)), flat8(wide(7)), pc512, ALU.mult)
                    tt(flat8(wide(9)), flat8(wide(1)), pc512, ALU.mult).then_inc(r_fac, 1)
                    dve.wait_ge(r_fac, w.next(r_fac))
                    tri = Cn("tri").rearrange("p (g o h c) -> p g o h c", g=2, o=1, h=2)
                    for name, dst in (("q1", R_m1), ("q2", R_m2)):
                        for g in range(2):
                            ps = panel(name, g).rearrange("p (k h c) -> p k h c", k=4, h=2)
                            read(name, g, tt(dst[:, g], ps, tri[:, g].to_broadcast([P, 4, 2, C]), ALU.mult))
                    one = id64.rearrange("p (o c) -> p o c", o=1).to_broadcast([P, 4, C])
                    low1 = Cn("level1").rearrange("p (h o c) -> p h o c", h=2, o=1)
                    for g in range(2):
                        ps = panel("q3", g)[:, 0:256].rearrange("p (k c) -> p k c", k=4)
                        read("q3", g, tt(R_x[:, g], ps, low1[:, g].to_broadcast([P, 4, C]), ALU.mult))
                        tt(R_z[:, g], R_m1[:, g, :, 0, :], low1[:, 1 - g].to_broadcast([P, 4, C]), ALU.mult).then_inc(dve_chain, 1)
                        dve.wait_ge(dve_chain, w.next(dve_chain))
                        tt(R_x[:, g], R_x[:, g], one, ALU.add)
                        tt(R_z[:, g], R_z[:, g], one, ALU.add).then_inc(r_inv, 1)
                        dve.wait_ge(r_inv, w.next(r_inv))
                    low = Cn("level").bitcast(U32).rearrange("p (m h o c) -> p m h o c", m=len(LEVELS), h=2, o=1)
                    for n, m in enumerate(LEVELS):
                        for name, dst, h in ((f"x{m}", R_x, 0), (f"z{m}", R_z, 1)):
                            if (name, 0) not in PLAN:
                                continue
                            for g in range(2):
                                ps = panel(name, g)[:, 0:256].rearrange("p (k c) -> p k c", k=4)
                                mask = low[:, n, (g + h) % 2].to_broadcast([P, 4, C])
                                read(name, g, dve.copy_predicated(dst[:, g], mask, ps))
                    for g in range(2):
                        ps = panel("y", g)[:, 0:256].rearrange("p (k c) -> p k c", k=4)
                        y = chunk(ht[:, 4:8, :], col[g])
                        read("y", g, tt(y, ps, y, ALU.add))
                    tt(flat8(wide(20)), flat8(wide(20)), pc512, ALU.mult).then_inc(dve_chain, 1)
                    dve.wait_ge(dve_chain, w.next(dve_chain))
                    for g in range(2):
                        ps = panel("s", g)[:, 0:256].rearrange("p (k c) -> p k c", k=4)
                        read("s", g, tt(R_s[:, g], R_s[:, g], ps, ALU.add))
                for o in ("dve", "act"):
                    banks.n[o] += turns * PLAN_N[o]

            def mix_out(layer):
                r, k, v = rkv[:, 0:4, :], rkv[:, 4:8, :], rkv[:, 8:12, :]
                for t in range(4):
                    ins = stt(scr[:, t, :], r[:, t, :], V(f"r_k{layer}", t), k[:, t, :], ALU.mult, ALU.mult)
                ins.then_inc(bonus_in, 1)
                for t in range(4):
                    j = banks.pair("dve")
                    dve.wait_ge(ready["dve"], banks.n["dve"])
                    px, pc = halves(j)
                    dve.wait_ge(y_scaled, w.next(y_scaled))
                    for f, ps in ((xs, px), (cs, pc)):
                        ins = tt(f(scr[:, t, :]), ps, f(v[:, t, :]), ALU.mult)
                    ins.then_inc(freed["dve"], 1)
                    dve.wait_ge(freed["dve"], banks.n["dve"])
                    for f in (xs, cs):
                        ins = tt(f(scr[:, t, :]), f(scr[:, t, :]), f(ht[:, 4 + t, :]), ALU.add)
                    ins.then_inc(dve_chain, 1)
                    dve.wait_ge(dve_chain, w.next(dve_chain))
                for t in range(4):
                    j = banks.pair("dve")
                    dve.wait_ge(ready["dve"], banks.n["dve"])
                    px, pc = halves(j)
                    tt(xs(ht[:, 4 + t, :]), px, xs(scr[:, t, :]), ALU.mult)
                    tt(cs(ht[:, 4 + t, :]), pc, cs(scr[:, t, :]), ALU.mult).then_inc(freed["dve"], 1)

            def add_gated(gate, layer, with_ctx, permuted):
                for k in range(KT):
                    j = banks.pair("dve")
                    dve.wait_ge(ready["dve"], banks.n["dve"])
                    px, pc = halves(j)
                    x = xs(xt[:, k, :])
                    if permuted and layer == 1:
                        x = x.rearrange("p (r c) -> p c r", c=GRID_W)
                        px = px.rearrange("p (c r) -> p c r", r=GRID_R)
                    ins = stt(x, px, mod[:, gate, k, 0:1], x, ALU.mult, ALU.add)
                    if with_ctx:
                        c = cs(xt[:, k, :])
                        ins = stt(c, pc, mod[:, gate, k, 1:2], c, ALU.mult, ALU.add)
                    ins.then_inc(freed["dve"], 1)
                    if k == KT - 1:
                        dve.wait_ge(freed["dve"], banks.n["dve"])

            def feed_forward(with_ctx):
                for t in range(FT // 2):
                    for _ in range(2):
                        banks.pair("act")
                    for h in range(2):
                        n = 2 * t + h
                        j = banks.pair("dve")
                        dve.wait_ge(ready["dve"], banks.n["dve"])
                        px, pc = halves(j)
                        dve.wait_ge(freed["act"], banks.n["act"] - 1 + h)
                        s = silu_ff[:, n % 4, :]
                        ins = tt(act_ff[:, n, CTX:768], px, s[:, CTX:768], ALU.mult)
                        if with_ctx:
                            ins = tt(act_ff[:, n, 0:CTX], pc, s[:, 0:CTX], ALU.mult)
                        ins.then_inc(freed["dve"], 1)

            def updated():
                dve.memset(mark, 0.0).then_inc(x_updated, 1)
                dve.wait_ge(x_updated, w.next(x_updated))

            dve.wait_ge(consts_in, 32)
            dve.memset(xt[:, :, CTX:XO], 0.0).then_inc(dve_chain, 1)
            dve.wait_ge(dve_chain, w.next(dve_chain))
            dve.memset(rs, 1.0).then_inc(dve_chain, 1)
            dve.wait_ge(dve_chain, w.next(dve_chain))
            dve.memset(junk, 0.0).then_inc(dve_chain, 1)
            dve.wait_ge(dve_chain, w.next(dve_chain))
            dve.wait_ge(x_in, 16 * 2 * KT)
            for layer in range(2):
                updated()
                modulation(layer)
                clear_pads()
                norm(0)
                gated_values(layer)
                token_shift(layer)
                long_convolution(layer)
                group_norm(0, 1e-5)
                key_norm(layer)
                dve.memset(wide(20), 0.0).then_inc(state, 1)
                dve.wait_ge(state, w.next(state))
                for turns in (CS, XS):
                    recurrence(layer, turns)
                group_norm(4, 64e-5)
                mix_out(layer)
                add_gated(2, layer, layer == 0, True)
                updated()
                norm(1)
                feed_forward(layer == 0)
                add_gated(5, layer, layer == 0, False)
            updated()
            norm(0, "final1")

            def lambdas():
                v = C2("lam").rearrange("p (a b c) -> p a b c", a=2, b=2)
                prod = rope_tmp[:, 0:2 * 64].rearrange("p (a c) -> p a c", a=2)
                tt(prod, v[:, :, 0, :], v[:, :, 1, :], ALU.mult).then_inc(dve_chain, 1)
                dve.wait_ge(dve_chain, w.next(dve_chain))
                dve.tensor_reduce(lam[:, 0:2], prod, AX_X, ALU.add).then_inc(lam_ready, 1)
                dve.wait_ge(lam_ready, w.next(lam_ready))
                dve.wait_ge(lam_exp, w.next(lam_exp))
                stt(lam[:, 4:5], lam[:, 3:4], -LAMBDA_INIT, lam[:, 2:3], ALU.add, ALU.subtract).then_inc(dve_chain, 1)
                dve.wait_ge(dve_chain, w.next(dve_chain))
                ts(lam[:, 5:6], V("subln"), 1.0 - LAMBDA_INIT, None, ALU.mult).then_inc(dve_chain, 1)
                dve.wait_ge(dve_chain, w.next(dve_chain))

            def norm_and_rope():
                for _ in range(3 * TK + 14):
                    banks.pair("act")
                for t in range(6):
                    j = banks.pair("dve")
                    dve.wait_ge(ready["dve"], banks.n["dve"])
                    ins = ts(sq_buf[:, t, CTX:KEYS], psum[:, 2 * j, :], 1e-6, None, ALU.add)
                    if t < 2:
                        ins = ts(sq_buf[:, t, 0:CTX], psum[:, 2 * j + 1, 0:CTX], 1e-6, None, ALU.add)
                    ins.then_inc(freed["dve"], 1)
                for t in range(6):
                    dve.wait_ge(gstd, w.next(gstd))
                    dst, a = (k_buf[:, t, :], 0) if t < 2 else (q_buf[:, t - 2, :], CTX)
                    r = sq_buf[:, t, a:KEYS]
                    dve.reciprocal(r, r).then_inc(dve_chain, 1)
                    dve.wait_ge(dve_chain, w.next(dve_chain))
                    stt(dst, dst, V("k_norm" if t < 2 else "q_norm"), r, ALU.mult, ALU.mult).then_inc(qk_normed, 1)
                    dve.wait_ge(qk_normed, w.next(qk_normed))
                for t in range(14):
                    j = banks.pair("dve")
                    dve.wait_ge(ready["dve"], banks.n["dve"])
                    dst = k_buf[:, t, CTX:KEYS] if t < 2 else q_buf[:, t - 2, :] if t < 10 else k_buf[:, t - 8, CTX:KEYS]
                    tt(rope_tmp, psum[:, 2 * j, :], C2("sin"), ALU.mult).then_inc(freed["dve"], 1)
                    tt(dst, dst, C2("cos"), ALU.mult).then_inc(dve_chain, 1)
                    dve.wait_ge(dve_chain, w.next(dve_chain))
                    tt(dst, dst, rope_tmp, ALU.add).then_inc(roped, 1)
                    dve.wait_ge(roped, w.next(roped))

            def attention():
                numbers, n_map = [], 0

                def finish(n):
                    nums, first = numbers[n]
                    dve.wait_ge(freed["act"], nums[-1])
                    a = prob[:, first % 4, :]
                    m = len(nums)
                    dve.reciprocal(row_inv[:, first:first + m], row_sum[:, first:first + m]).then_inc(dve_chain, 1)
                    dve.wait_ge(dve_chain, w.next(dve_chain))
                    if m == 1:
                        ts(a, a, row_inv[:, first:first + 1], None, ALU.mult).then_inc(prob_ready, 1)
                        dve.wait_ge(prob_ready, w.next(prob_ready))
                        return
                    ts(a, a, row_inv[:, first:first + 1], None, ALU.mult)
                    tt(row_inv[:, first + 1:first + 2], row_inv[:, first + 1:first + 2], lam[:, 4:5], ALU.mult).then_inc(dve_chain, 1)
                    dve.wait_ge(dve_chain, w.next(dve_chain))
                    stt(a, prob[:, (first + 1) % 4, :], row_inv[:, first + 1:first + 2], a, ALU.mult, ALU.add).then_inc(prob_ready, 1)
                    dve.wait_ge(prob_ready, w.next(prob_ready))

                for n, (head, qt, maps) in enumerate(GROUPS):
                    nums = []
                    for c in range(len(maps)):
                        j = banks.pair("act")
                        nums.append(banks.n["act"])
                        dve.wait_ge(ready["act"], banks.n["act"])
                        nm = neg_max[:, n_map + c:n_map + c + 1]
                        dve.tensor_reduce(nm, psum[:, 2 * j:2 * j + 2, :].rearrange("p b c -> p (b c)")[:, 0:KEYS], AX_X, ALU.max).then_inc(dve_chain, 1)
                        dve.wait_ge(dve_chain, w.next(dve_chain))
                        ts(nm, nm, -0.125, None, ALU.mult).then_inc(maxed, 1)
                        dve.wait_ge(maxed, w.next(maxed))
                    numbers.append((nums, n_map))
                    n_map += len(maps)
                    if n >= 1:
                        finish(n - 1)
                        banks.pair("act")
                        if GROUPS[n - 1][1] == TQ - 1:
                            banks.pair("act")
                finish(len(GROUPS) - 1)
                banks.pair("act")
                banks.pair("act")
                for t in range(4):
                    j = banks.pair("dve")
                    dve.wait_ge(ready["dve"], banks.n["dve"])
                    ts(q_buf[:, t, :], psum[:, 2 * j, :], 8.0, 1e-6, ALU.mult, ALU.add).then_inc(freed["dve"], 1)
                for t in range(4):
                    dve.wait_ge(gstd, w.next(gstd))
                    dve.reciprocal(q_buf[:, t, :], q_buf[:, t, :]).then_inc(dve_chain, 1)
                    dve.wait_ge(dve_chain, w.next(dve_chain))
                    x = xs(ht[:, 4 + t, :])
                    ins = stt(x, x, lam[:, 5:6], q_buf[:, t, :], ALU.mult, ALU.mult)
                    if t == 3:
                        ins.then_inc(attended, 1)
                        dve.wait_ge(attended, w.next(attended))

            def routing():
                for t in range(TQ):
                    j = banks.pair("dve")
                    dve.wait_ge(ready["dve"], banks.n["dve"])
                    tt(logit[:, t, :], psum[:, 2 * j, 0:NE], C2("b_router"), ALU.add).then_inc(freed["dve"], 1)
                    dve.wait_ge(freed["dve"], banks.n["dve"])
                for _ in range(TQ):
                    banks.pair("act")
                iota = C2("iota")
                for t in range(TQ):
                    dve.max(top8[:, t, :], logit[:, t, :]).then_inc(dve_chain, 1)
                    dve.wait_ge(dve_chain, w.next(dve_chain))
                    dve.max_index(idx8[:, t, :].bitcast(U32), top8[:, t, :], logit[:, t, :]).then_inc(dve_chain, 1)
                    dve.wait_ge(dve_chain, w.next(dve_chain))
                    ts(expv[:, t, :], top8[:, t, 0:TOPK], top8[:, t, 0:1], None, ALU.subtract).then_inc(dve_chain, 1)
                    dve.wait_ge(dve_chain, w.next(dve_chain))
                dve.tensor_copy(idxf, idx8.bitcast(U32)).then_inc(top_ready, 1)
                dve.wait_ge(top_ready, w.next(top_ready))
                dve.memset(gates, 0.0).then_inc(dve_chain, 1)
                dve.wait_ge(dve_chain, w.next(dve_chain))
                dve.memset(picked, 0.0).then_inc(dve_chain, 1)
                dve.wait_ge(dve_chain, w.next(dve_chain))
                dve.wait_ge(top_exp, w.next(top_exp))
                dve.tensor_reduce(esum, expv, AX_X, ALU.add).then_inc(dve_chain, 1)
                dve.wait_ge(dve_chain, w.next(dve_chain))
                dve.reciprocal(einv, esum).then_inc(dve_chain, 1)
                dve.wait_ge(dve_chain, w.next(dve_chain))
                for t in range(TQ):
                    g = gates[:, t, 0:NE]
                    for j in range(TOPK):
                        ts(hot, iota[:, 0:NE], idxf[:, t, j:j + 1], None, ALU.is_equal).then_inc(dve_chain, 1)
                        dve.wait_ge(dve_chain, w.next(dve_chain))
                        tt(picked[:, t, :], picked[:, t, :], hot, ALU.add).then_inc(dve_chain, 1)
                        dve.wait_ge(dve_chain, w.next(dve_chain))
                        stt(g, hot, expv[:, t, j:j + 1], g, ALU.mult, ALU.add).then_inc(dve_chain, 1)
                        dve.wait_ge(dve_chain, w.next(dve_chain))
                    ts(g, g, einv[:, t:t + 1], None, ALU.mult).then_inc(dve_chain, 1)
                    dve.wait_ge(dve_chain, w.next(dve_chain))
                dve.memset(mark, 0.0).then_inc(gates_ready, 1)
                dve.wait_ge(gates_ready, w.next(gates_ready))
                dve.memset(rank, -1.0).then_inc(dve_chain, 1)
                dve.wait_ge(dve_chain, w.next(dve_chain))
                for t in range(TQ):
                    j = banks.pair("dve")
                    dve.wait_ge(ready["dve"], banks.n["dve"])
                    stt(rank[:, t, 0:NE], psum[:, 2 * j, 0:NE], 1.0, picked[:, t, :], ALU.add, ALU.mult).then_inc(freed["dve"], 1)
                    dve.wait_ge(freed["dve"], banks.n["dve"])
                ts(rank[:, :, 0:NE], rank[:, :, 0:NE], 1.0, None, ALU.subtract).then_inc(dve_chain, 1)
                dve.wait_ge(dve_chain, w.next(dve_chain))
                for r in range(1, ROUNDS):
                    ts(rank[:, :, NE * r:NE * r + NE], rank[:, :, 0:NE], float(CAP * r), None, ALU.subtract)
                    dve.tensor_copy(gates[:, :, NE * r:NE * r + NE], gates[:, :, 0:NE]).then_inc(dve_chain, 1)
                    dve.wait_ge(dve_chain, w.next(dve_chain))
                j = banks.pair("dve")
                dve.wait_ge(ready["dve"], banks.n["dve"])
                dve.tensor_reduce(esum[:, 0:1], psum[:, 2 * j, 0:NE], AX_X, ALU.max).then_inc(freed["dve"], 1)
                dve.wait_ge(freed["dve"], banks.n["dve"])
                ts(flag[:, 0:1].bitcast(mybir.dt.int32), esum[:, 0:1], float(CAP), None, ALU.is_gt).then_inc(rank_ready, 1)
                dve.wait_ge(rank_ready, w.next(rank_ready))
                j = banks.pair("dve")
                dve.wait_ge(ready["dve"], banks.n["dve"])
                dve.tensor_copy(gate_t[0:NE, :], psum[0:NE, 2 * j, :]).then_inc(freed["dve"], 1)
                for k in range(KT):
                    j = banks.pair("dve")
                    dve.wait_ge(ready["dve"], banks.n["dve"])
                    dve.tensor_copy(y_acc[:, k, :], psum[:, 2 * j, :]).then_inc(freed["dve"], 1)
                    if k == KT - 1:
                        dve.wait_ge(freed["dve"], banks.n["dve"])

            def select(dst, col, gated, sem):
                for t in range(TQ):
                    ins = ts(dst[:, t, :], C2("iota"), rank[:, t, bass.ds(col, 1)], gates[:, t, bass.ds(col, 1)] if gated else None,
                             ALU.is_equal, *([ALU.mult] if gated else []))
                ins.then_inc(sem, 1)
                dve.wait_ge(sem, w.next(sem))

            def experts(loops, first):
                base = dict(banks.n)
                with w.loop(dve, loops, {sel_ready: 1, gate_ready: 1, act_ready: 1, glu_ready: 1, sig_ready: 1, dve_chain: 2}) as (i, e):
                    turn = Turn(base, i)
                    dve.wait_ge(freed["act"], turn.count("gather", True))
                    dve.wait_ge(freed["dve"], turn.count("spread", True))
                    select(sel_gate, i + first, True, gate_ready)
                    select(sel, i + (first + 1), False, sel_ready)
                    dve.wait_ge(ready["dve"], turn.count("hidden"))
                    bias = C2("b_in")
                    for dst, b, c in ((glu, 0, 0), (lin, 2, KT)):
                        bc = bias[:, bass.ds(e * 16 + c, KT)].rearrange("p (k c) -> p k c", c=1).to_broadcast([P, KT, P])
                        ins = tt(dst.rearrange("p (k c) -> p k c", k=KT), psum[:, b:b + 2, :].rearrange("p b (k c) -> p (b k) c", c=P), bc, ALU.add)
                    ins.then_inc(freed["dve"], 1)
                    dve.wait_ge(freed["dve"], turn.count("hidden"))
                    ts(glu, glu, LIMIT, None, ALU.min).then_inc(glu_ready, 1)
                    dve.wait_ge(glu_ready, w.next(glu_ready))
                    ts(lin, lin, LIMIT, -LIMIT, ALU.min, ALU.max).then_inc(dve_chain, 1)
                    dve.wait_ge(dve_chain, w.next(dve_chain))
                    stt(lin, lin, 1.0, glu, ALU.add, ALU.mult).then_inc(dve_chain, 1)
                    dve.wait_ge(dve_chain, w.next(dve_chain))
                    dve.wait_ge(sig_ready, w.next(sig_ready))
                    tt(sig, sig, lin, ALU.mult).then_inc(act_ready, 1)
                    dve.wait_ge(act_ready, w.next(act_ready))
                    for k in range(KT):
                        dve.wait_ge(ready["dve"], turn.count(f"add{k}"))
                        tt(y_acc[:, k, :], y_acc[:, k, :], psum[:, 4 + k % 4, :], ALU.add).then_inc(freed["dve"], 1)
                    dve.wait_ge(ready["dve"], turn.count("spread"))
                    dve.tensor_copy(spread, psum[:, 0, :]).then_inc(freed["dve"], 1)
                    dve.wait_ge(freed["dve"], turn.count("spread"))
                for o in ("dve", "act"):
                    banks.n[o] += int(np.prod(loops)) * EPLAN_N[o]

            def last_add():
                for k in range(KT):
                    banks.n["dve"] += 1
                    dve.wait_ge(ready["dve"], banks.n["dve"])
                    tt(y_acc[:, k, :], y_acc[:, k, :], psum[:, 4 + k % 4, :], ALU.add).then_inc(freed["dve"], 1)
                    if k == KT - 1:
                        dve.wait_ge(freed["dve"], banks.n["dve"])

            dve.memset(mark, 0.0).then_inc(attention_free, 1)
            dve.wait_ge(attention_free, w.next(attention_free))
            dve.wait_ge(con2_in, 16)
            dve.wait_ge(ctx2_in, 16)
            updated()
            lambdas()
            modulation(2)
            norm(0)
            norm_and_rope()
            attention()
            add_gated(2, 2, False, False)
            updated()
            norm(1)
            routing()
            dve.memset(spread, 0.0).then_inc(dve_chain, 1)
            dve.wait_ge(dve_chain, w.next(dve_chain))
            dve.memset(y_sel, 0.0).then_inc(dve_chain, 1)
            dve.wait_ge(dve_chain, w.next(dve_chain))
            select(sel, 0, False, sel_ready)
            banks.n["act"] += 1
            dve.wait_ge(freed["act"], banks.n["act"])
            experts([NE], 0)
            last_add()
            over = dve.alloc_register("over_dve")
            dve.reg_load(over, flag[0:1, 0:1].bitcast(mybir.dt.int32))
            with dve.If_eq(over, 1):
                dve.memset(spread, 0.0).then_inc(cleared, 1)
                dve.wait_ge(cleared, w.next(cleared))
                experts([ROUNDS - 1, NE], NE)
                last_add()

            for k in range(KT):
                x = xs(xt[:, k, :])
                ins = stt(x, y_acc[:, k, :], mod[:, 5, k, 0:1], x, ALU.mult, ALU.add)
            ins.then_inc(fin_chain, 1)
            dve.wait_ge(fin_chain, 1)
            tt(xs(ht), xs(xt), xs(xt), ALU.mult).then_inc(fin_sq, 1)
            dve.wait_ge(fin_ms, 1)
            ts(xs(rs), psum[:, 0, :], 1e-6, None, ALU.add).then_inc(fin_eps, 1)
            dve.wait_ge(fin_std, 1)
            dve.reciprocal(xs(rs), xs(rs)).then_inc(fin_chain, 1)
            dve.wait_ge(fin_chain, 2)
            for k in range(KT):
                stt(xs(xt[:, k, :]), xs(xt[:, k, :]), V("final2", k), xs(rs), ALU.mult, ALU.mult).then_inc(fin_x, 1)
            for t in range(TQ):
                dve.wait_ge(fin_tok, t + 1)
                dve.tensor_copy(out_buf[:, t, :], psum[:, 2 * t:2 * t + 2, :].rearrange("p b c -> p (b c)")).then_inc(fin_row, 1)

        @block.scalar
        def _(act):
            w = Counts()
            banks = Results()
            fn = act.activation

            def modulation():
                for q in range(6):
                    j = banks.pair("act")
                    act.wait_ge(ready["act"], banks.n["act"])
                    fn(row[:, q % 2, :], psum[0:2, 2 * j:2 * j + 2, :].rearrange("p b c -> p (b c)"), ACT.Copy
                       ).then_inc(freed["act"], 1)
                    banks.pair("dve")

            def norm(shift, final=False):
                fn(ht[:, 0:4, :], xt[:, 0:4, :], ACT.Square).then_inc(sq_act, 1)
                banks.pair("dve")
                act.wait_ge(freed["dve"], banks.n["dve"])
                fn(rs, rs, ACT.Sqrt).then_inc(std_ready, 1)
                for k in range(0 if final else KT):
                    act.wait_ge(normed, w.next(normed))
                    for f, c in ((xs, 0), (cs, 1)):
                        ins = fn(f(ht[:, k, :]), f(ht[:, k, :]), ACT.Identity, bias=mod[:, shift, k, c:c + 1])
                    ins.then_inc(h_ready, 1)

            def gate_sigmoids(layer):
                for t in range(2):
                    for h in range(2):
                        j = banks.pair("act")
                        act.wait_ge(ready["act"], banks.n["act"])
                        px, pc = halves(j)
                        g = kk[:, 2 * t + h, :]
                        fn(grid(xs(g), layer), natural(px), ACT.Sigmoid)
                        fn(cs(g), pc, ACT.Sigmoid).then_inc(freed["act"], 1)
                    for _ in range(2):
                        banks.pair("dve")

            def raw_columns(layer):
                for n in range(16):
                    j = banks.pair("act")
                    act.wait_ge(ready["act"], banks.n["act"])
                    px, pc = halves(j)
                    rows = 64 if n in (12, 13) else 32 if n == 15 else P
                    if n >= 2:
                        act.wait_ge(raw_used, w.next(raw_used))
                    dst = tmp[0:rows, n % 2, 1:1 + W]
                    fn(grid(xs(dst), layer), natural(px[0:rows]), ACT.Copy)
                    fn(cs(dst), pc[0:rows], ACT.Copy).then_inc(freed["act"], 1)
                w.skip(raw_used, 2)
                act.wait_ge(shifted, w.next(shifted))
                fn(lo[0:64, 0, :], lo[0:64, 0, :], ACT.Tanh)
                fn(lo[:, 2, :], lo[:, 2, :], ACT.Sigmoid)
                fn(lo[0:32, 3, :], lo[0:32, 3, :], ACT.Sigmoid).then_inc(lo_tanh, 1)

            def roots():
                for t in range(4):
                    banks.pair("dve")
                    act.wait_ge(freed["dve"], banks.n["dve"])
                    fn(scr[:, t, :], scr[:, t, :], ACT.Sqrt).then_inc(gstd, 1)

            def group_norm(base):
                for t in range(4):
                    banks.pair("dve")
                    act.wait_ge(freed["dve"], banks.n["dve"])
                    fn(scr[:, t, :], ht[:, base + t, :], ACT.Square).then_inc(sq_grp, 1)
                roots()

            def key_norm():
                act.wait_ge(kk_raw, w.next(kk_raw))
                fn(scr, kk, ACT.Square).then_inc(kk_sq, 1)
                roots()
                act.wait_ge(grp_normed, w.next(grp_normed, 4))

            def recurrence(turns):
                base = dict(banks.n)
                per = {r_cum: 1, act_chain: 0}
                with w.loop(act, [turns], per) as (i, _):
                    col = {0: i * C + f0[turns], 1: i * (-C) + b0[turns]}

                    def panel(name, g):
                        bank, o, n = PLAN[name, g]
                        act.wait_ge(ready[o], i * PLAN_N[o] + (base[o] + n))
                        return psum[:, bank, :]

                    for h, name in enumerate(("decay", "rate")):
                        for g in range(2):
                            fn(R_sgaa[:, 512 * h + 256 * g:512 * h + 256 * g + 256], panel(name, g)[:, 0:256], ACT.Exp,
                               scale=-1.0).then_inc(freed["act"], 1)
                    act.wait_ge(r_cum, w.next(r_cum))
                    flat8 = lambda t: t.rearrange("p g k c -> p (g k) c")
                    fn(flat8(R_kr[:, :, :, C:]), flat8(R_li), ACT.Exp, scale=-DECAY).then_inc(r_pow, 1)
                    fn(flat8(R_kr[:, :, :, 0:C]), flat8(R_lx), ACT.Exp, scale=-DECAY).then_inc(r_pow, 1)
                    fn(R_pi, wide(2), ACT.Exp, scale=DECAY).then_inc(r_pow, 1)
                    fn(R_pc, R_tot, ACT.Exp, scale=-DECAY).then_inc(r_pow, 1)
                    for g in range(2):
                        fn(R_vc[:, g], chunk(rkv[:, 8:12, :], col[g]), ACT.Copy).then_inc(r_vcopy, 1)
                    for g in range(2):
                        fn(R_vb[:, :, g, :], panel("vb", g).rearrange("p (h k) -> p h k", h=2), ACT.Copy
                           ).then_inc(freed["act"], 1)
                    for g in range(2):
                        fn(R_ktk[:, g], pairs4(panel("kt", g)[:, 0:256]), ACT.Copy).then_inc(freed["act"], 1)
                    for m in LEVELS:
                        for g in range(2):
                            fn(R_w[:, g], pairs4(panel(f"w{m}", g)[:, 0:256]), ACT.Copy).then_inc(freed["act"], 1)
                    for g in range(2):
                        fn(R_w1[:, g], pairs4(panel("rhs", g)[:, 0:256]), ACT.Copy).then_inc(freed["act"], 1)
                    for g in range(2):
                        fn(R_u[:, g], pairs4(panel("u", g)[:, 0:256]), ACT.Copy).then_inc(freed["act"], 1)
                for o in ("dve", "act"):
                    banks.n[o] += turns * PLAN_N[o]

            def feed_forward(with_ctx):
                for t in range(FT // 2):
                    for h in range(2):
                        n = 2 * t + h
                        j = banks.pair("act")
                        act.wait_ge(ready["act"], banks.n["act"])
                        px, pc = halves(j)
                        if n >= 4:
                            act.wait_ge(freed["dve"], banks.n["dve"] + h - 3)
                        s = silu_ff[:, n % 4, :]
                        ins = fn(s[:, CTX:768], px, ACT.Silu)
                        if with_ctx:
                            ins = fn(s[:, 0:CTX], pc, ACT.Silu)
                        ins.then_inc(freed["act"], 1)
                    for _ in range(2):
                        banks.pair("dve")

            act.wait_ge(consts_in, 32)
            for b in range(2):
                fn(condv[b], V(f"cond{b}", 0, 16).rearrange("p (k c) -> p k c", k=KT), ACT.Silu).then_inc(cond_ready, 1)
            for layer in range(2):
                act.wait_ge(x_updated, w.next(x_updated))
                modulation()
                norm(0)
                act.wait_ge(zeroed, w.next(zeroed))
                gate_sigmoids(layer)
                raw_columns(layer)
                group_norm(0)
                for t in range(4):
                    act.wait_ge(grp_normed, w.next(grp_normed))
                    fn(ht[:, t, :], ht[:, t, :], ACT.Silu, bias=V(f"cn_b{layer}", t), scale=V(f"cn_g{layer}", t)).then_inc(conv_done, 1)
                key_norm()
                for turns in (CS, XS):
                    recurrence(turns)
                group_norm(4)
                for t in range(4):
                    act.wait_ge(grp_normed, w.next(grp_normed))
                    fn(ht[:, 4 + t, :], ht[:, 4 + t, :], ACT.Identity, bias=V(f"gn_b{layer}", t), scale=V(f"gn_g{layer}", t)).then_inc(y_scaled, 1)
                for _ in range(8 + 8):
                    banks.pair("dve")
                act.wait_ge(x_updated, w.next(x_updated))
                norm(3)
                feed_forward(layer == 0)
                for _ in range(8):
                    banks.pair("dve")
            else:
                act.wait_ge(x_updated, w.next(x_updated))
                norm(0, final=True)

            def projections():
                for s, cols in enumerate((256, 256, 128)):
                    for t in range(TK):
                        j = banks.pair("act")
                        act.wait_ge(ready["act"], banks.n["act"])
                        c = (128, 384, 0)[s]
                        fn(v_buf[:, t, c:c + cols], psum[:, 2 * j, 0:cols], ACT.Copy).then_inc(freed["act"], 1)
                for t in range(14):
                    j = banks.pair("act")
                    act.wait_ge(ready["act"], banks.n["act"])
                    px, pc = halves(j)
                    keys = t < 2 or t >= 10
                    dst = k_buf[:, t if t < 2 else t - 8, CTX:KEYS] if keys else q_buf[:, t - 2, :]
                    fn(dst, px, ACT.Copy)
                    if keys:
                        ins = fn(k_buf[:, t if t < 2 else t - 8, 0:CTX], pc, ACT.Copy)
                    if t < 6:
                        fn(sq_buf[:, t, CTX:KEYS], px, ACT.Square)
                        if t < 2:
                            fn(sq_buf[:, t, 0:CTX], pc, ACT.Square)
                    fn(junk, junk, ACT.Copy).then_inc(freed["act"], 1)
                    act.wait_ge(freed["act"], banks.n["act"])
                    if t < 6:
                        fn(junk, junk, ACT.Copy).then_inc(head_sq, 1)
                        act.wait_ge(head_sq, w.next(head_sq))
                for t in range(6):
                    banks.pair("dve")
                    act.wait_ge(freed["dve"], banks.n["dve"])
                    r = sq_buf[:, t, 0 if t < 2 else CTX:KEYS]
                    fn(r, r, ACT.Sqrt).then_inc(gstd, 1)
                for t in range(14):
                    banks.pair("dve")

            def attention():
                n_map = [0]

                def turn_over(n):
                    head, qt, _ = GROUPS[n]
                    j = banks.pair("act")
                    act.wait_ge(ready["act"], banks.n["act"])
                    src = psum[:, 2 * j:2 * j + 2, :].rearrange("p b c -> p (b c)")[:, 0:KEYS].rearrange("p (t q) -> p t q", q=P)
                    fn(pt_buf[:, head % 2, :, P * qt:P * qt + P], src, ACT.Copy).then_inc(freed["act"], 1)

                def weigh(head):
                    j = banks.pair("act")
                    act.wait_ge(ready["act"], banks.n["act"])
                    if head < 8:
                        r = slice(64 * (head % 2), 64 * (head % 2) + 64)
                        fn(xs(ht[r, head // 2, :]), psum[r, 2 * j, :], ACT.Copy).then_inc(freed["act"], 1)
                    else:
                        fn(xs(ht[:, 4 + head - 8, :]), psum[:, 2 * j, :], ACT.Copy)
                        fn(q_buf[:, head - 8, :], psum[:, 2 * j, :], ACT.Square).then_inc(freed["act"], 1)
                        act.wait_ge(freed["act"], banks.n["act"])
                        fn(junk, junk, ACT.Copy).then_inc(head_sq, 1)
                        act.wait_ge(head_sq, w.next(head_sq))

                for n, (head, qt, maps) in enumerate(GROUPS):
                    for _ in maps:
                        m = n_map[0]
                        n_map[0] += 1
                        j = banks.pair("act")
                        act.wait_ge(ready["act"], banks.n["act"])
                        act.wait_ge(maxed, w.next(maxed))
                        src = psum[:, 2 * j:2 * j + 2, :].rearrange("p b c -> p (b c)")[:, 0:KEYS]
                        fn(prob[:, m % 4, :], src, ACT.Exp, bias=neg_max[:, m:m + 1], scale=0.125, accum_out=row_sum[:, m:m + 1]).then_inc(freed["act"], 1)
                    if n >= 1:
                        turn_over(n - 1)
                        if GROUPS[n - 1][1] == TQ - 1:
                            weigh(GROUPS[n - 1][0])
                turn_over(len(GROUPS) - 1)
                weigh(GROUPS[-1][0])
                for t in range(4):
                    banks.pair("dve")
                    act.wait_ge(freed["dve"], banks.n["dve"])
                    fn(q_buf[:, t, :], q_buf[:, t, :], ACT.Sqrt).then_inc(gstd, 1)

            def routing():
                for t in range(TQ):
                    banks.pair("dve")
                for t in range(TQ):
                    j = banks.pair("act")
                    act.wait_ge(ready["act"], banks.n["act"])
                    fn(htok[:, t, :], psum[:, 2 * j:2 * j + 2, :].rearrange("p b c -> p (b c)"), ACT.Copy).then_inc(freed["act"], 1)
                act.wait_ge(top_ready, w.next(top_ready))
                fn(expv, expv, ACT.Exp).then_inc(top_exp, 1)
                for _ in range(TQ + 2 + KT):
                    banks.pair("dve")

            def copy_selected(own=False):
                fn(x_sel, psum[:, 4:6, :].rearrange("p b (k c) -> p (b k) c", c=P), ACT.Copy).then_inc(freed["act"], 1)

            def experts(loops):
                base = dict(banks.n)
                with w.loop(act, loops, {glu_ready: 1}) as (i, _):
                    turn = Turn(base, i)
                    act.wait_ge(glu_ready, w.next(glu_ready))
                    fn(sig, glu, ACT.Sigmoid, scale=ALPHA).then_inc(sig_ready, 1)
                    act.wait_ge(ready["act"], turn.count("gather"))
                    copy_selected()
                    act.wait_ge(ready["act"], turn.count("expert_out"))
                    fn(y_sel, psum[:, 6:8, :].rearrange("p b c -> p (b c)"), ACT.Copy).then_inc(freed["act"], 1)
                for o in ("dve", "act"):
                    banks.n[o] += int(np.prod(loops)) * EPLAN_N[o]

            act.wait_ge(x_updated, w.next(x_updated))
            act.wait_ge(lam_ready, w.next(lam_ready))
            fn(lam[:, 2:4], lam[:, 0:2], ACT.Exp).then_inc(lam_exp, 1)
            modulation()
            norm(0)
            projections()
            attention()
            for _ in range(8):
                banks.pair("dve")
            act.wait_ge(x_updated, w.next(x_updated))
            norm(3)
            routing()
            banks.n["act"] += 1
            act.wait_ge(ready["act"], banks.n["act"])
            copy_selected()
            experts([NE])
            banks.n["dve"] += KT
            act.wait_ge(rank_ready, 1)
            over = act.alloc_register("over_act")
            act.reg_load(over, flag[0:1, 0:1].bitcast(mybir.dt.int32))
            with act.If_eq(over, 1):
                experts([ROUNDS - 1, NE])
                banks.n["dve"] += KT
            act.wait_ge(fin_eps, 1)
            fn(xs(rs), xs(rs), ACT.Sqrt).then_inc(fin_std, 1)


def constants():
    c = np.zeros((P, NC), np.float32)

    def put(name, a):
        o, n = COFF[name]
        c[:, o:o + n] = a

    p = np.arange(P)
    q = p % C
    put("ident", np.eye(P))
    put("mean_dm", 1.0 / DM)
    same = (p[:, None] // C == p[None, :] // C)
    put("head_mean", same / C)
    put("head_sum", same)
    put("scan", np.arange(512) % C != 0)
    t = np.arange(C)
    tri = [q[:, None] < t, q[:, None] <= t, q[:, None] > t, q[:, None] >= t]
    put("tri", np.concatenate(tri, 1))
    lows = []
    for m in (1,) + LEVELS:
        a, b = q[:, None] // m, t[None, :] // m
        lows += [(a % 2 == 1) & (b == a - 1), (a % 2 == 0) & (b == a + 1)]
    put("level1", np.concatenate(lows[:2], 1))
    put("level", np.concatenate(lows[2:], 1))
    put("id64", q[:, None] == t)
    return c


def lay_out(inp):
    def cm(a):
        return np.ascontiguousarray(np.asarray(a, np.float32).reshape(-1, P).T)

    vecs = np.zeros((P, NV), np.float32)

    def put(name, a):
        o, n = VOFF[name]
        vecs[:, o:o + n] = a

    for l in range(2):
        put(f"ada_b{l}", cm(inp["ada_b"][l]))
        put(f"norm1{l}", cm(inp["norm1_g"][l]))
        put(f"norm2{l}", cm(inp["norm2_g"][l]))
        for n, src in (("k_k", "k_k"), ("k_a", "k_a"), ("r_k", "r_k"), ("gn_g", "gn_g"), ("gn_b", "gn_b"),
                       ("conv_b", "conv_b"), ("cn_g", "cnorm_g"), ("cn_b", "cnorm_b")):
            put(f"{n}{l}", cm(inp[src][l]))
        cw = np.asarray(inp["conv_w"][l])
        put(f"conv_w{l}", cw.reshape(TAPS, 4, P).transpose(2, 1, 0).reshape(P, -1))
        sw = np.asarray(inp["shift_w"][l])
        s = np.zeros((16, P, 3), np.float32)
        s[:12] = sw[:, :1536].reshape(3, 12, P).transpose(1, 2, 0)
        s[12, :64], s[13, :64] = sw[:, 1536:1600].T, sw[:, 1600:1664].T
        s[14], s[15, :32] = sw[:, 1664:1792].T, sw[:, 1792:1824].T
        put(f"shift_w{l}", s.transpose(1, 0, 2).reshape(P, -1))
    put("final1", cm(inp["final_g"]))
    put("ada_b2", cm(inp["b_ada_2"][0]))
    put("norm12", cm(inp["g_attn_2"][0]))
    put("norm22", cm(inp["g_ffn_2"][0]))
    put("q_norm", np.tile(np.asarray(inp["gqa_q_norm_2"][0]), 2)[:, None])
    put("k_norm", np.tile(np.asarray(inp["gqa_k_norm_2"][0]), 2)[:, None])
    put("subln", np.asarray(inp["diff_subln_2"][0])[:, None])
    put("final2", cm(inp["g_final_2"]))
    for b, (c0, c1) in enumerate((("c", "c_ctx"), ("c_2", "c_ctx_2"))):
        put(f"cond{b}", np.stack([cm(np.asarray(inp[c0]).reshape(-1)), cm(np.asarray(inp[c1]).reshape(-1))], 2).reshape(P, 16))

    def slots(wt):
        k, n = wt.shape
        kt = k // P
        out = []
        for c in range(0, n, 256):
            for k0 in range(0, kt, 8):
                s = np.zeros((P, 8, 256), np.float32)
                part = wt[k0 * P:min(k0 + 8, kt) * P, c:c + 256]
                s[:, :part.shape[0] // P, :part.shape[1]] = part.reshape(-1, P, part.shape[1]).transpose(1, 0, 2)
                out.append(s.reshape(P, SLOT))
        return out

    stream = []
    for l in range(2):
        stream += slots(np.asarray(inp["ada_w"][l]))
        wi = np.asarray(inp["w_in"][l])
        stream += slots(np.concatenate([wi[:, 512:768], wi[:, 0:256], wi[:, 768:1024], wi[:, 256:512], wi[:, 1024:]], 1))
        s = np.zeros((P, SLOT), np.float32)
        for h, (up, b0) in enumerate((("decay_up", "decay_b0"), ("iclr_up", "iclr_b0"))):
            s[0:64, 1024 * h:1024 * h + 1024] = np.asarray(inp[up][l]).transpose(1, 0, 2).reshape(64, 1024)
            s[64, 1024 * h:1024 * h + 1024] = np.asarray(inp[b0][l]).reshape(1024)
        stream.append(s)
        s = np.zeros((P, SLOT), np.float32)
        gu = np.asarray(inp["g_up"][l])
        s[:, 0:512], s[0:32, 512:1024] = gu[0:P], gu[P:160]
        stream.append(s)
        stream += slots(np.asarray(inp["w_out"][l]))
        g, u = slots(np.asarray(inp["ffn_wg"][l])), slots(np.asarray(inp["ffn_wu"][l]))
        for a, b in zip(g, u):
            stream += [a, b]
        stream += slots(np.asarray(inp["ffn_wd"][l]))
    stream += slots(np.asarray(inp["w_ada_2"][0]))
    wq = np.asarray(inp["w_qkv_2"][0])
    qa, ka, va, qb, kb, vb = (wq[:, a:b] for a, b in ((0, 512), (512, 640), (640, 768), (768, 1280), (1280, 1792), (1792, 2304)))
    stream += slots(vb) + slots(va)
    stream += slots(np.concatenate([ka[:, 0:64], ka[:, 0:64], ka[:, 64:128], ka[:, 64:128]], 1))
    stream += slots(qa) + slots(qb) + slots(kb)
    stream += slots(np.asarray(inp["w_o_2"][0]))
    s = np.zeros((P, SLOT), np.float32)
    s[:, 0:256] = np.asarray(inp["w_router_2"][0]).reshape(KT, P, NE).transpose(1, 0, 2).reshape(P, -1)
    s[0:NE, 256:1280] = np.asarray(inp["b_out_2"][0])
    stream.append(s)
    while len(stream) < MIX_SLOTS:
        stream.append(np.zeros_like(s))
    return vecs, stream


def second_constants(inp):
    c = np.zeros((P, NC2), np.float32)

    def put(name, a):
        o, n = C2OFF[name]
        c[:, o:o + n] = a

    put("lam", np.asarray(inp["diff_lambda_2"][0]).reshape(1, -1))
    put("b_router", np.asarray(inp["b_router_2"][0])[None, :])
    put("b_in", np.asarray(inp["b_in_2"][0]).reshape(NE, 16, P).transpose(2, 0, 1).reshape(P, -1))
    i = np.arange(P)
    first = (i % 32) < 16
    rot = np.zeros((P, P), np.float32)
    rot[i[first] + 16, i[first]] = -1.0
    rot[i[~first] - 16, i[~first]] = 1.0
    put("rot", rot)
    t = np.arange(SEQ)
    freq = 10000.0 ** (-np.arange(16) / 16.0)
    pos = np.where(((i % 64) < 32)[:, None], (t // GRID_W)[None, :], (t % GRID_W)[None, :])
    ang = pos * freq[i % 16][:, None]
    put("cos", np.cos(ang))
    put("sin", np.sin(ang))
    put("before", i[:, None] < i[None, :])
    put("ones", 1.0)
    put("iota", i[None, :])
    return c


def columns(x):
    x = np.asarray(x)
    return np.ascontiguousarray(x.T.reshape(KT, P, -1).transpose(1, 0, 2))



def kernel(**inputs):
    from concourse import bacc
    from concourse.bass_utils import run_bass_kernel_spmd

    inp = {k: np.asarray(v) for k, v in inputs.items()}
    vecs, stream = lay_out(inp)
    arrays = dict(vecs=vecs, consts=constants(), stream=np.stack(stream), x_cm=columns(inp["x"][0]), ctx_cm=columns(inp["ctx"][0]),
                  con2=second_constants(inp), ctx2_cm=columns(inp["ctx_2"][0]),
                  w_in=np.ascontiguousarray(inp["w_in_2"][0]), w_out=np.ascontiguousarray(inp["w_out_2"][0]))
    nc = bacc.Bacc("TRN2", target_bir_lowering=False, num_devices=1)
    ins = {n: nc.dram_tensor(n, a.shape, F32, kind="ExternalInput").ap() for n, a in arrays.items()}
    out = nc.dram_tensor("out_0_dram", (1, SEQ, DM), F32, kind="ExternalOutput").ap()
    build(nc, ins, out)
    r = run_bass_kernel_spmd(nc, [arrays], core_ids=[0])
    return r.results[0]["out_0_dram"]
```

```python
import numpy as np
from contextlib import ExitStack, contextmanager

import concourse.bass as bass
from concourse import mybir

F32 = mybir.dt.float32
U32 = mybir.dt.uint32
ALU = mybir.AluOpType
ACT = mybir.ActivationFunctionType
AX_X = mybir.AxisListType.X

P = 128
DM = 1024
KT = DM // P
SEQ, CTX = 512, 256
GRID_W, GRID_R = 64, 8
GAP = 15
XO = CTX + GAP
W = XO + SEQ
TAPS = 31
PADW = GAP + W + GAP
FT = 22
RING = 4
SLOT = 2048
C = 64
CS, XS = CTX // C, SEQ // C
DECAY = 0.606531
LEVELS = (2, 4, 8, 16, 32)
KEYS = CTX + SEQ
TK, TQ = KEYS // P, SEQ // P
NE, TOPK, CAP = 32, 4, P
ROUNDS = SEQ // CAP
EXPERT_SLOTS = 12
MIX_SLOTS = 192
ALPHA, LIMIT = 1.702, 7.0
EPS, LN_EPS, GN_EPS = 1e-6, 1e-5, 64e-5
LAMBDA_INIT = 0.8 - 0.6 * float(np.exp(0.0))

LAYER_VECS = [("ada_b", 48), ("norm1", 8), ("norm2", 8), ("k_k", 4), ("k_a", 4), ("r_k", 4), ("gn_g", 4),
              ("gn_b", 4), ("conv_b", 4), ("cn_g", 4), ("cn_b", 4), ("conv_w", 4 * TAPS), ("shift_w", 48)]
VECS = [(f"{n}{l}", c) for l in range(2) for n, c in LAYER_VECS] + [
    ("final1", 8), ("ada_b2", 48), ("norm12", 8), ("norm22", 8), ("q_norm", 1), ("k_norm", 1), ("subln", 1),
    ("final2", 8), ("cond0", 16), ("cond1", 16)]
VOFF = {}
for _n, _c in VECS:
    VOFF[_n] = (sum(c for _, c in VOFF.values()), _c)
CON2 = [("lam", 256), ("b_router", 32), ("b_in", 512), ("rot", 128), ("cos", 512), ("sin", 512), ("before", 128),
        ("ones", 128), ("iota", 128)]
C2OFF = {}
for _n, _c in CON2:
    C2OFF[_n] = (sum(c for _, c in C2OFF.values()), _c)
NC2 = sum(c for _, c in CON2)
NV = sum(c for _, c in VECS)
CONSTS = [("ident", 128), ("mean_dm", 128), ("head_mean", 128), ("head_sum", 128), ("scan", 512),
          ("tri", 4 * C), ("level", 2 * len(LEVELS) * C), ("level1", 2 * C), ("id64", C)]
COFF = {}
for _n, _c in CONSTS:
    COFF[_n] = (sum(c for _, c in COFF.values()), _c)
NC = sum(c for _, c in CONSTS)


class Counts:

    def __init__(self):
        self.seen, self.turn, self.per = {}, None, {}

    def value(self, sem, n):
        return n if self.turn is None else self.turn * self.per[sem] + n

    def next(self, sem, more=1):
        self.seen[sem] = self.seen.get(sem, 0) + more
        return self.value(sem, self.seen[sem])

    def skip(self, sem, more=1):
        self.seen[sem] = self.seen.get(sem, 0) + more

    @contextmanager
    def loop(self, eng, loops, per):
        start = dict(self.seen)
        self.per = per
        if len(loops) == 1:
            with eng.Fori(0, loops[0]) as e:
                self.turn = e
                yield e, e
                self.turn = None
        else:
            with eng.Fori(0, loops[0]) as r:
                with eng.Fori(0, loops[1]) as e:
                    self.turn = r * loops[1] + e
                    yield self.turn, e
                    self.turn = None
        turns = int(np.prod(loops))
        for sem in set(self.seen) | set(per):
            n = self.seen.get(sem, 0) - start.get(sem, 0)
            assert n == per.get(sem, 0), (sem, n, per.get(sem, 0))
            self.seen[sem] = start.get(sem, 0) + n * turns


class Results:

    def __init__(self):
        self.n = {"dve": 0, "act": 0}
        self.tile, self.last = 0, {}

    def pair(self, owner):
        self.n[owner] += 1
        self.tile += 1
        return (self.tile - 1) % 4

    def place(self, owner):
        j = self.pair(owner)
        stands = self.last.get(j, (None, 0))
        self.last[j] = (owner, self.n[owner])
        return (j,) + stands


def recurrence_plan(main=True, ahead=True, emit=True):
    names = []
    if main:
        names += [("q1", "dve"), ("q2", "dve"), ("q3", "dve"), ("vb", "act"), ("kt", "act")]
        for m in LEVELS:
            names.append((f"w{m}", "act"))
            if m != LEVELS[-1]:
                names.append((f"x{m}", "dve"))
            names.append((f"z{m}", "dve"))
    if ahead:
        names += [("decay", "act"), ("rate", "act")]
    if main:
        names += [("rhs", "act"), ("u", "act")] + ([("y", "dve")] if emit else []) + [("s", "dve")]
    plan, n = {}, {"dve": 0, "act": 0}
    for i, (name, owner) in enumerate(names):
        for g in range(2):
            n[owner] += 1
            plan[name, g] = (4 * g + i % 4, owner, n[owner])
    return plan, n


class Chunk:

    def __init__(self, base, i=None, **kinds):
        self.plan, self.total = recurrence_plan(**kinds)
        self.base, self.i = base, i

    def bank(self, name, g):
        return self.plan[name, g][0]

    def owner(self, name, g):
        return self.plan[name, g][1]

    def number(self, owner, n):
        m = self.base[owner] + n
        return m if self.i is None else self.i * self.total[owner] + m

    def count(self, name, g):
        _, o, n = self.plan[name, g]
        return self.number(o, n)


def recurrence_turns(w, eng, banks, per, emit_ctx):
    base = banks.n
    for turns, first, last in ((CS, (0, CTX - C), (XO, XO + SEQ - C)), (XS, (XO, XO + SEQ - C), None)):
        emit = emit_ctx or turns == XS
        with w.loop(eng, [turns - 1], per) as (i, _):
            t = Chunk(dict(base), i, emit=emit)
            yield t, (i * C + first[0], i * (-C) + first[1]), (i * C + (first[0] + C), i * (-C) + (first[1] - C)), emit
        for o in base:
            base[o] += (turns - 1) * t.total[o]
        t = Chunk(dict(base), ahead=last is not None, emit=emit)
        yield t, (first[0] + (turns - 1) * C, first[1] - (turns - 1) * C), last, emit
        for o in base:
            base[o] += t.total[o]


def expert_plan():
    names = [("hidden", (0, 1, 2, 3), "dve"), ("gather", (4, 5), "act")] + [(f"add{k}", (k % 4,), "dve") for k in range(KT)] + [
        ("spread", (4,), "dve"), ("expert_out", (6, 7), "act")]
    plan, n = {}, {"dve": 0, "act": 0}
    for name, b, owner in names:
        n[owner] += 1
        plan[name] = (b, owner, n[owner])
    return plan, n


EPLAN, EPLAN_N = expert_plan()


class Turn:

    def __init__(self, base, i):
        self.base, self.i = base, i
        self.users = {b: (name, True) for name, (banks, _, _) in EPLAN.items() for b in banks}

    def count(self, name, before=False):
        _, o, n = EPLAN[name]
        return self.i * EPLAN_N[o] + (self.base[o] + n - (EPLAN_N[o] if before else 0))

    def stands(self, name):
        need = {}
        for b in EPLAN[name][0]:
            user, before = self.users[b]
            o, n = EPLAN[user][1:]
            need[o] = max(need.get(o, (-99,)), (n - EPLAN_N[o] * before, user, before))
            self.users[b] = (name, False)
        return [(o, self.count(user, before)) for o, (_, user, before) in need.items()]


def build(nc, ins, out):
    ctx = ExitStack()
    with ctx:
        def sb(name, cols, parts=P):
            return ctx.enter_context(nc.sbuf_tensor(name, [parts, cols], F32))[:, :]

        def sem(name):
            return ctx.enter_context(nc.semaphore(name))

        xt = sb("xt", KT * W).rearrange("p (k w) -> p k w", k=KT)
        ht = sb("ht", KT * W).rearrange("p (k w) -> p k w", k=KT)
        ring = sb("ring", RING * SLOT).rearrange("p (s c) -> p s c", s=RING)
        vec = sb("vec", NV)
        con = sb("con", NC)
        mod = [sb(f"mod{b}", 96).rearrange("p (q k c) -> p q k c", q=6, k=KT) for b in range(2)]
        gain = [sb(f"gain{b}", 32).rearrange("p (h k c) -> p h k c", h=2, k=KT) for b in range(2)]
        rs = sb("rs", W)
        mark, junk = sb("mark", 1), sb("junk", 1)
        ahead = sb("ahead", 4 * 512)
        work = sb("work", 12 * W + 4 * W + 4 * W + 4 * PADW + 4 * W + 4450)
        rkv = work[:, 0:12 * W].rearrange("p (k w) -> p k w", k=12)
        lo = work[:, 12 * W:16 * W].rearrange("p (k w) -> p k w", k=4)
        kk = work[:, 16 * W:20 * W].rearrange("p (k w) -> p k w", k=4)
        zoff = 20 * W
        zp = work[:, zoff:zoff + 4 * PADW].rearrange("p (k w) -> p k w", k=4)
        scr = work[:, zoff + 4 * PADW:zoff + 4 * PADW + 4 * W].rearrange("p (k w) -> p k w", k=4)
        toff = zoff + 4 * PADW + 4 * W
        tmp = work[:, toff:toff + 2 * (W + 2)].rearrange("p (k w) -> p k w", k=2)
        row = work[0:2, toff + 1600:toff + 1600 + 2048].rearrange("p (b c) -> p b c", b=2)
        act_ff = work[:, 0:FT * (SEQ + CTX)].rearrange("p (k w) -> p k w", k=FT)
        silu_ff = work[:, FT * 768:FT * 768 + 4 * 768].rearrange("p (k w) -> p k w", k=4)
        rec = work[:, zoff:zoff + 21 * 512 + 64]

        def wide(i, n=1):
            return rec[:, 512 * i:512 * (i + n)]

        at = [0]

        def carve(n):
            at[0] += n
            assert at[0] <= work.shape[1], at[0]
            return work[:, at[0] - n:at[0]]

        con2 = carve(NC2)
        q_buf = carve(8 * SEQ).rearrange("p (k c) -> p k c", k=8)
        k_buf = carve(6 * KEYS).rearrange("p (k c) -> p k c", k=6)
        v_buf = carve(TK * 640).rearrange("p (t c) -> p t c", t=TK)
        pt_buf = carve(2 * TK * SEQ).rearrange("p (b t q) -> p b t q", b=2, t=TK)
        sq_buf = work[:, at[0] - 2 * TK * SEQ:at[0] - 2 * TK * SEQ + 6 * KEYS].rearrange("p (k c) -> p k c", k=6)
        prob = carve(4 * KEYS).rearrange("p (b c) -> p b c", b=4)
        neg_max, row_sum, row_inv = carve(64), carve(64), carve(64)
        lam = sb("lam", 8)
        rope_tmp = carve(SEQ)
        at[0] = NC2
        htok = carve(TQ * DM).rearrange("p (t c) -> p t c", t=TQ)
        y_acc = carve(KT * SEQ).rearrange("p (k c) -> p k c", k=KT)
        x_sel = carve(DM).rearrange("p (k c) -> p k c", k=KT)
        glu, lin, sig = carve(DM), carve(DM), carve(DM)
        y_sel = carve(DM)
        sel = carve(SEQ).rearrange("p (t c) -> p t c", t=TQ)
        sel_gate = carve(SEQ).rearrange("p (t c) -> p t c", t=TQ)
        spread = carve(SEQ)
        gate_t = carve(SEQ)
        EC = ROUNDS * NE + 1
        rank = carve(TQ * EC).rearrange("p (t c) -> p t c", t=TQ)
        gates = carve(TQ * EC).rearrange("p (t c) -> p t c", t=TQ)
        picked = carve(TQ * NE).rearrange("p (t c) -> p t c", t=TQ)
        logit = carve(TQ * NE).rearrange("p (t c) -> p t c", t=TQ)
        top8 = carve(TQ * 8).rearrange("p (t c) -> p t c", t=TQ)
        idx8 = carve(TQ * 8).rearrange("p (t c) -> p t c", t=TQ)
        idxf = carve(TQ * 8).rearrange("p (t c) -> p t c", t=TQ)
        expv = carve(TQ * 4).rearrange("p (t c) -> p t c", t=TQ)
        esum, einv, hot = carve(TQ), carve(TQ), carve(NE)
        flag = carve(4)
        out_buf = htok

        psum = ctx.enter_context(nc.psum_tensor("psum", [P, 8 * 512], F32))[:, :].rearrange("p (b c) -> p b c", b=8)

        def V(name, i=0, n=None):
            o, c = VOFF[name]
            return vec[:, o + i:o + i + (n or 1)]

        def Cn(name, rows=P):
            o, c = COFF[name]
            return con[0:rows, o:o + c]

        def C2(name):
            o, c = C2OFF[name]
            return con2[:, o:o + c]

        ident = Cn("ident")
        id64 = Cn("id64")

        consts_in = sem("consts_in")
        x_in = sem("x_in")
        zeroed = sem("zeroed")
        slot_loaded = [sem(f"slot_loaded{i}") for i in range(RING)]
        slot_used = sem("slot_used")
        ready = {o: sem(f"product_ready_{o}") for o in ("dve", "act")}
        freed = {o: sem(f"product_read_{o}") for o in ("dve", "act")}
        dve_chain = sem("dve_chain")
        cond_ready = sem("cond_ready")
        modulated = sem("modulated")
        x_updated = sem("x_updated")
        sq_act = sem("squares_act")
        sq_dve = sem("squares_dve")
        std_ready = sem("std_ready")
        normed = sem("normed")
        h_ready = sem("h_ready")
        raw_used = sem("raw_used")
        shifted = sem("shifted")
        conv_out = sem("conv_out")
        sq_grp = sem("sq_grp")
        gstd = sem("gstd")
        grp_normed = sem("grp_normed")
        conv_done = sem("conv_done")
        kk_raw = sem("kk_raw")
        kk_sq = sem("kk_sq")
        lo_tanh = sem("lo_tanh")
        r_cum = sem("r_cum")
        r_pow = sem("r_pow")
        r_fac = sem("r_fac")
        r_vcopy = sem("r_vcopy")
        r_inv = sem("r_inv")
        state = sem("state")
        y_scaled = sem("y_scaled")
        bonus_in = sem("bonus_in")
        stored = sem("stored")
        con2_in = sem("con2_in")
        ctx2_in = sem("ctx2_in")
        lam_exp = sem("lam_exp")
        lam_ready = sem("lam_ready")
        attention_free = sem("attention_free")
        qk_normed = sem("qk_normed")
        roped = sem("roped")
        maxed = sem("maxed")
        prob_ready = sem("prob_ready")
        head_sq = sem("head_sq")
        attended = sem("attended")
        top_ready = sem("top_ready")
        top_exp = sem("top_exp")
        gates_ready = sem("gates_ready")
        rank_ready = sem("rank_ready")
        sel_ready = sem("sel_ready")
        gate_ready = sem("gate_ready")
        glu_ready = sem("glu_ready")
        sig_ready = sem("sig_ready")
        act_ready = sem("act_ready")
        cleared = sem("cleared")
        logs = sem("logs")
        fin_chain = sem("fin_chain")
        fin_sq = sem("fin_sq")
        fin_ms = sem("fin_ms")
        fin_log = sem("fin_log")
        fin_std = sem("fin_std")
        fin_x = sem("fin_x")
        fin_tok = sem("fin_tok")
        fin_row = sem("fin_row")
        passed_pe = sem("passed_pe")
        passed_dve = sem("passed_dve")

        def xs(t):
            return t[..., XO:XO + SEQ]

        def cs(t):
            return t[..., 0:CTX]

        def parts(with_ctx):
            return ((xs, 0), (cs, 1)) if with_ctx else ((xs, 0),)

        def grid(t, layer):
            return t.rearrange("p (c r) -> p r c", r=GRID_R) if layer == 1 else t.rearrange("p (r c) -> p r c", c=GRID_W)

        def natural(t):
            return t.rearrange("p (r c) -> p r c", c=GRID_W)

        def halves(j):
            return psum[:, 2 * j, :], psum[:, 2 * j + 1, 0:CTX]

        def pairs4(t):
            return t.rearrange("p (k c) -> p k c", k=4)

        GROUPS, GROUP_PROB, n_map = [], [], 0
        for head in range(12):
            for qt in range(TQ):
                if head < 8:
                    r = slice(64 * (head % 2), 64 * (head % 2) + 64)
                    maps = [("shared", head // 2, head // 4, r)]
                else:
                    maps = [("paired", 4 + head - 8, 2 + head - 8, slice(64 * c, 64 * c + 64)) for c in range(2)]
                GROUPS.append((head, qt, maps))
                GROUP_PROB.append(n_map % 4)
                n_map += len(maps)

        def heads(t):
            return t.rearrange("p (g k c) -> p g k c", g=2, k=4)

        condv = [sb(f"cond_silu{b}", 16).rearrange("p (k c) -> p k c", k=KT) for b in range(2)]
        R_sgaa = wide(0, 2)
        R_sg, R_aa = heads(wide(0)), heads(wide(1))
        R_li, R_lx = heads(wide(2)), heads(wide(3))
        R_kr = wide(4, 2).rearrange("p (g k c) -> p g k c", g=2, k=4)
        R_pi, R_bh, R_kh = wide(6), heads(wide(7)), heads(wide(1))
        R_bb, R_kb, R_vc = heads(wide(8)), heads(wide(9)), heads(wide(10))
        R_m1 = wide(11, 2).rearrange("p (g k h c) -> p g k h c", g=2, k=4, h=2)
        R_m2 = wide(13, 2).rearrange("p (g k h c) -> p g k h c", g=2, k=4, h=2)
        R_x, R_z, R_w, R_w1, R_u = heads(wide(15)), heads(wide(16)), heads(wide(0)), heads(ahead[:, 0:512]), heads(ahead[:, 512:1024])
        R_pow = ahead[:, 1024:2048].rearrange("p (g k c) -> p g k c", g=2, k=4)
        R_vt, R_bt, R_ktk, R_s = heads(wide(17)), heads(wide(18)), heads(wide(19)), heads(wide(20))
        R_vb = wide(17, 2).rearrange("p (h g k) -> p h g k", h=2, g=2)
        R_tot, R_pc = rec[:, 21 * 512:21 * 512 + 8], rec[:, 21 * 512 + 8:21 * 512 + 16]

        def chunk(t, col):
            return t[:, :, bass.ds(col, C)]
        block = ctx.enter_context(nc.Block())

        @block.sync
        def _(sp):
            sp.dma_start(vec, ins["vecs"]).then_inc(consts_in, 16)
            sp.dma_start(con, ins["consts"]).then_inc(consts_in, 16)
            stream = ins["stream"]
            n_slots = stream.shape[0]
            for s in range(RING):
                sp.dma_start(ring[:, s, :], stream[s]).then_inc(slot_loaded[s], 16)
                if s == 0:
                    for k in range(KT):
                        sp.dma_start(xs(xt[:, k, :]), ins["x_cm"][:, k, :]).then_inc(x_in, 16)
                        sp.dma_start(cs(xt[:, k, :]), ins["ctx_cm"][:, k, :]).then_inc(x_in, 16)
            with sp.Fori(1, n_slots // RING) as turn:
                for s in range(RING):
                    sp.wait_ge(slot_used, turn * RING + (s + 1 - RING))
                    sp.dma_start(ring[:, s, :], stream[bass.ds(turn * RING + s, 1)].rearrange("o p c -> (o p) c")
                                 ).then_inc(slot_loaded[s], 16)

            def expert_weights(e, turn, late):
                for j in range(EXPERT_SLOTS):
                    sp.wait_ge(slot_used, turn * EXPERT_SLOTS + (MIX_SLOTS + j + 1 - RING + late))
                    if j < KT:
                        src = ins["w_in"][bass.ds(e, 1), P * j:P * j + P, :].rearrange("o p c -> (o p) c")
                        dst = ring[:, j % RING, :]
                    else:
                        f = 2 * P * (j - KT)
                        src = ins["w_out"][bass.ds(e, 1), f:f + 2 * P, :].rearrange("o (f p) c -> (o p) f c", p=P)
                        dst = ring[:, j % RING, :].rearrange("p (f c) -> p f c", f=2)
                    sp.dma_start(dst, src).then_inc(slot_loaded[j % RING], 16)

            with sp.Fori(0, NE) as e:
                expert_weights(e, e, 0)
            sp.wait_ge(rank_ready, 1)
            over = sp.alloc_register("over_sp")
            sp.reg_load(over, flag[0:1, 0:1].bitcast(mybir.dt.int32))
            with sp.If_eq(over, 1):
                with sp.Fori(1, ROUNDS) as r:
                    with sp.Fori(0, NE) as e:
                        expert_weights(e, r * NE + e, 1)
            for t in range(TQ):
                sp.wait_ge(fin_row, t + 1)
                sp.dma_start(out[0, P * t:P * t + P, :], out_buf[:, t, :]).then_inc(stored, 16)
            sp.wait_ge(stored, 16 * TQ)

        @block.gpsimd
        def _(pool):
            pool.wait_ge(attention_free, 1)
            pool.dma_start(con2, ins["con2"]).then_inc(con2_in, 16)
            pool.dma_start(cs(xt), ins["ctx2_cm"]).then_inc(ctx2_in, 16)

        @block.tensor
        def _(pe):
            w = Counts()
            banks = Results()
            slot = [0]
            used_up = [0]

            def matmul(*args, **kwargs):
                mm = pe.matmul(*args, **kwargs)
                if used_up[0]:
                    mm.then_inc(slot_used, used_up[0])
                    used_up[0] = 0
                return mm

            def take_slot():
                n = slot[0]
                slot[0] += 1
                pe.wait_ge(slot_loaded[n % RING], 16 * (n // RING + 1))
                return ring[:, n % RING, :]

            def product(owner, terms, with_ctx=True, rows=P, used=0, with_x=True):
                j, stands, n_stands = banks.place(owner)
                if stands:
                    pe.wait_ge(freed[stands], n_stands)
                px, pc = halves(j)
                n = len(terms)
                for i, (lhs, rhs) in enumerate(terms):
                    if with_x:
                        mm = matmul(px[0:rows], lhs, xs(rhs), start=(i == 0), stop=(i == n - 1))
                if with_ctx:
                    for i, (lhs, rhs) in enumerate(terms):
                        mm = matmul(pc[0:rows], lhs, cs(rhs), start=(i == 0), stop=(i == n - 1))
                mm.then_inc(ready[owner], 1)
                used_up[0] += used

            def modulation(block_n):
                for q in range(7):
                    if q < 6:
                        j, stands, n_stands = banks.place("act")
                        if stands:
                            pe.wait_ge(freed[stands], n_stands)
                        for s in range(4):
                            wt = take_slot().rearrange("p (k c) -> p k c", k=KT)
                            for k in range(KT):
                                mm = matmul(psum[0:2, 2 * j + s // 2, 256 * (s % 2):256 * (s % 2) + 256],
                                            condv[block_n][:, k, :], wt[:, k, :], start=(k == 0), stop=(k == KT - 1))
                            used_up[0] += 1
                        mm.then_inc(ready["act"], 1)
                    if q > 0:
                        pe.wait_ge(freed["act"], banks.n["act"] - (q < 6))
                        j, stands, n_stands = banks.place("act")
                        if stands:
                            pe.wait_ge(freed[stands], n_stands)
                        for k in range(KT):
                            mm = pe.transpose(psum[:, 2 * j, 2 * k:2 * k + 2], row[:, (q - 1) % 2, 128 * k:128 * k + 128], ident[0:2, 0:2])
                            if used_up[0]:
                                mm.then_inc(slot_used, used_up[0])
                                used_up[0] = 0
                        mm.then_inc(ready["act"], 1)

            def mean_square(with_ctx):
                pe.wait_ge(sq_act, w.next(sq_act))
                pe.wait_ge(sq_dve, w.next(sq_dve))
                product("act", [(Cn("mean_dm"), ht[:, k, :]) for k in range(KT)], with_ctx)

            def input_projection():
                pe.wait_ge(h_ready, w.next(h_ready, KT))
                for t in range(4):
                    wt = take_slot().rearrange("p (k c) -> p k c", k=KT)
                    for h in range(2):
                        product("act" if t % 2 == 0 else "dve",
                                [(wt[:, k, 128 * h:128 * h + 128], ht[:, k, :]) for k in range(KT)], used=h)
                for t in range(6):
                    wt = take_slot().rearrange("p (k c) -> p k c", k=KT)
                    for h in range(2):
                        product("act", [(wt[:, k, 128 * h:128 * h + 128], ht[:, k, :]) for k in range(KT)], used=h)
                wt = take_slot().rearrange("p (k c) -> p k c", k=KT)
                product("act", [(wt[:, k, 0:64], ht[:, k, :]) for k in range(KT)], rows=64)
                product("act", [(wt[:, k, 64:128], ht[:, k, :]) for k in range(KT)], rows=64)
                product("act", [(wt[:, k, 128:256], ht[:, k, :]) for k in range(KT)], used=1)
                wt = take_slot().rearrange("p (k c) -> p k c", k=KT)
                product("act", [(wt[:, k, 0:32], ht[:, k, :]) for k in range(KT)], rows=32, used=1)

            def group_norm(base, with_ctx):
                if base == 0:
                    pe.wait_ge(conv_out, w.next(conv_out))
                for t in range(4):
                    product("dve", [(Cn("head_mean"), ht[:, base + t, :])], with_ctx)
                for t in range(4):
                    pe.wait_ge(sq_grp, w.next(sq_grp))
                    product("act", [(Cn("head_mean"), scr[:, t, :])], with_ctx)

            def key_norm():
                pe.wait_ge(kk_sq, w.next(kk_sq))
                for t in range(4):
                    product("dve", [(Cn("head_sum"), scr[:, t, :])])

            def recurrence(lora, emit_ctx):
                up_d = lora[0:65, 0:1024].rearrange("p (g c) -> p g c", g=2)
                up_a = lora[0:65, 1024:2048].rearrange("p (g c) -> p g c", g=2)
                for o in ("dve", "act"):
                    pe.wait_ge(freed[o], banks.n[o])
                banks.last = {}
                hs = (slice(0, 64), slice(64, 128))

                def result(t, users, name, g):
                    bank = t.bank(name, g)
                    if bank in users:
                        pe.wait_ge(freed[t.owner(*users[bank])], t.count(*users[bank]))
                        pe.sem_inc(passed_pe, 1)
                    users[bank] = (name, g)
                    return psum[:, bank, :]

                def decays_and_rates(t, users, col):
                    for name, up, src in (("decay", up_d, lo[0:65, 0, :]), ("rate", up_a, lo[0:65, 1, :])):
                        for g in range(2):
                            ps = result(t, users, name, g)
                            for p in range(4):
                                mm = matmul(ps[:, 64 * p:64 * p + 64], up[:, g, 128 * p:128 * p + 128],
                                            src[:, bass.ds(col[g], C)], start=True, stop=True)
                            mm.then_inc(ready["act"], 1)

                def each(t, users, name, g, terms, cols=64):
                    ps = result(t, users, name, g)
                    for p in range(4):
                        for r in hs:
                            n = len(terms)
                            for k, (lhs, rhs) in enumerate(terms):
                                mm = matmul(ps[r, cols * p:cols * p + cols], lhs(g, p, r), rhs(g, p, r),
                                            start=(k == 0), stop=(k == n - 1))
                    mm.then_inc(ready[t.owner(name, g)], 1)

                def op(t):
                    return lambda g, p, r: t[r, g, p, :]

                def read(t, name, g):
                    pe.wait_ge(freed[t.owner(name, g)], t.count(name, g))
                    pe.sem_inc(passed_pe, 1)

                first = Chunk(dict(banks.n), main=False)
                decays_and_rates(first, {}, (0, CTX - C))
                for o in banks.n:
                    banks.n[o] += first.total[o]
                for t, col, next_col, emit in recurrence_turns(w, pe, banks, {r_fac: 2, r_vcopy: 2, r_inv: 2}, emit_ctx):
                    users = {}
                    pe.wait_ge(r_fac, w.next(r_fac))
                    pe.sem_inc(passed_pe, 1)
                    for g in range(2):
                        each(t, users, "q1", g, [(op(R_bh), lambda g, p, r: R_kr[r, g, p, :])], cols=128)
                    for g in range(2):
                        each(t, users, "q2", g, [(op(R_kh), lambda g, p, r: R_kr[r, g, p, :])], cols=128)
                    for g in range(2):
                        each(t, users, "q3", g, [(lambda g, p, r: R_kr[r, g, p, 0:64], op(R_bh))])
                    pe.wait_ge(r_fac, w.next(r_fac))
                    pe.sem_inc(passed_pe, 1)
                    pe.wait_ge(r_vcopy, w.next(r_vcopy, 2))
                    pe.sem_inc(passed_pe, 1)
                    for g in range(2):
                        ps = result(t, users, "vb", g)
                        for h, src in ((0, R_vc), (1, R_bb)):
                            for p in range(4):
                                for r in hs:
                                    mm = matmul(ps[r, 256 * h + 64 * p:256 * h + 64 * p + 64], src[r, g, p, :], id64[r, :],
                                                start=True, stop=True)
                        mm.then_inc(ready["act"], 1)
                    for g in range(2):
                        each(t, users, "kt", g, [(op(R_kb), lambda g, p, r: id64[r, :])])
                    pe.wait_ge(r_inv, w.next(r_inv, 2))
                    pe.sem_inc(passed_pe, 1)
                    for n, m in enumerate(LEVELS):
                        for g in range(2):
                            if n:
                                read(t, f"x{LEVELS[n - 1]}", g)
                            each(t, users, f"w{m}", g, [(lambda g, p, r: R_m1[r, g, p, 0, :], op(R_x))])
                        for g in range(2):
                            read(t, f"w{m}", g)
                            if n:
                                read(t, f"z{LEVELS[n - 1]}", g)
                            if m != LEVELS[-1]:
                                each(t, users, f"x{m}", g, [(op(R_z), op(R_w))])
                        for g in range(2):
                            each(t, users, f"z{m}", g, [(op(R_w), op(R_z))])
                    if next_col:
                        decays_and_rates(t, users, next_col)
                    for g in range(2):
                        each(t, users, "rhs", g, [(lambda g, p, r: R_kr[r, g, p, 0:64], op(R_s)),
                                                  (lambda g, p, r: R_m2[r, g, p, 0, :], op(R_vt))])
                    for g in range(2):
                        read(t, f"z{LEVELS[-1]}", g)
                        read(t, "rhs", g)
                        each(t, users, "u", g, [(op(R_z), op(R_w1))])
                    for g in range(2):
                        read(t, "u", g)
                        if emit:
                            each(t, users, "y", g, [(op(R_s), lambda g, p, r: R_kr[r, g, p, 64:128]),
                                                    (op(R_u), lambda g, p, r: R_m1[r, g, p, 1, :]),
                                                    (op(R_vt), lambda g, p, r: R_m2[r, g, p, 1, :])])
                    for g in range(2):
                        each(t, users, "s", g, [(op(R_bt), op(R_u)), (op(R_ktk), op(R_vt))])
                for o in ("dve", "act"):
                    pe.wait_ge(freed[o], banks.n[o])
                banks.last = {}

            def mix_out(gup, with_ctx):
                g_hi, g_lo = gup[:, 0:512], gup[0:32, 512:1024]
                pe.wait_ge(bonus_in, w.next(bonus_in))
                for t in range(4):
                    product("dve", [(Cn("head_sum"), scr[:, t, :])], with_ctx)
                for t in range(4):
                    j, stands, n_stands = banks.place("dve")
                    if stands:
                        pe.wait_ge(freed[stands], n_stands)
                    for f, b in parts(with_ctx):
                        dst = halves(j)[b]
                        matmul(dst, g_hi[:, 128 * t:128 * t + 128], f(lo[:, 2, :]), start=True, stop=False)
                        mm = matmul(dst, g_lo[:, 128 * t:128 * t + 128], f(lo[0:32, 3, :]), start=False, stop=True)
                    mm.then_inc(ready["dve"], 1)
                used_up[0] += 2

            def output_projection(with_ctx):
                pe.wait_ge(freed["dve"], banks.n["dve"])
                pe.wait_ge(conv_done, w.next(conv_done, 4))
                for t in range(4):
                    wt = take_slot().rearrange("p (k c) -> p k c", k=KT)
                    for h in range(2):
                        product("dve", [(wt[:, k, 128 * h:128 * h + 128], ht[:, k, :]) for k in range(KT)], with_ctx, used=h)

            def output_projection_2():
                pe.wait_ge(attended, w.next(attended))
                pe.wait_ge(freed["act"], banks.n["act"])
                for t in range(4):
                    wt = take_slot().rearrange("p (k c) -> p k c", k=KT)
                    for h in range(2):
                        product("dve", [(wt[:, k, 128 * h:128 * h + 128], ht[:, k, :]) for k in range(KT)], False, used=h)

            def feed_forward(with_ctx):
                pe.wait_ge(h_ready, w.next(h_ready, KT))
                for t in range(FT // 2):
                    for owner in ("act", "dve"):
                        wt = take_slot().rearrange("p (k c) -> p k c", k=KT)
                        for h in range(2):
                            product(owner, [(wt[:, k, 128 * h:128 * h + 128], ht[:, k, :]) for k in range(KT)], with_ctx, used=h)
                pe.wait_ge(freed["dve"], banks.n["dve"])
                for t in range(4):
                    parts = [take_slot().rearrange("p (k c) -> p k c", k=KT) for _ in range(3)]
                    for h in range(2):
                        j, stands, n_stands = banks.place("dve")
                        if stands:
                            pe.wait_ge(freed[stands], n_stands)
                        px, pc = halves(j)
                        dsts = ((px, CTX, 768), (pc, 0, CTX))[:2 if with_ctx else 1]
                        for dst, a, b in dsts:
                            for k in range(FT):
                                mm = matmul(dst, parts[k // 8][:, k % 8, 128 * h:128 * h + 128], act_ff[:, k, a:b],
                                               start=(k == 0), stop=(k == FT - 1))
                                if h and dst is dsts[-1][0] and k in (7, 15):
                                    mm.then_inc(slot_used, 1)
                        mm.then_inc(ready["dve"], 1)
                        used_up[0] += h

            pe.wait_ge(consts_in, 32)
            pe.wait_ge(cond_ready, w.next(cond_ready, 2))
            for layer in range(2):
                if layer == 0:
                    modulation(0)
                mean_square(True)
                input_projection()
                modulation((layer + 1) // 2)
                group_norm(0, layer == 0)
                key_norm()
                lora, gup = take_slot(), take_slot()
                pe.wait_ge(lo_tanh, w.next(lo_tanh))
                pe.wait_ge(state, w.next(state))
                recurrence(lora, layer == 0)
                group_norm(4, layer == 0)
                mix_out(gup, layer == 0)
                output_projection(layer == 0)
                mean_square(layer == 0)
                feed_forward(layer == 0)
            else:
                mean_square(False)

            def qkv():
                pe.wait_ge(h_ready, w.next(h_ready, KT))
                for cols, used in ((256, 1), (256, 1), (128, 1)):
                    wt = take_slot().rearrange("p (k c) -> p k c", k=KT)
                    for t in range(TK):
                        j, stands, n_stands = banks.place("act")
                        if stands:
                            pe.wait_ge(freed[stands], n_stands)
                        c = P * t if t < 2 else XO + P * (t - 2)
                        for k in range(KT):
                            mm = matmul(psum[:, 2 * j, 0:cols], ht[:, k, c:c + P], wt[:, k, 0:cols], start=(k == 0), stop=(k == KT - 1))
                        mm.then_inc(ready["act"], 1)
                    used_up[0] += used
                for t in range(7):
                    wt = take_slot().rearrange("p (k c) -> p k c", k=KT)
                    for h in range(2):
                        product("act", [(wt[:, k, 128 * h:128 * h + 128], ht[:, k, :]) for k in range(KT)],
                                with_ctx=t in (0, 5, 6), used=h)
                for t in range(6):
                    pe.wait_ge(head_sq, w.next(head_sq))
                    j, stands, n_stands = banks.place("act")
                    if stands:
                        pe.wait_ge(freed[stands], n_stands)
                    mm = matmul(psum[:, 2 * j, :], Cn("head_mean"), sq_buf[:, t, CTX:KEYS], start=True, stop=True)
                    if t < 2:
                        mm = matmul(psum[:, 2 * j + 1, 0:CTX], Cn("head_mean"), sq_buf[:, t, 0:CTX], start=True, stop=True)
                    mm.then_inc(ready["act"], 1)
                for t in range(14):
                    if t < 6:
                        pe.wait_ge(qk_normed, w.next(qk_normed))
                    j, stands, n_stands = banks.place("dve")
                    if stands:
                        pe.wait_ge(freed[stands], n_stands)
                    src = k_buf[:, t, CTX:KEYS] if t < 2 else q_buf[:, t - 2, :] if t < 10 else k_buf[:, t - 8, CTX:KEYS]
                    matmul(psum[:, 2 * j, :], C2("rot"), src, start=True, stop=True).then_inc(ready["dve"], 1)

            def attention():
                pe.wait_ge(roped, w.next(roped, 14))
                pending = []

                def turn_over(n):
                    pe.wait_ge(prob_ready, w.next(prob_ready))
                    j, stands, n_stands = banks.place("act")
                    if stands:
                        pe.wait_ge(freed[stands], n_stands)
                    for t in range(TK):
                        b, c = divmod(P * t, 512)
                        mm = pe.transpose(psum[:, 2 * j + b, c:c + P], prob[:, GROUP_PROB[n], P * t:P * t + P], ident)
                    mm.then_inc(ready["act"], 1)

                def weigh(head):
                    pe.wait_ge(freed["act"], banks.n["act"])
                    j, stands, n_stands = banks.place("act")
                    if stands:
                        pe.wait_ge(freed[stands], n_stands)
                    rows = slice(0, P) if head >= 8 else slice(64 * (head % 2), 64 * (head % 2) + 64)
                    c = 64 * (head // 4) if head < 8 else 128 + 128 * (head - 8)
                    for t in range(TK):
                        mm = matmul(psum[rows, 2 * j, :], v_buf[:, t, c:c + (128 if head >= 8 else 64)], pt_buf[:, head % 2, t, :],
                                    start=(t == 0), stop=(t == TK - 1))
                    mm.then_inc(ready["act"], 1)

                for n, (head, qt, maps) in enumerate(GROUPS):
                    for kind, tile, key, r in maps:
                        j, stands, n_stands = banks.place("act")
                        if stands:
                            pe.wait_ge(freed[stands], n_stands)
                        q = q_buf[r, tile, P * qt:P * qt + P]
                        matmul(psum[:, 2 * j, :], q, k_buf[r, key, 0:512], start=True, stop=True)
                        matmul(psum[:, 2 * j + 1, 0:KEYS - 512], q, k_buf[r, key, 512:KEYS], start=True, stop=True
                               ).then_inc(ready["act"], 1)
                    if n >= 1:
                        turn_over(n - 1)
                        if n >= 1 and GROUPS[n - 1][1] == TQ - 1:
                            weigh(GROUPS[n - 1][0])
                turn_over(len(GROUPS) - 1)
                weigh(GROUPS[-1][0])
                for t in range(4):
                    pe.wait_ge(head_sq, w.next(head_sq))
                    j, stands, n_stands = banks.place("act")
                    if stands:
                        pe.wait_ge(freed[stands], n_stands)
                    matmul(psum[:, 2 * j, :], Cn("mean_dm"), q_buf[:, t, :], start=True, stop=True).then_inc(ready["act"], 1)

            def routing():
                pe.wait_ge(h_ready, w.next(h_ready, KT))
                misc = take_slot()
                for t in range(TQ):
                    j, stands, n_stands = banks.place("dve")
                    if stands:
                        pe.wait_ge(freed[stands], n_stands)
                    for k in range(KT):
                        mm = matmul(psum[:, 2 * j, 0:NE], ht[:, k, XO + P * t:XO + P * t + P], misc[:, NE * k:NE * k + NE],
                                    start=(k == 0), stop=(k == KT - 1))
                    mm.then_inc(ready["dve"], 1)
                for t in range(TQ):
                    j, stands, n_stands = banks.place("act")
                    if stands:
                        pe.wait_ge(freed[stands], n_stands)
                    for k in range(KT):
                        mm = pe.transpose(psum[:, 2 * j + k // 4, P * (k % 4):P * (k % 4) + P], ht[:, k, XO + P * t:XO + P * t + P], ident)
                    mm.then_inc(ready["act"], 1)
                pe.wait_ge(gates_ready, w.next(gates_ready))
                for t in range(TQ + 1):
                    j, stands, n_stands = banks.place("dve")
                    if stands:
                        pe.wait_ge(freed[stands], n_stands)
                    terms = [(C2("ones"), picked[:, u, :]) for u in range(min(t, TQ))] + ([(C2("before"), picked[:, t, :])] if t < TQ else [])
                    for n, (lhs, rhs) in enumerate(terms):
                        mm = matmul(psum[:, 2 * j, 0:NE], lhs, rhs, start=(n == 0), stop=(n == len(terms) - 1))
                    mm.then_inc(ready["dve"], 1)
                j, stands, n_stands = banks.place("dve")
                if stands:
                    pe.wait_ge(freed[stands], n_stands)
                for t in range(TQ):
                    mm = pe.transpose(psum[0:NE, 2 * j, P * t:P * t + P], gates[:, t, 0:NE], ident)
                mm.then_inc(ready["dve"], 1)
                pe.wait_ge(freed["dve"], banks.n["dve"])
                for k in range(KT):
                    j, stands, n_stands = banks.place("dve")
                    if stands:
                        pe.wait_ge(freed[stands], n_stands)
                    mm = matmul(psum[:, 2 * j, :], misc[0:NE, 256 + P * k:256 + P * k + P], gate_t[0:NE, :], start=True, stop=True)
                    mm.then_inc(ready["dve"], 1)
                used_up[0] += 1
                for o in ("dve", "act"):
                    pe.wait_ge(freed[o], banks.n[o])
                banks.last = {}

            def gather():
                for k in range(KT):
                    for t in range(TQ):
                        mm = matmul(psum[:, 4 + k // 4, P * (k % 4):P * (k % 4) + P], htok[:, t, P * k:P * k + P], sel[:, t, :],
                                    start=(t == 0), stop=(t == TQ - 1))
                mm.then_inc(ready["act"], 1)

            def add_back(turn, k):
                pe.matmul(psum[:, k % 4, :], y_sel[:, P * k:P * k + P], spread, start=True, stop=True).then_inc(ready["dve"], 1)

            def experts(loops, slots_before):
                base = dict(banks.n)
                loads = [16 * ((slots_before + s) // RING) for s in range(RING)]
                with w.loop(pe, loops, {sel_ready: 1, gate_ready: 1, act_ready: 1}) as (i, _):
                    turn = Turn(base, i)
                    used_up[0] = 1
                    n_slot = [0]

                    def slot_of_turn():
                        n = n_slot[0]
                        n_slot[0] += 1
                        pe.wait_ge(slot_loaded[n % RING], i * (16 * EXPERT_SLOTS // RING) + (loads[n % RING] + 16 * (n // RING + 1)))
                        return ring[:, n % RING, :]

                    pe.wait_ge(freed["act"], turn.count("gather", True))
                    for o, n in turn.stands("hidden"):
                        pe.wait_ge(freed[o], n)
                    for k in range(KT):
                        wt = slot_of_turn()
                        for f in range(16):
                            mm = matmul(psum[:, f // 4, P * (f % 4):P * (f % 4) + P], wt[:, P * f:P * f + P], x_sel[:, k, :],
                                        start=(k == 0 and f % 4 == 0), stop=(k == KT - 1), skip_group_check=True)
                        if k < KT - 1:
                            used_up[0] += 1
                    mm.then_inc(ready["dve"], 1)
                    used_up[0] += 1
                    pe.wait_ge(sel_ready, w.next(sel_ready))
                    for o, n in turn.stands("gather"):
                        pe.wait_ge(freed[o], n)
                    gather()
                    pe.wait_ge(freed["dve"], turn.count("spread", True))
                    pe.wait_ge(freed["act"], turn.count("expert_out", True))
                    for k in range(KT):
                        for o, n in turn.stands(f"add{k}"):
                            pe.wait_ge(freed[o], n)
                        add_back(turn, k)
                    pe.wait_ge(gate_ready, w.next(gate_ready))
                    for o, n in turn.stands("spread"):
                        pe.wait_ge(freed[o], n)
                    for t in range(TQ):
                        mm = pe.transpose(psum[:, 4, P * t:P * t + P], sel_gate[:, t, :], ident)
                    mm.then_inc(ready["dve"], 1)
                    pe.wait_ge(act_ready, w.next(act_ready))
                    for o, n in turn.stands("expert_out"):
                        pe.wait_ge(freed[o], n)
                    for h in range(4):
                        wt = slot_of_turn().rearrange("p (f c) -> p f c", f=2)
                        for f in range(2):
                            for c in range(2):
                                mm = matmul(psum[:, 6 + c, :], sig[:, P * (2 * h + f):P * (2 * h + f) + P], wt[:, f, 512 * c:512 * c + 512],
                                            start=(h == 0 and f == 0), stop=(h == 3 and f == 1))
                        used_up[0] += 1
                    mm.then_inc(ready["act"], 1)
                    assert used_up[0] == 1
                for o in ("dve", "act"):
                    banks.n[o] += int(np.prod(loops)) * EPLAN_N[o]

            def first_gather():
                pe.wait_ge(sel_ready, w.next(sel_ready))
                gather()
                banks.n["act"] += 1
                pe.wait_ge(freed["act"], banks.n["act"])

            def last_add():
                pe.wait_ge(freed["dve"], banks.n["dve"])
                pe.wait_ge(freed["act"], banks.n["act"])
                for k in range(KT):
                    if k >= 4:
                        pe.wait_ge(freed["dve"], banks.n["dve"] - 3)
                    add_back(None, k)
                    banks.n["dve"] += 1
                for o in ("dve", "act"):
                    pe.wait_ge(freed[o], banks.n[o])
                banks.last = {}

            mean_square(True)
            qkv()
            attention()
            output_projection_2()
            mean_square(False)
            routing()
            first_gather()
            take_slot()
            used_up[0] += 1
            experts([NE], MIX_SLOTS)
            last_add()
            pe.wait_ge(rank_ready, 1)
            over = pe.alloc_register("over_pe")
            pe.reg_load(over, flag[0:1, 0:1].bitcast(mybir.dt.int32))
            with pe.If_eq(over, 1):
                pe.wait_ge(cleared, w.next(cleared))
                experts([ROUNDS - 1, NE], MIX_SLOTS + NE * EXPERT_SLOTS)
                last_add()
            pe.wait_ge(fin_sq, 1)
            for k in range(KT):
                mm = pe.matmul(psum[:, 0, :], Cn("mean_dm"), xs(ht[:, k, :]), start=(k == 0), stop=(k == KT - 1))
            mm.then_inc(fin_ms, 1)
            pe.wait_ge(fin_x, KT)
            for t in range(TQ):
                for k in range(KT):
                    mm = pe.transpose(psum[:, 2 * t + k // 4, P * (k % 4):P * (k % 4) + P], xt[:, k, XO + P * t:XO + P * t + P], ident)
                mm.then_inc(fin_tok, 1)

        @block.vector
        def _(dve):
            w = Counts()
            banks = Results()
            tt, ts, stt = dve.tensor_tensor, dve.tensor_scalar, dve.scalar_tensor_tensor


            def modulation(layer):
                m, g = mod[layer % 2], gain[layer % 2]
                for _ in range(12):
                    banks.pair("act")
                dve.wait_ge(freed["act"], banks.n["act"])
                flat = m.rearrange("p q k c -> p (q k) c")
                tt(flat, flat, V(f"ada_b{layer}", 0, 48).rearrange("p (k c) -> p k c", c=1).to_broadcast([P, 48, 2]), ALU.add
                   ).then_inc(dve_chain, 1)
                dve.wait_ge(dve_chain, w.next(dve_chain))
                for h in range(2):
                    norm_g = V(f"norm{1 + h}{layer}", 0, 8).rearrange("p (k c) -> p k c", c=1).to_broadcast([P, KT, 2])
                    ins = stt(g[:, h], m[:, 3 * h + 1], 1.0, norm_g, ALU.add, ALU.mult)
                ins.then_inc(modulated, 1)
                dve.wait_ge(modulated, w.next(modulated))

            def norm(which, layer, with_ctx, final=None):
                for f, b in parts(with_ctx):
                    ins = tt(f(ht[:, 4:8, :]), f(xt[:, 4:8, :]), f(xt[:, 4:8, :]), ALU.mult)
                ins.then_inc(sq_dve, 1)
                banks.pair("act")
                dve.wait_ge(std_ready, w.next(std_ready))
                for k in range(KT):
                    if final:
                        ins = stt(xs(xt[:, k, :]), xs(xt[:, k, :]), V(final, k), xs(rs), ALU.mult, ALU.mult)
                        continue
                    for f, b in parts(with_ctx):
                        ins = stt(f(ht[:, k, :]), f(xt[:, k, :]), gain[layer % 2][:, which, k, b:b + 1], f(rs), ALU.mult, ALU.mult)
                    ins.then_inc(normed, 1)
                if final:
                    ins.then_inc(dve_chain, 1)
                    dve.wait_ge(dve_chain, w.next(dve_chain))

            def clear_pads():
                dve.memset(zp, 0.0)
                dve.memset(tmp, 0.0).then_inc(zeroed, 1)
                dve.wait_ge(zeroed, w.next(zeroed))

            def gated_values(layer):
                for t in range(2):
                    for _ in range(2):
                        banks.pair("act")
                    for h in range(2):
                        c = 2 * t + h
                        j = banks.pair("dve")
                        dve.wait_ge(ready["dve"], banks.n["dve"])
                        px, pc = halves(j)
                        dve.wait_ge(freed["act"], banks.n["act"] - 1 + h)
                        z = zp[:, c, GAP:GAP + W]
                        tt(grid(xs(z), layer), natural(px), grid(xs(kk[:, c, :]), layer), ALU.mult)
                        tt(cs(z), pc, cs(kk[:, c, :]), ALU.mult).then_inc(freed["dve"], 1)

            def token_shift(layer):
                for n in range(16):
                    banks.pair("act")
                    dve.wait_ge(freed["act"], banks.n["act"])
                    rows = 64 if n in (12, 13) else 32 if n == 15 else P
                    dst = (rkv[:, n, :] if n < 12 else lo[:, n - 12, :])[0:rows]
                    src = tmp[0:rows, n % 2, :]
                    tap = lambda k: V(f"shift_w{layer}", 3 * n + k)[0:rows]
                    ts(dst, src[:, 1:1 + W], tap(1), None, ALU.mult).then_inc(dve_chain, 1)
                    dve.wait_ge(dve_chain, w.next(dve_chain))
                    stt(dst, src[:, 0:W], tap(0), dst, ALU.mult, ALU.add).then_inc(dve_chain, 1)
                    dve.wait_ge(dve_chain, w.next(dve_chain))
                    stt(dst, src[:, 2:2 + W], tap(2), dst, ALU.mult, ALU.add).then_inc(raw_used, 1)
                    dve.wait_ge(raw_used, w.next(raw_used))
                dve.memset(lo[64:65, 0:2, :], 1.0).then_inc(shifted, 1)

            def long_convolution(layer):
                for k in range(TAPS):
                    for c in range(4):
                        a = 0 if layer == 0 else XO
                        src, dst, wt = zp[:, c, k + a:k + W], ht[:, c, a:W], V(f"conv_w{layer}", c * TAPS + k)
                        if k:
                            dve.wait_ge(dve_chain, w.seen[dve_chain] - 3)
                            ins = stt(dst, src, wt, dst, ALU.mult, ALU.add)
                        else:
                            ins = ts(dst, src, wt, V(f"conv_b{layer}", c), ALU.mult, ALU.add)
                        if k == TAPS - 1 and c == 3:
                            ins.then_inc(conv_out, 1)
                        else:
                            ins.then_inc(dve_chain, 1)
                            w.skip(dve_chain)
                dve.wait_ge(conv_out, w.next(conv_out))

            def scale_tiles(target, with_ctx):
                for t in range(4):
                    dve.wait_ge(gstd, w.next(gstd))
                    for f, b in parts(with_ctx):
                        ins = tt(f(target[:, t, :]), f(target[:, t, :]), f(scr[:, t, :]), ALU.mult)
                    ins.then_inc(grp_normed, 1)
                dve.wait_ge(grp_normed, w.next(grp_normed, 4))

            def group_norm(base, with_ctx):
                for t in range(4):
                    j = banks.pair("dve")
                    dve.wait_ge(ready["dve"], banks.n["dve"])
                    for f, b in parts(with_ctx):
                        h = f(ht[:, base + t, :])
                        ins = tt(h, h, halves(j)[b], ALU.subtract)
                    ins.then_inc(freed["dve"], 1)
                dve.wait_ge(freed["dve"], banks.n["dve"])
                for t in range(4):
                    banks.pair("act")
                scale_tiles(ht[:, base:base + 4, :], with_ctx)

            def key_norm(layer):
                for t in range(4):
                    ins = ts(kk[:, t, :], rkv[:, 4 + t, :], V(f"k_k{layer}", t), None, ALU.mult)
                ins.then_inc(kk_raw, 1)
                dve.wait_ge(kk_raw, w.next(kk_raw))
                for t in range(4):
                    j = banks.pair("dve")
                    dve.wait_ge(ready["dve"], banks.n["dve"])
                    px, pc = halves(j)
                    ts(xs(scr[:, t, :]), px, 1e-24, None, ALU.max)
                    ts(cs(scr[:, t, :]), pc, 1e-24, None, ALU.max).then_inc(freed["dve"], 1)
                scale_tiles(kk, True)

            def recurrence(layer):
                k_a = V(f"k_a{layer}", 0, 4).rearrange("p (k c) -> p k c", c=1).to_broadcast([P, 4, C])
                tot1 = R_tot[:, 4:8].rearrange("p (k c) -> p k c", c=1).to_broadcast([P, 4, C])
                pc512 = R_pc.rearrange("p (k c) -> p k c", c=1).to_broadcast([P, 8, C])
                tri = Cn("tri").rearrange("p (g o h c) -> p g o h c", g=2, o=1, h=2)
                one = id64.rearrange("p (o c) -> p o c", o=1).to_broadcast([P, 4, C])
                low1 = Cn("level1").rearrange("p (h o c) -> p h o c", h=2, o=1)
                low = Cn("level").bitcast(U32).rearrange("p (m h o c) -> p m h o c", m=len(LEVELS), h=2, o=1)

                def flat8(t):
                    return t.rearrange("p (k c) -> p k c", k=8)

                def sums_of_decays(t, col):
                    dve.wait_ge(freed["act"], t.count("rate", 1))
                    ts(R_sgaa, R_sgaa, 0.5, 0.5, ALU.mult, ALU.add).then_inc(dve_chain, 1)
                    dve.wait_ge(dve_chain, w.next(dve_chain))
                    dve.tensor_tensor_scan(wide(2), Cn("scan"), wide(0), 0.0, ALU.mult, ALU.add).then_inc(dve_chain, 1)
                    dve.wait_ge(dve_chain, w.next(dve_chain))
                    dve.tensor_copy(R_tot.rearrange("p (g k) -> p g k", g=2), R_li[:, :, :, C - 1]).then_inc(dve_chain, 1)
                    dve.wait_ge(dve_chain, w.next(dve_chain))
                    tt(R_lx[:, 1], tot1, R_li[:, 1], ALU.subtract).then_inc(dve_chain, 1)
                    tt(R_lx[:, 0], R_li[:, 0], R_sg[:, 0], ALU.subtract)
                    dve.wait_ge(dve_chain, w.next(dve_chain))
                    tt(R_li[:, 1], R_lx[:, 1], R_sg[:, 1], ALU.add).then_inc(r_cum, 1)
                    for g in range(2):
                        tt(R_bh[:, g], chunk(kk, col[g]), R_aa[:, g], ALU.mult).then_inc(dve_chain, 1)
                    dve.wait_ge(dve_chain, w.next(dve_chain, 2))
                    for g in range(2):
                        stt(R_aa[:, g], R_aa[:, g], -1.0, k_a, ALU.add, ALU.mult).then_inc(dve_chain, 1)
                    dve.wait_ge(dve_chain, w.next(dve_chain, 2))
                    for g in range(2):
                        stt(R_aa[:, g], R_aa[:, g], 1.0, chunk(rkv[:, 4:8, :], col[g]), ALU.add, ALU.mult).then_inc(dve_chain, 1)
                    dve.wait_ge(dve_chain, w.next(dve_chain, 2))

                def state_read(t, name, g):
                    dve.wait_ge(ready["dve"], t.count(name, g))
                    return psum[:, t.bank(name, g), 0:256].rearrange("p (k c) -> p k c", k=4)

                first = Chunk(dict(banks.n), main=False)
                sums_of_decays(first, (0, CTX - C))
                for o in banks.n:
                    banks.n[o] += first.total[o]
                per = {dve_chain: 13, r_pow: 4, r_fac: 2, r_inv: 2}
                for t, col, next_col, emit in recurrence_turns(w, dve, banks, per, layer == 0):
                    dve.wait_ge(r_pow, w.next(r_pow, 3))
                    for g in range(2):
                        stt(R_kr[:, g, :, 0:C], chunk(kk, col[g]), -1.0, R_pow[:, g, :, 0:C], ALU.mult, ALU.mult)
                        tt(R_kr[:, g, :, C:], R_pow[:, g, :, C:], chunk(rkv[:, 0:4, :], col[g]), ALU.mult)
                    tt(wide(7), wide(7), R_pi, ALU.mult)
                    tt(wide(1), wide(1), R_pi, ALU.mult).then_inc(r_fac, 1)
                    dve.wait_ge(r_fac, w.next(r_fac))
                    dve.wait_ge(r_pow, w.next(r_pow))
                    tt(flat8(wide(8)), flat8(wide(7)), pc512, ALU.mult)
                    tt(flat8(wide(9)), flat8(wide(1)), pc512, ALU.mult).then_inc(r_fac, 1)
                    dve.wait_ge(r_fac, w.next(r_fac))
                    for name, dst in (("q1", R_m1), ("q2", R_m2)):
                        for g in range(2):
                            dve.wait_ge(ready["dve"], t.count(name, g))
                            ps = psum[:, t.bank(name, g), :].rearrange("p (k h c) -> p k h c", k=4, h=2)
                            tt(dst[:, g], ps, tri[:, g].to_broadcast([P, 4, 2, C]), ALU.mult).then_inc(freed["dve"], 1)
                    dve.wait_ge(freed["dve"], t.count("q2", 1))
                    for g in range(2):
                        ps = state_read(t, "q3", g)
                        tt(R_x[:, g], ps, low1[:, g].to_broadcast([P, 4, C]), ALU.mult).then_inc(freed["dve"], 1)
                        tt(R_z[:, g], R_m1[:, g, :, 0, :], low1[:, 1 - g].to_broadcast([P, 4, C]), ALU.mult).then_inc(dve_chain, 1)
                    dve.wait_ge(dve_chain, w.next(dve_chain, 2))
                    for g in range(2):
                        tt(R_x[:, g], R_x[:, g], one, ALU.add)
                        tt(R_z[:, g], R_z[:, g], one, ALU.add).then_inc(r_inv, 1)
                    dve.wait_ge(r_inv, w.next(r_inv, 2))
                    for n, m in enumerate(LEVELS):
                        for name, dst, h in ((f"x{m}", R_x, 0), (f"z{m}", R_z, 1)):
                            if (name, 0) not in t.plan:
                                continue
                            for g in range(2):
                                ps = state_read(t, name, g)
                                dve.sem_inc(passed_dve, 1)
                                mask = low[:, n, (g + h) % 2].to_broadcast([P, 4, C])
                                dve.copy_predicated(dst[:, g], mask, ps).then_inc(freed["dve"], 1)
                                dve.wait_ge(freed["dve"], t.count(name, g))
                    if next_col:
                        sums_of_decays(t, next_col)
                    for g in range(2 if emit else 0):
                        ps = state_read(t, "y", g)
                        y = chunk(ht[:, 4:8, :], col[g])
                        tt(y, ps, y, ALU.add).then_inc(freed["dve"], 1)
                        dve.wait_ge(freed["dve"], t.count("y", g))
                    ps = [state_read(t, "s", 0), state_read(t, "s", 1)]
                    tt(flat8(wide(20)), flat8(wide(20)), pc512, ALU.mult).then_inc(dve_chain, 1)
                    dve.wait_ge(dve_chain, w.next(dve_chain))
                    for g in range(2):
                        tt(R_s[:, g], R_s[:, g], ps[g], ALU.add).then_inc(freed["dve"], 1)
                    dve.wait_ge(freed["dve"], t.count("s", 1))

            def mix_out(layer):
                r, k, v = rkv[:, 0:4, :], rkv[:, 4:8, :], rkv[:, 8:12, :]
                for t in range(4):
                    ins = stt(scr[:, t, :], r[:, t, :], V(f"r_k{layer}", t), k[:, t, :], ALU.mult, ALU.mult)
                ins.then_inc(bonus_in, 1)
                for t in range(4):
                    j = banks.pair("dve")
                    dve.wait_ge(ready["dve"], banks.n["dve"])
                    for f, b in parts(layer == 0):
                        ins = tt(f(scr[:, t, :]), halves(j)[b], f(v[:, t, :]), ALU.mult)
                    ins.then_inc(freed["dve"], 1)
                    dve.wait_ge(freed["dve"], banks.n["dve"])
                    dve.wait_ge(y_scaled, w.next(y_scaled))
                    for f, b in parts(layer == 0):
                        ins = tt(f(scr[:, t, :]), f(scr[:, t, :]), f(ht[:, 4 + t, :]), ALU.add)
                    ins.then_inc(dve_chain, 1)
                dve.wait_ge(dve_chain, w.next(dve_chain, 4))
                for t in range(4):
                    j = banks.pair("dve")
                    dve.wait_ge(ready["dve"], banks.n["dve"])
                    for f, b in parts(layer == 0):
                        ins = tt(f(ht[:, 4 + t, :]), halves(j)[b], f(scr[:, t, :]), ALU.mult)
                    ins.then_inc(freed["dve"], 1)

            def add_gated(gate, layer, with_ctx, permuted):
                for k in range(KT):
                    j = banks.pair("dve")
                    dve.wait_ge(ready["dve"], banks.n["dve"])
                    px, pc = halves(j)
                    x = xs(xt[:, k, :])
                    if permuted and layer == 1:
                        x = x.rearrange("p (r c) -> p c r", c=GRID_W)
                        px = px.rearrange("p (c r) -> p c r", r=GRID_R)
                    ins = stt(x, px, mod[layer % 2][:, gate, k, 0:1], x, ALU.mult, ALU.add)
                    if with_ctx:
                        c = cs(xt[:, k, :])
                        ins = stt(c, pc, mod[layer % 2][:, gate, k, 1:2], c, ALU.mult, ALU.add)
                    ins.then_inc(freed["dve"], 1)
                    if k == KT - 1:
                        dve.wait_ge(freed["dve"], banks.n["dve"])

            def feed_forward(with_ctx):
                for t in range(FT // 2):
                    for _ in range(2):
                        banks.pair("act")
                    for h in range(2):
                        n = 2 * t + h
                        j = banks.pair("dve")
                        dve.wait_ge(ready["dve"], banks.n["dve"])
                        px, pc = halves(j)
                        dve.wait_ge(freed["act"], banks.n["act"] - 1 + h)
                        s = silu_ff[:, n % 4, :]
                        ins = tt(act_ff[:, n, CTX:768], px, s[:, CTX:768], ALU.mult)
                        if with_ctx:
                            ins = tt(act_ff[:, n, 0:CTX], pc, s[:, 0:CTX], ALU.mult)
                        ins.then_inc(freed["dve"], 1)

            def updated():
                dve.memset(mark, 0.0).then_inc(x_updated, 1)
                dve.wait_ge(x_updated, w.next(x_updated))

            dve.wait_ge(consts_in, 32)
            dve.memset(xt[:, :, CTX:XO], 0.0).then_inc(dve_chain, 1)
            dve.wait_ge(dve_chain, w.next(dve_chain))
            dve.memset(rs, 1.0).then_inc(dve_chain, 1)
            dve.wait_ge(dve_chain, w.next(dve_chain))
            dve.memset(junk, 0.0).then_inc(dve_chain, 1)
            dve.wait_ge(dve_chain, w.next(dve_chain))
            dve.wait_ge(x_in, 16 * 2 * KT)
            for layer in range(2):
                updated()
                if layer == 0:
                    modulation(0)
                clear_pads()
                norm(0, layer, True)
                gated_values(layer)
                token_shift(layer)
                long_convolution(layer)
                modulation(layer + 1)
                group_norm(0, layer == 0)
                key_norm(layer)
                dve.memset(ht[:, 4:8, :], 0.0)
                dve.memset(wide(20), 0.0).then_inc(state, 1)
                dve.wait_ge(state, w.next(state))
                recurrence(layer)
                group_norm(4, layer == 0)
                mix_out(layer)
                add_gated(2, layer, layer == 0, True)
                updated()
                norm(1, layer, layer == 0)
                feed_forward(layer == 0)
                add_gated(5, layer, layer == 0, False)
            updated()
            norm(0, 1, False, "final1")

            def lambdas():
                v = C2("lam").rearrange("p (a b c) -> p a b c", a=2, b=2)
                prod = rope_tmp[:, 0:2 * 64].rearrange("p (a c) -> p a c", a=2)
                tt(prod, v[:, :, 0, :], v[:, :, 1, :], ALU.mult).then_inc(dve_chain, 1)
                dve.wait_ge(dve_chain, w.next(dve_chain))
                dve.tensor_reduce(lam[:, 0:2], prod, AX_X, ALU.add).then_inc(lam_ready, 1)
                dve.wait_ge(lam_ready, w.next(lam_ready))
                dve.wait_ge(lam_exp, w.next(lam_exp))
                stt(lam[:, 4:5], lam[:, 3:4], -LAMBDA_INIT, lam[:, 2:3], ALU.add, ALU.subtract).then_inc(dve_chain, 1)
                dve.wait_ge(dve_chain, w.next(dve_chain))
                ts(lam[:, 5:6], V("subln"), 1.0 - LAMBDA_INIT, None, ALU.mult).then_inc(dve_chain, 1)
                dve.wait_ge(dve_chain, w.next(dve_chain))

            def norm_and_rope():
                for _ in range(3 * TK + 14):
                    banks.pair("act")
                for t in range(6):
                    banks.pair("act")
                for t in range(6):
                    dve.wait_ge(gstd, w.next(gstd))
                    dst, a = (k_buf[:, t, :], 0) if t < 2 else (q_buf[:, t - 2, :], CTX)
                    stt(dst, dst, V("k_norm" if t < 2 else "q_norm"), sq_buf[:, t, a:KEYS], ALU.mult, ALU.mult).then_inc(qk_normed, 1)
                dve.wait_ge(qk_normed, w.next(qk_normed, 6))
                for t in range(14):
                    j = banks.pair("dve")
                    dve.wait_ge(ready["dve"], banks.n["dve"])
                    dst = k_buf[:, t, CTX:KEYS] if t < 2 else q_buf[:, t - 2, :] if t < 10 else k_buf[:, t - 8, CTX:KEYS]
                    tt(rope_tmp, psum[:, 2 * j, :], C2("sin"), ALU.mult).then_inc(freed["dve"], 1)
                    tt(dst, dst, C2("cos"), ALU.mult).then_inc(dve_chain, 1)
                    dve.wait_ge(dve_chain, w.next(dve_chain))
                    tt(dst, dst, rope_tmp, ALU.add).then_inc(roped, 1)
                    dve.wait_ge(roped, w.next(roped))

            def attention():
                numbers, n_map = [], 0

                def finish(n):
                    nums, first = numbers[n]
                    dve.wait_ge(freed["act"], nums[-1])
                    a = prob[:, first % 4, :]
                    m = len(nums)
                    dve.reciprocal(row_inv[:, first:first + m], row_sum[:, first:first + m]).then_inc(dve_chain, 1)
                    dve.wait_ge(dve_chain, w.next(dve_chain))
                    if m == 1:
                        ts(a, a, row_inv[:, first:first + 1], None, ALU.mult).then_inc(prob_ready, 1)
                        dve.wait_ge(prob_ready, w.next(prob_ready))
                        return
                    ts(a, a, row_inv[:, first:first + 1], None, ALU.mult)
                    tt(row_inv[:, first + 1:first + 2], row_inv[:, first + 1:first + 2], lam[:, 4:5], ALU.mult).then_inc(dve_chain, 1)
                    dve.wait_ge(dve_chain, w.next(dve_chain))
                    stt(a, prob[:, (first + 1) % 4, :], row_inv[:, first + 1:first + 2], a, ALU.mult, ALU.add).then_inc(prob_ready, 1)
                    dve.wait_ge(prob_ready, w.next(prob_ready))

                for n, (head, qt, maps) in enumerate(GROUPS):
                    nums = []
                    for c in range(len(maps)):
                        j = banks.pair("act")
                        nums.append(banks.n["act"])
                        dve.wait_ge(ready["act"], banks.n["act"])
                        nm = neg_max[:, n_map + c:n_map + c + 1]
                        dve.tensor_reduce(nm, psum[:, 2 * j:2 * j + 2, :].rearrange("p b c -> p (b c)")[:, 0:KEYS], AX_X, ALU.max).then_inc(dve_chain, 1)
                        dve.wait_ge(dve_chain, w.next(dve_chain))
                        ts(nm, nm, -0.125, None, ALU.mult).then_inc(maxed, 1)
                        dve.wait_ge(maxed, w.next(maxed))
                    numbers.append((nums, n_map))
                    n_map += len(maps)
                    if n >= 1:
                        finish(n - 1)
                        banks.pair("act")
                        if GROUPS[n - 1][1] == TQ - 1:
                            banks.pair("act")
                finish(len(GROUPS) - 1)
                banks.pair("act")
                banks.pair("act")
                for t in range(4):
                    banks.pair("act")
                for t in range(4):
                    dve.wait_ge(gstd, w.next(gstd))
                    x = xs(ht[:, 4 + t, :])
                    ins = stt(x, x, lam[:, 5:6], q_buf[:, t, :], ALU.mult, ALU.mult)
                    if t == 3:
                        ins.then_inc(attended, 1)
                        dve.wait_ge(attended, w.next(attended))

            def routing():
                for t in range(TQ):
                    j = banks.pair("dve")
                    dve.wait_ge(ready["dve"], banks.n["dve"])
                    tt(logit[:, t, :], psum[:, 2 * j, 0:NE], C2("b_router"), ALU.add).then_inc(freed["dve"], 1)
                    dve.wait_ge(freed["dve"], banks.n["dve"])
                for _ in range(TQ):
                    banks.pair("act")
                iota = C2("iota")
                for t in range(TQ):
                    dve.max(top8[:, t, :], logit[:, t, :]).then_inc(dve_chain, 1)
                    dve.wait_ge(dve_chain, w.next(dve_chain))
                    dve.max_index(idx8[:, t, :].bitcast(U32), top8[:, t, :], logit[:, t, :]).then_inc(dve_chain, 1)
                    dve.wait_ge(dve_chain, w.next(dve_chain))
                    ts(expv[:, t, :], top8[:, t, 0:TOPK], top8[:, t, 0:1], None, ALU.subtract).then_inc(dve_chain, 1)
                    dve.wait_ge(dve_chain, w.next(dve_chain))
                dve.tensor_copy(idxf, idx8.bitcast(U32)).then_inc(top_ready, 1)
                dve.wait_ge(top_ready, w.next(top_ready))
                dve.memset(gates, 0.0).then_inc(dve_chain, 1)
                dve.wait_ge(dve_chain, w.next(dve_chain))
                dve.memset(picked, 0.0).then_inc(dve_chain, 1)
                dve.wait_ge(dve_chain, w.next(dve_chain))
                dve.wait_ge(top_exp, w.next(top_exp))
                dve.tensor_reduce(esum, expv, AX_X, ALU.add).then_inc(dve_chain, 1)
                dve.wait_ge(dve_chain, w.next(dve_chain))
                dve.reciprocal(einv, esum).then_inc(dve_chain, 1)
                dve.wait_ge(dve_chain, w.next(dve_chain))
                for t in range(TQ):
                    g = gates[:, t, 0:NE]
                    for j in range(TOPK):
                        ts(hot, iota[:, 0:NE], idxf[:, t, j:j + 1], None, ALU.is_equal).then_inc(dve_chain, 1)
                        dve.wait_ge(dve_chain, w.next(dve_chain))
                        tt(picked[:, t, :], picked[:, t, :], hot, ALU.add).then_inc(dve_chain, 1)
                        dve.wait_ge(dve_chain, w.next(dve_chain))
                        stt(g, hot, expv[:, t, j:j + 1], g, ALU.mult, ALU.add).then_inc(dve_chain, 1)
                        dve.wait_ge(dve_chain, w.next(dve_chain))
                    ts(g, g, einv[:, t:t + 1], None, ALU.mult).then_inc(dve_chain, 1)
                    dve.wait_ge(dve_chain, w.next(dve_chain))
                dve.memset(mark, 0.0).then_inc(gates_ready, 1)
                dve.wait_ge(gates_ready, w.next(gates_ready))
                dve.memset(rank, -1.0).then_inc(dve_chain, 1)
                dve.wait_ge(dve_chain, w.next(dve_chain))
                for t in range(TQ):
                    j = banks.pair("dve")
                    dve.wait_ge(ready["dve"], banks.n["dve"])
                    stt(rank[:, t, 0:NE], psum[:, 2 * j, 0:NE], 1.0, picked[:, t, :], ALU.add, ALU.mult).then_inc(freed["dve"], 1)
                    dve.wait_ge(freed["dve"], banks.n["dve"])
                ts(rank[:, :, 0:NE], rank[:, :, 0:NE], 1.0, None, ALU.subtract).then_inc(dve_chain, 1)
                dve.wait_ge(dve_chain, w.next(dve_chain))
                for r in range(1, ROUNDS):
                    ts(rank[:, :, NE * r:NE * r + NE], rank[:, :, 0:NE], float(CAP * r), None, ALU.subtract)
                    dve.tensor_copy(gates[:, :, NE * r:NE * r + NE], gates[:, :, 0:NE]).then_inc(dve_chain, 1)
                    dve.wait_ge(dve_chain, w.next(dve_chain))
                j = banks.pair("dve")
                dve.wait_ge(ready["dve"], banks.n["dve"])
                dve.tensor_reduce(esum[:, 0:1], psum[:, 2 * j, 0:NE], AX_X, ALU.max).then_inc(freed["dve"], 1)
                dve.wait_ge(freed["dve"], banks.n["dve"])
                ts(flag[:, 0:1].bitcast(mybir.dt.int32), esum[:, 0:1], float(CAP), None, ALU.is_gt).then_inc(rank_ready, 1)
                dve.wait_ge(rank_ready, w.next(rank_ready))
                j = banks.pair("dve")
                dve.wait_ge(ready["dve"], banks.n["dve"])
                dve.tensor_copy(gate_t[0:NE, :], psum[0:NE, 2 * j, :]).then_inc(freed["dve"], 1)
                for k in range(KT):
                    j = banks.pair("dve")
                    dve.wait_ge(ready["dve"], banks.n["dve"])
                    dve.tensor_copy(y_acc[:, k, :], psum[:, 2 * j, :]).then_inc(freed["dve"], 1)
                    if k == KT - 1:
                        dve.wait_ge(freed["dve"], banks.n["dve"])

            def select(dst, col, gated, sem):
                for t in range(TQ):
                    ins = ts(dst[:, t, :], C2("iota"), rank[:, t, bass.ds(col, 1)], gates[:, t, bass.ds(col, 1)] if gated else None,
                             ALU.is_equal, *([ALU.mult] if gated else []))
                ins.then_inc(sem, 1)
                dve.wait_ge(sem, w.next(sem))

            def experts(loops, first):
                base = dict(banks.n)
                with w.loop(dve, loops, {sel_ready: 1, gate_ready: 1, act_ready: 1, glu_ready: 1, sig_ready: 1, dve_chain: 2}) as (i, e):
                    turn = Turn(base, i)
                    dve.wait_ge(freed["act"], turn.count("gather", True))
                    dve.wait_ge(freed["dve"], turn.count("spread", True))
                    select(sel_gate, i + first, True, gate_ready)
                    select(sel, i + (first + 1), False, sel_ready)
                    dve.wait_ge(ready["dve"], turn.count("hidden"))
                    bias = C2("b_in")
                    for dst, b, c in ((glu, 0, 0), (lin, 2, KT)):
                        bc = bias[:, bass.ds(e * 16 + c, KT)].rearrange("p (k c) -> p k c", c=1).to_broadcast([P, KT, P])
                        ins = tt(dst.rearrange("p (k c) -> p k c", k=KT), psum[:, b:b + 2, :].rearrange("p b (k c) -> p (b k) c", c=P), bc, ALU.add)
                    ins.then_inc(freed["dve"], 1)
                    dve.wait_ge(freed["dve"], turn.count("hidden"))
                    ts(glu, glu, LIMIT, None, ALU.min).then_inc(glu_ready, 1)
                    dve.wait_ge(glu_ready, w.next(glu_ready))
                    ts(lin, lin, LIMIT, -LIMIT, ALU.min, ALU.max).then_inc(dve_chain, 1)
                    dve.wait_ge(dve_chain, w.next(dve_chain))
                    stt(lin, lin, 1.0, glu, ALU.add, ALU.mult).then_inc(dve_chain, 1)
                    dve.wait_ge(dve_chain, w.next(dve_chain))
                    dve.wait_ge(sig_ready, w.next(sig_ready))
                    tt(sig, sig, lin, ALU.mult).then_inc(act_ready, 1)
                    dve.wait_ge(act_ready, w.next(act_ready))
                    for k in range(KT):
                        dve.wait_ge(ready["dve"], turn.count(f"add{k}"))
                        tt(y_acc[:, k, :], y_acc[:, k, :], psum[:, k % 4, :], ALU.add).then_inc(freed["dve"], 1)
                    dve.wait_ge(ready["dve"], turn.count("spread"))
                    dve.tensor_copy(spread, psum[:, 4, :]).then_inc(freed["dve"], 1)
                    dve.wait_ge(freed["dve"], turn.count("spread"))
                for o in ("dve", "act"):
                    banks.n[o] += int(np.prod(loops)) * EPLAN_N[o]

            def last_add():
                for k in range(KT):
                    banks.n["dve"] += 1
                    dve.wait_ge(ready["dve"], banks.n["dve"])
                    tt(y_acc[:, k, :], y_acc[:, k, :], psum[:, k % 4, :], ALU.add).then_inc(freed["dve"], 1)
                    if k == KT - 1:
                        dve.wait_ge(freed["dve"], banks.n["dve"])

            dve.memset(mark, 0.0).then_inc(attention_free, 1)
            dve.wait_ge(attention_free, w.next(attention_free))
            dve.wait_ge(con2_in, 16)
            dve.wait_ge(ctx2_in, 16)
            updated()
            lambdas()
            norm(0, 2, True)
            norm_and_rope()
            attention()
            add_gated(2, 2, False, False)
            updated()
            norm(1, 2, False)
            routing()
            dve.memset(spread, 0.0).then_inc(dve_chain, 1)
            dve.wait_ge(dve_chain, w.next(dve_chain))
            dve.memset(y_sel, 0.0).then_inc(dve_chain, 1)
            dve.wait_ge(dve_chain, w.next(dve_chain))
            select(sel, 0, False, sel_ready)
            banks.n["act"] += 1
            dve.wait_ge(freed["act"], banks.n["act"])
            experts([NE], 0)
            last_add()
            over = dve.alloc_register("over_dve")
            dve.reg_load(over, flag[0:1, 0:1].bitcast(mybir.dt.int32))
            with dve.If_eq(over, 1):
                dve.memset(spread, 0.0).then_inc(cleared, 1)
                dve.wait_ge(cleared, w.next(cleared))
                experts([ROUNDS - 1, NE], NE)
                last_add()

            for k in range(KT):
                x = xs(xt[:, k, :])
                ins = stt(x, y_acc[:, k, :], mod[0][:, 5, k, 0:1], x, ALU.mult, ALU.add)
            ins.then_inc(fin_chain, 1)
            dve.wait_ge(fin_chain, 1)
            tt(xs(ht), xs(xt), xs(xt), ALU.mult).then_inc(fin_sq, 1)
            dve.wait_ge(fin_std, 1)
            for k in range(KT):
                stt(xs(xt[:, k, :]), xs(xt[:, k, :]), V("final2", k), xs(rs), ALU.mult, ALU.mult).then_inc(fin_x, 1)
            for t in range(TQ):
                dve.wait_ge(fin_tok, t + 1)
                dve.tensor_copy(out_buf[:, t, :], psum[:, 2 * t:2 * t + 2, :].rearrange("p b c -> p (b c)")).then_inc(fin_row, 1)

        @block.scalar
        def _(act):
            w = Counts()
            banks = Results()
            fn = act.activation

            def modulation(layer):
                for q in range(7):
                    if q < 6:
                        j = banks.pair("act")
                        act.wait_ge(ready["act"], banks.n["act"])
                        fn(row[:, q % 2, :], psum[0:2, 2 * j:2 * j + 2, :].rearrange("p b c -> p (b c)"), ACT.Copy
                           ).then_inc(freed["act"], 1)
                    if q > 0:
                        j = banks.pair("act")
                        act.wait_ge(ready["act"], banks.n["act"])
                        fn(mod[layer % 2][:, q - 1].rearrange("p k c -> p (k c)"), psum[:, 2 * j, 0:16], ACT.Copy
                           ).then_inc(freed["act"], 1)

            def norm(shift, layer, with_ctx, final=False):
                for f, b in parts(with_ctx):
                    ins = fn(f(ht[:, 0:4, :]), f(xt[:, 0:4, :]), ACT.Square)
                ins.then_inc(sq_act, 1)
                j = banks.pair("act")
                act.wait_ge(ready["act"], banks.n["act"])
                for f, b in parts(with_ctx):
                    ins = fn(f(rs), halves(j)[b], ACT.Ln, bias=EPS)
                ins.then_inc(freed["act"], 1)
                act.wait_ge(freed["act"], banks.n["act"])
                for f, b in parts(with_ctx):
                    ins = fn(f(rs), f(rs), ACT.Exp, scale=-0.5)
                ins.then_inc(std_ready, 1)
                for k in range(0 if final else KT):
                    act.wait_ge(normed, w.next(normed))
                    for f, b in parts(with_ctx):
                        ins = fn(f(ht[:, k, :]), f(ht[:, k, :]), ACT.Identity, bias=mod[layer % 2][:, shift, k, b:b + 1])
                    ins.then_inc(h_ready, 1)

            def gate_sigmoids(layer):
                for t in range(2):
                    for h in range(2):
                        j = banks.pair("act")
                        act.wait_ge(ready["act"], banks.n["act"])
                        px, pc = halves(j)
                        g = kk[:, 2 * t + h, :]
                        fn(grid(xs(g), layer), natural(px), ACT.Sigmoid)
                        fn(cs(g), pc, ACT.Sigmoid).then_inc(freed["act"], 1)
                    for _ in range(2):
                        banks.pair("dve")

            def raw_columns(layer):
                for n in range(16):
                    j = banks.pair("act")
                    act.wait_ge(ready["act"], banks.n["act"])
                    px, pc = halves(j)
                    rows = 64 if n in (12, 13) else 32 if n == 15 else P
                    if n >= 2:
                        act.wait_ge(raw_used, w.next(raw_used))
                    dst = tmp[0:rows, n % 2, 1:1 + W]
                    fn(grid(xs(dst), layer), natural(px[0:rows]), ACT.Copy)
                    fn(cs(dst), pc[0:rows], ACT.Copy).then_inc(freed["act"], 1)
                w.skip(raw_used, 2)
                act.wait_ge(shifted, w.next(shifted))
                fn(lo[0:64, 0, :], lo[0:64, 0, :], ACT.Tanh)
                fn(lo[:, 2, :], lo[:, 2, :], ACT.Sigmoid)
                fn(lo[0:32, 3, :], lo[0:32, 3, :], ACT.Sigmoid).then_inc(lo_tanh, 1)

            def group_norm(base, with_ctx, eps):
                for t in range(4):
                    banks.pair("dve")
                    act.wait_ge(freed["dve"], banks.n["dve"])
                    for f, b in parts(with_ctx):
                        ins = fn(f(scr[:, t, :]), f(ht[:, base + t, :]), ACT.Square)
                    ins.then_inc(sq_grp, 1)
                for t in range(4):
                    j = banks.pair("act")
                    act.wait_ge(ready["act"], banks.n["act"])
                    for f, b in parts(with_ctx):
                        ins = fn(f(scr[:, t, :]), halves(j)[b], ACT.Ln, bias=eps)
                    ins.then_inc(freed["act"], 1)
                act.wait_ge(freed["act"], banks.n["act"])
                for t in range(4):
                    for f, b in parts(with_ctx):
                        ins = fn(f(scr[:, t, :]), f(scr[:, t, :]), ACT.Exp, scale=-0.5)
                    ins.then_inc(gstd, 1)

            def key_norm():
                act.wait_ge(kk_raw, w.next(kk_raw))
                fn(scr, kk, ACT.Square).then_inc(kk_sq, 1)
                for t in range(4):
                    banks.pair("dve")
                    act.wait_ge(freed["dve"], banks.n["dve"])
                    for f, b in parts(True):
                        ins = fn(f(scr[:, t, :]), f(scr[:, t, :]), ACT.Ln)
                    ins.then_inc(logs, 1)
                act.wait_ge(logs, w.next(logs, 4))
                for t in range(4):
                    for f, b in parts(True):
                        ins = fn(f(scr[:, t, :]), f(scr[:, t, :]), ACT.Exp, scale=-0.5)
                    ins.then_inc(gstd, 1)
                act.wait_ge(grp_normed, w.next(grp_normed, 4))

            def recurrence(emit_ctx):
                def bank(t, name, g):
                    act.wait_ge(ready["act"], t.count(name, g))
                    return psum[:, t.bank(name, g), :]

                def tangents(t):
                    for h, name in enumerate(("decay", "rate")):
                        for g in range(2):
                            fn(R_sgaa[:, 512 * h + 256 * g:512 * h + 256 * g + 256], bank(t, name, g)[:, 0:256], ACT.Tanh,
                               scale=0.5).then_inc(freed["act"], 1)

                def powers():
                    act.wait_ge(r_cum, w.next(r_cum))
                    fn(flat8(R_pow[:, :, :, C:]), flat8(R_li), ACT.Exp, scale=-DECAY).then_inc(r_pow, 1)
                    fn(flat8(R_pow[:, :, :, 0:C]), flat8(R_lx), ACT.Exp, scale=-DECAY).then_inc(r_pow, 1)
                    fn(R_pi, wide(2), ACT.Exp, scale=DECAY).then_inc(r_pow, 1)

                def values(col):
                    for g in range(2):
                        fn(R_vc[:, g], chunk(rkv[:, 8:12, :], col[g]), ACT.Copy).then_inc(r_vcopy, 1)

                def flat8(t):
                    return t.rearrange("p g k c -> p (g k) c")

                first = Chunk(dict(banks.n), main=False)
                tangents(first)
                powers()
                values((0, CTX - C))
                fn(R_pc, R_tot, ACT.Exp, scale=-DECAY).then_inc(r_pow, 1)
                for o in banks.n:
                    banks.n[o] += first.total[o]
                for t, col, next_col, emit in recurrence_turns(w, act, banks, {r_cum: 1}, emit_ctx):
                    for g in range(2):
                        fn(R_vb[:, :, g, :], bank(t, "vb", g).rearrange("p (h k) -> p h k", h=2), ACT.Copy
                           ).then_inc(freed["act"], 1)
                    for g in range(2):
                        fn(R_ktk[:, g], pairs4(bank(t, "kt", g)[:, 0:256]), ACT.Copy).then_inc(freed["act"], 1)
                    for m in LEVELS:
                        for g in range(2):
                            fn(R_w[:, g], pairs4(bank(t, f"w{m}", g)[:, 0:256]), ACT.Copy).then_inc(freed["act"], 1)
                    if next_col:
                        tangents(t)
                    for g in range(2):
                        fn(R_w1[:, g], pairs4(bank(t, "rhs", g)[:, 0:256]), ACT.Copy).then_inc(freed["act"], 1)
                    if next_col:
                        powers()
                    for g in range(2):
                        fn(R_u[:, g], pairs4(bank(t, "u", g)[:, 0:256]), ACT.Copy).then_inc(freed["act"], 1)
                    if next_col:
                        values(next_col)
                        act.wait_ge(freed["dve"], t.count("s", 1))
                        fn(R_pc, R_tot, ACT.Exp, scale=-DECAY).then_inc(r_pow, 1)

            def feed_forward(with_ctx):
                for t in range(FT // 2):
                    for h in range(2):
                        n = 2 * t + h
                        j = banks.pair("act")
                        act.wait_ge(ready["act"], banks.n["act"])
                        px, pc = halves(j)
                        if n >= 4:
                            act.wait_ge(freed["dve"], banks.n["dve"] + h - 3)
                        s = silu_ff[:, n % 4, :]
                        ins = fn(s[:, CTX:768], px, ACT.Silu)
                        if with_ctx:
                            ins = fn(s[:, 0:CTX], pc, ACT.Silu)
                        ins.then_inc(freed["act"], 1)
                    for _ in range(2):
                        banks.pair("dve")

            act.wait_ge(consts_in, 32)
            for b in range(2):
                fn(condv[b], V(f"cond{b}", 0, 16).rearrange("p (k c) -> p k c", k=KT), ACT.Silu).then_inc(cond_ready, 1)
            for layer in range(2):
                act.wait_ge(x_updated, w.next(x_updated))
                if layer == 0:
                    modulation(0)
                act.wait_ge(modulated, w.next(modulated))
                norm(0, layer, True)
                act.wait_ge(zeroed, w.next(zeroed))
                gate_sigmoids(layer)
                raw_columns(layer)
                modulation(layer + 1)
                group_norm(0, layer == 0, LN_EPS)
                for t in range(4):
                    act.wait_ge(grp_normed, w.next(grp_normed))
                    for f, b in parts(layer == 0):
                        ins = fn(f(ht[:, t, :]), f(ht[:, t, :]), ACT.Silu, bias=V(f"cn_b{layer}", t), scale=V(f"cn_g{layer}", t))
                    ins.then_inc(conv_done, 1)
                key_norm()
                recurrence(layer == 0)
                group_norm(4, layer == 0, GN_EPS)
                for t in range(4):
                    act.wait_ge(grp_normed, w.next(grp_normed))
                    for f, b in parts(layer == 0):
                        ins = fn(f(ht[:, 4 + t, :]), f(ht[:, 4 + t, :]), ACT.Identity, bias=V(f"gn_b{layer}", t), scale=V(f"gn_g{layer}", t))
                    ins.then_inc(y_scaled, 1)
                for _ in range(8 + 8):
                    banks.pair("dve")
                act.wait_ge(x_updated, w.next(x_updated))
                norm(3, layer, layer == 0)
                feed_forward(layer == 0)
                for _ in range(8):
                    banks.pair("dve")
            else:
                act.wait_ge(x_updated, w.next(x_updated))
                norm(0, 1, False, final=True)

            def projections():
                for s, cols in enumerate((256, 256, 128)):
                    for t in range(TK):
                        j = banks.pair("act")
                        act.wait_ge(ready["act"], banks.n["act"])
                        c = (128, 384, 0)[s]
                        fn(v_buf[:, t, c:c + cols], psum[:, 2 * j, 0:cols], ACT.Copy).then_inc(freed["act"], 1)
                for t in range(14):
                    j = banks.pair("act")
                    act.wait_ge(ready["act"], banks.n["act"])
                    px, pc = halves(j)
                    keys = t < 2 or t >= 10
                    dst = k_buf[:, t if t < 2 else t - 8, CTX:KEYS] if keys else q_buf[:, t - 2, :]
                    fn(dst, px, ACT.Copy)
                    if keys:
                        ins = fn(k_buf[:, t if t < 2 else t - 8, 0:CTX], pc, ACT.Copy)
                    if t < 6:
                        fn(sq_buf[:, t, CTX:KEYS], px, ACT.Square)
                        if t < 2:
                            fn(sq_buf[:, t, 0:CTX], pc, ACT.Square)
                    fn(junk, junk, ACT.Copy).then_inc(freed["act"], 1)
                    act.wait_ge(freed["act"], banks.n["act"])
                    if t < 6:
                        fn(junk, junk, ACT.Copy).then_inc(head_sq, 1)
                        act.wait_ge(head_sq, w.next(head_sq))
                for t in range(6):
                    j = banks.pair("act")
                    act.wait_ge(ready["act"], banks.n["act"])
                    px, pc = halves(j)
                    ins = fn(sq_buf[:, t, CTX:KEYS], px, ACT.Ln, bias=EPS)
                    if t < 2:
                        ins = fn(sq_buf[:, t, 0:CTX], pc, ACT.Ln, bias=EPS)
                    ins.then_inc(freed["act"], 1)
                act.wait_ge(freed["act"], banks.n["act"])
                for t in range(6):
                    r = sq_buf[:, t, 0 if t < 2 else CTX:KEYS]
                    fn(r, r, ACT.Exp, scale=-0.5).then_inc(gstd, 1)
                for t in range(14):
                    banks.pair("dve")

            def attention():
                n_map = [0]

                def turn_over(n):
                    head, qt, _ = GROUPS[n]
                    j = banks.pair("act")
                    act.wait_ge(ready["act"], banks.n["act"])
                    src = psum[:, 2 * j:2 * j + 2, :].rearrange("p b c -> p (b c)")[:, 0:KEYS].rearrange("p (t q) -> p t q", q=P)
                    fn(pt_buf[:, head % 2, :, P * qt:P * qt + P], src, ACT.Copy).then_inc(freed["act"], 1)

                def weigh(head):
                    j = banks.pair("act")
                    act.wait_ge(ready["act"], banks.n["act"])
                    if head < 8:
                        r = slice(64 * (head % 2), 64 * (head % 2) + 64)
                        fn(xs(ht[r, head // 2, :]), psum[r, 2 * j, :], ACT.Copy).then_inc(freed["act"], 1)
                    else:
                        fn(xs(ht[:, 4 + head - 8, :]), psum[:, 2 * j, :], ACT.Copy)
                        fn(q_buf[:, head - 8, :], psum[:, 2 * j, :], ACT.Square).then_inc(freed["act"], 1)
                        act.wait_ge(freed["act"], banks.n["act"])
                        fn(junk, junk, ACT.Copy).then_inc(head_sq, 1)
                        act.wait_ge(head_sq, w.next(head_sq))

                for n, (head, qt, maps) in enumerate(GROUPS):
                    for _ in maps:
                        m = n_map[0]
                        n_map[0] += 1
                        j = banks.pair("act")
                        act.wait_ge(ready["act"], banks.n["act"])
                        act.wait_ge(maxed, w.next(maxed))
                        src = psum[:, 2 * j:2 * j + 2, :].rearrange("p b c -> p (b c)")[:, 0:KEYS]
                        fn(prob[:, m % 4, :], src, ACT.Exp, bias=neg_max[:, m:m + 1], scale=0.125, accum_out=row_sum[:, m:m + 1]).then_inc(freed["act"], 1)
                    if n >= 1:
                        turn_over(n - 1)
                        if GROUPS[n - 1][1] == TQ - 1:
                            weigh(GROUPS[n - 1][0])
                turn_over(len(GROUPS) - 1)
                weigh(GROUPS[-1][0])
                for t in range(4):
                    j = banks.pair("act")
                    act.wait_ge(ready["act"], banks.n["act"])
                    fn(q_buf[:, t, :], psum[:, 2 * j, :], ACT.Ln, bias=EPS, scale=float(DM // P)).then_inc(freed["act"], 1)
                act.wait_ge(freed["act"], banks.n["act"])
                for t in range(4):
                    fn(q_buf[:, t, :], q_buf[:, t, :], ACT.Exp, scale=-0.5).then_inc(gstd, 1)

            def routing():
                for t in range(TQ):
                    banks.pair("dve")
                for t in range(TQ):
                    j = banks.pair("act")
                    act.wait_ge(ready["act"], banks.n["act"])
                    fn(htok[:, t, :], psum[:, 2 * j:2 * j + 2, :].rearrange("p b c -> p (b c)"), ACT.Copy).then_inc(freed["act"], 1)
                act.wait_ge(top_ready, w.next(top_ready))
                fn(expv, expv, ACT.Exp).then_inc(top_exp, 1)
                for _ in range(TQ + 2 + KT):
                    banks.pair("dve")

            def copy_selected(own=False):
                fn(x_sel, psum[:, 4:6, :].rearrange("p b (k c) -> p (b k) c", c=P), ACT.Copy).then_inc(freed["act"], 1)

            def experts(loops):
                base = dict(banks.n)
                with w.loop(act, loops, {glu_ready: 1}) as (i, _):
                    turn = Turn(base, i)
                    act.wait_ge(glu_ready, w.next(glu_ready))
                    fn(sig, glu, ACT.Sigmoid, scale=ALPHA).then_inc(sig_ready, 1)
                    act.wait_ge(ready["act"], turn.count("gather"))
                    copy_selected()
                    act.wait_ge(ready["act"], turn.count("expert_out"))
                    fn(y_sel, psum[:, 6:8, :].rearrange("p b c -> p (b c)"), ACT.Copy).then_inc(freed["act"], 1)
                for o in ("dve", "act"):
                    banks.n[o] += int(np.prod(loops)) * EPLAN_N[o]

            act.wait_ge(x_updated, w.next(x_updated))
            act.wait_ge(lam_ready, w.next(lam_ready))
            fn(lam[:, 2:4], lam[:, 0:2], ACT.Exp).then_inc(lam_exp, 1)
            act.wait_ge(modulated, w.next(modulated))
            norm(0, 2, True)
            projections()
            attention()
            for _ in range(8):
                banks.pair("dve")
            act.wait_ge(x_updated, w.next(x_updated))
            norm(3, 2, False)
            routing()
            banks.n["act"] += 1
            act.wait_ge(ready["act"], banks.n["act"])
            copy_selected()
            experts([NE])
            banks.n["dve"] += KT
            act.wait_ge(rank_ready, 1)
            over = act.alloc_register("over_act")
            act.reg_load(over, flag[0:1, 0:1].bitcast(mybir.dt.int32))
            with act.If_eq(over, 1):
                experts([ROUNDS - 1, NE])
                banks.n["dve"] += KT
            act.wait_ge(fin_ms, 1)
            fn(xs(rs), psum[:, 0, :], ACT.Ln, bias=EPS).then_inc(fin_log, 1)
            act.wait_ge(fin_log, 1)
            fn(xs(rs), xs(rs), ACT.Exp, scale=-0.5).then_inc(fin_std, 1)


def constants():
    c = np.zeros((P, NC), np.float32)

    def put(name, a):
        o, n = COFF[name]
        c[:, o:o + n] = a

    p = np.arange(P)
    q = p % C
    put("ident", np.eye(P))
    put("mean_dm", 1.0 / DM)
    same = (p[:, None] // C == p[None, :] // C)
    put("head_mean", same / C)
    put("head_sum", same)
    put("scan", np.arange(512) % C != 0)
    t = np.arange(C)
    tri = [q[:, None] < t, q[:, None] <= t, q[:, None] > t, q[:, None] >= t]
    put("tri", np.concatenate(tri, 1))
    lows = []
    for m in (1,) + LEVELS:
        a, b = q[:, None] // m, t[None, :] // m
        lows += [(a % 2 == 1) & (b == a - 1), (a % 2 == 0) & (b == a + 1)]
    put("level1", np.concatenate(lows[:2], 1))
    put("level", np.concatenate(lows[2:], 1))
    put("id64", q[:, None] == t)
    return c


def lay_out(inp):
    def cm(a):
        return np.ascontiguousarray(np.asarray(a, np.float32).reshape(-1, P).T)

    vecs = np.zeros((P, NV), np.float32)

    def put(name, a):
        o, n = VOFF[name]
        vecs[:, o:o + n] = a

    for l in range(2):
        put(f"ada_b{l}", cm(inp["ada_b"][l]))
        put(f"norm1{l}", cm(inp["norm1_g"][l]))
        put(f"norm2{l}", cm(inp["norm2_g"][l]))
        for n, src in (("k_k", "k_k"), ("k_a", "k_a"), ("r_k", "r_k"), ("gn_g", "gn_g"), ("gn_b", "gn_b"),
                       ("conv_b", "conv_b"), ("cn_g", "cnorm_g"), ("cn_b", "cnorm_b")):
            put(f"{n}{l}", cm(inp[src][l]))
        cw = np.asarray(inp["conv_w"][l])
        put(f"conv_w{l}", cw.reshape(TAPS, 4, P).transpose(2, 1, 0).reshape(P, -1))
        sw = np.asarray(inp["shift_w"][l])
        s = np.zeros((16, P, 3), np.float32)
        s[:12] = sw[:, :1536].reshape(3, 12, P).transpose(1, 2, 0)
        s[12, :64], s[13, :64] = sw[:, 1536:1600].T, sw[:, 1600:1664].T
        s[14], s[15, :32] = sw[:, 1664:1792].T, sw[:, 1792:1824].T
        put(f"shift_w{l}", s.transpose(1, 0, 2).reshape(P, -1))
    put("final1", cm(inp["final_g"]))
    put("ada_b2", cm(inp["b_ada_2"][0]))
    put("norm12", cm(inp["g_attn_2"][0]))
    put("norm22", cm(inp["g_ffn_2"][0]))
    put("q_norm", np.tile(np.asarray(inp["gqa_q_norm_2"][0]), 2)[:, None])
    put("k_norm", np.tile(np.asarray(inp["gqa_k_norm_2"][0]), 2)[:, None])
    put("subln", np.asarray(inp["diff_subln_2"][0])[:, None])
    put("final2", cm(inp["g_final_2"]))
    for b, (c0, c1) in enumerate((("c", "c_ctx"), ("c_2", "c_ctx_2"))):
        put(f"cond{b}", np.stack([cm(np.asarray(inp[c0]).reshape(-1)), cm(np.asarray(inp[c1]).reshape(-1))], 2).reshape(P, 16))

    def slots(wt):
        k, n = wt.shape
        kt = k // P
        out = []
        for c in range(0, n, 256):
            for k0 in range(0, kt, 8):
                s = np.zeros((P, 8, 256), np.float32)
                part = wt[k0 * P:min(k0 + 8, kt) * P, c:c + 256]
                s[:, :part.shape[0] // P, :part.shape[1]] = part.reshape(-1, P, part.shape[1]).transpose(1, 0, 2)
                out.append(s.reshape(P, SLOT))
        return out

    stream = []
    stream += slots(np.asarray(inp["ada_w"][0]))
    for l in range(2):
        wi = np.asarray(inp["w_in"][l])
        stream += slots(np.concatenate([wi[:, 512:768], wi[:, 0:256], wi[:, 768:1024], wi[:, 256:512], wi[:, 1024:]], 1))
        stream += slots(np.asarray(inp["ada_w"][1] if l == 0 else inp["w_ada_2"][0]))
        s = np.zeros((P, SLOT), np.float32)
        for h, (up, b0) in enumerate((("decay_up", "decay_b0"), ("iclr_up", "iclr_b0"))):
            s[0:64, 1024 * h:1024 * h + 1024] = np.asarray(inp[up][l]).transpose(1, 0, 2).reshape(64, 1024)
            s[64, 1024 * h:1024 * h + 1024] = np.asarray(inp[b0][l]).reshape(1024)
        stream.append(s)
        s = np.zeros((P, SLOT), np.float32)
        gu = np.asarray(inp["g_up"][l])
        s[:, 0:512], s[0:32, 512:1024] = gu[0:P], gu[P:160]
        stream.append(s)
        stream += slots(np.asarray(inp["w_out"][l]))
        g, u = slots(np.asarray(inp["ffn_wg"][l])), slots(np.asarray(inp["ffn_wu"][l]))
        for a, b in zip(g, u):
            stream += [a, b]
        stream += slots(np.asarray(inp["ffn_wd"][l]))
    wq = np.asarray(inp["w_qkv_2"][0])
    qa, ka, va, qb, kb, vb = (wq[:, a:b] for a, b in ((0, 512), (512, 640), (640, 768), (768, 1280), (1280, 1792), (1792, 2304)))
    stream += slots(vb) + slots(va)
    stream += slots(np.concatenate([ka[:, 0:64], ka[:, 0:64], ka[:, 64:128], ka[:, 64:128]], 1))
    stream += slots(qa) + slots(qb) + slots(kb)
    stream += slots(np.asarray(inp["w_o_2"][0]))
    s = np.zeros((P, SLOT), np.float32)
    s[:, 0:256] = np.asarray(inp["w_router_2"][0]).reshape(KT, P, NE).transpose(1, 0, 2).reshape(P, -1)
    s[0:NE, 256:1280] = np.asarray(inp["b_out_2"][0])
    stream.append(s)
    while len(stream) < MIX_SLOTS:
        stream.append(np.zeros_like(s))
    return vecs, stream


def second_constants(inp):
    c = np.zeros((P, NC2), np.float32)

    def put(name, a):
        o, n = C2OFF[name]
        c[:, o:o + n] = a

    put("lam", np.asarray(inp["diff_lambda_2"][0]).reshape(1, -1))
    put("b_router", np.asarray(inp["b_router_2"][0])[None, :])
    put("b_in", np.asarray(inp["b_in_2"][0]).reshape(NE, 16, P).transpose(2, 0, 1).reshape(P, -1))
    i = np.arange(P)
    first = (i % 32) < 16
    rot = np.zeros((P, P), np.float32)
    rot[i[first] + 16, i[first]] = -1.0
    rot[i[~first] - 16, i[~first]] = 1.0
    put("rot", rot)
    t = np.arange(SEQ)
    freq = 10000.0 ** (-np.arange(16) / 16.0)
    pos = np.where(((i % 64) < 32)[:, None], (t // GRID_W)[None, :], (t % GRID_W)[None, :])
    ang = pos * freq[i % 16][:, None]
    put("cos", np.cos(ang))
    put("sin", np.sin(ang))
    put("before", i[:, None] < i[None, :])
    put("ones", 1.0)
    put("iota", i[None, :])
    return c


def columns(x):
    x = np.asarray(x)
    return np.ascontiguousarray(x.T.reshape(KT, P, -1).transpose(1, 0, 2))



def kernel(**inputs):
    from concourse import bacc
    from concourse.bass_utils import run_bass_kernel_spmd

    inp = {k: np.asarray(v) for k, v in inputs.items()}
    vecs, stream = lay_out(inp)
    arrays = dict(vecs=vecs, consts=constants(), stream=np.stack(stream), x_cm=columns(inp["x"][0]), ctx_cm=columns(inp["ctx"][0]),
                  con2=second_constants(inp), ctx2_cm=columns(inp["ctx_2"][0]),
                  w_in=np.ascontiguousarray(inp["w_in_2"][0]), w_out=np.ascontiguousarray(inp["w_out_2"][0]))
    nc = bacc.Bacc("TRN2", target_bir_lowering=False, num_devices=1)
    ins = {n: nc.dram_tensor(n, a.shape, F32, kind="ExternalInput").ap() for n, a in arrays.items()}
    out = nc.dram_tensor("out_0_dram", (1, SEQ, DM), F32, kind="ExternalOutput").ap()
    build(nc, ins, out)
    r = run_bass_kernel_spmd(nc, [arrays], core_ids=[0])
    return r.results[0]["out_0_dram"]
```
